# Optimizing a Trainium2 kernel written in Bass

```python
import jax, jax.numpy as jnp
from jax import lax
import numpy as np

"""Two layers of a hybrid causal decoder trunk.

layer 0: RMSNorm -> one combined projection feeding two parallel head groups:
         (A) LongNet-style dilated sliding-window attention, 3 dilation branches merged
             by their softmax denominators, and (B) sliding-window GQA with per-head
             attention sinks; outputs concatenated -> one output projection; residual;
         RMSNorm -> dense SwiGLU; residual.
layer 1: RMSNorm -> HGRN2 gated linear recurrence with state expansion (chunkwise form,
         per-layer forget-gate lower bound) with output gate; residual;
         RMSNorm -> top-2-of-8 routed SwiGLU experts; residual.
final RMSNorm.
inputs : x (BATCH, SEQ, D_MODEL) float32, positions (BATCH, SEQ) int32, parameters.
output : (BATCH, SEQ, D_MODEL).
"""

D_MODEL = 1024
BATCH = 1
SEQ = 256
DEPTH = 2

HEAD_DIM = 64
EPS = 1e-6
A_HEADS = 8
A_PATTERNS = ((128, 1), (512, 4), (2048, 16))
B_Q_HEADS = 8
B_KV_HEADS = 2
B_GROUP = B_Q_HEADS // B_KV_HEADS
B_WINDOW = 128
ATTN_BLOCK = 128
ROPE_THETA = 500000.0
ROT_DIM = HEAD_DIM // 4
C_HEADS = 8
C_KEY_DIM = D_MODEL // C_HEADS
C_VAL_DIM = D_MODEL // C_HEADS
C_CHUNK = 64
D_FF = (7 * D_MODEL) // 2
N_EXPERTS = 8
TOP_K = 2
MOE_BLOCK = 128

N_EVEN = (DEPTH + 1) // 2
N_ODD = DEPTH // 2
A_WIDTH = A_HEADS * HEAD_DIM
B_Q_WIDTH = B_Q_HEADS * HEAD_DIM
B_KV_WIDTH = B_KV_HEADS * HEAD_DIM
IN_ATTN = 3 * A_WIDTH + B_Q_WIDTH + 2 * B_KV_WIDTH
MIX_ATTN = A_WIDTH + B_Q_WIDTH
C_K_WIDTH = C_HEADS * C_KEY_DIM
C_V_WIDTH = C_HEADS * C_VAL_DIM
IN_REC = 2 * C_K_WIDTH + 2 * C_V_WIDTH

kernel_name = "hybrid_dilated_swa_hgrn2_moe"

def rms_norm(x, g):
    xf = x.astype(jnp.float32)
    y = xf * lax.rsqrt(jnp.mean(xf * xf, axis=-1, keepdims=True) + EPS)
    return (y * g.astype(jnp.float32)).astype(x.dtype)

def rope(x, cos, sin):
    half = ROT_DIM // 2
    xf = x.astype(jnp.float32)
    x1 = xf[..., :half]
    x2 = xf[..., half:ROT_DIM]
    out = jnp.concatenate([x1 * cos - x2 * sin, x2 * cos + x1 * sin, xf[..., ROT_DIM:]], axis=-1)
    return out.astype(x.dtype)

def banded_attention(q, k, v, n_back, sink=None):
    bsz, grp, rep, L, dh = q.shape
    blk = ATTN_BLOCK
    pad = (-L) % blk
    lp = L + pad
    nb = lp // blk
    q = jnp.pad(q, ((0, 0), (0, 0), (0, 0), (0, pad), (0, 0)))
    k = jnp.pad(k, ((0, 0), (0, 0), (0, pad), (0, 0)))
    v = jnp.pad(v, ((0, 0), (0, 0), (0, pad), (0, 0)))
    qb = q.reshape(bsz, grp, rep, nb, blk, dh)
    kb = k.reshape(bsz, grp, nb, blk, dh)
    vb = v.reshape(bsz, grp, nb, blk, dh)
    kk = jnp.concatenate([jnp.concatenate([jnp.zeros_like(kb[:, :, :1]), kb[:, :, :-1]], axis=2), kb], axis=3)
    vv = jnp.concatenate([jnp.concatenate([jnp.zeros_like(vb[:, :, :1]), vb[:, :, :-1]], axis=2), vb], axis=3)
    s = jnp.einsum('bgrnqd,bgnkd->bgrnqk', qb, kk, preferred_element_type=jnp.float32) * (dh ** -0.5)
    qi = jnp.arange(blk)[:, None]
    kj = jnp.arange(2 * blk)[None, :]
    dist = blk + qi - kj
    band = (dist >= 0) & (dist <= n_back)
    valid = band[None] & ((jnp.arange(nb)[:, None, None] > 0) | (kj >= blk)[None])
    s = jnp.where(valid, s, -jnp.inf)
    m = jnp.max(s, axis=-1, keepdims=True)
    if sink is not None:
        sk = sink.astype(jnp.float32)[None, :, :, None, None, None]
        m = jnp.maximum(m, sk)
    p = jnp.exp(s - m)
    l = jnp.sum(p, axis=-1, keepdims=True)
    if sink is not None:
        l = l + jnp.exp(sk - m)
    o = jnp.einsum('bgrnqk,bgnkd->bgrnqd', p, vv.astype(jnp.float32)) / l
    lse = (m + jnp.log(l))[..., 0]
    o = o.reshape(bsz, grp, rep, lp, dh)[:, :, :, :L].astype(q.dtype)
    lse = lse.reshape(bsz, grp, rep, lp)[:, :, :, :L]
    return o, lse

def dilated_attention(q, k, v):
    bsz, nh, S, dh = q.shape
    outs, lses = [], []
    for window, d in A_PATTERNS:
        L = S // d
        def to_res(t):
            return t.reshape(bsz, nh, L, d, dh).transpose(0, 1, 3, 2, 4).reshape(bsz, nh * d, L, dh)
        o, lse = banded_attention(to_res(q)[:, :, None], to_res(k), to_res(v), window // d)
        outs.append(o[:, :, 0].reshape(bsz, nh, d, L, dh).transpose(0, 1, 3, 2, 4).reshape(bsz, nh, S, dh))
        lses.append(lse[:, :, 0].reshape(bsz, nh, d, L).transpose(0, 1, 3, 2).reshape(bsz, nh, S))
    w = jax.nn.softmax(jnp.stack(lses, axis=0), axis=0)
    out = jnp.sum(w[..., None] * jnp.stack(outs, axis=0).astype(jnp.float32), axis=0)
    return out.astype(q.dtype)

def attn_mixer(h, w_in, sinks, w_out, cos, sin):
    bsz, S, _ = h.shape
    proj = h @ w_in
    splits = [A_WIDTH, 2 * A_WIDTH, 3 * A_WIDTH, 3 * A_WIDTH + B_Q_WIDTH, 3 * A_WIDTH + B_Q_WIDTH + B_KV_WIDTH]
    qa, ka, va, qb, kb, vb = jnp.split(proj, splits, axis=-1)
    heads = lambda t, n: t.reshape(bsz, S, n, HEAD_DIM)
    qa = rope(heads(qa, A_HEADS), cos, sin).transpose(0, 2, 1, 3)
    ka = rope(heads(ka, A_HEADS), cos, sin).transpose(0, 2, 1, 3)
    va = heads(va, A_HEADS).transpose(0, 2, 1, 3)
    oa = dilated_attention(qa, ka, va)
    qb = rope(heads(qb, B_Q_HEADS), cos, sin).reshape(bsz, S, B_KV_HEADS, B_GROUP, HEAD_DIM).transpose(0, 2, 3, 1, 4)
    kb = rope(heads(kb, B_KV_HEADS), cos, sin).transpose(0, 2, 1, 3)
    vb = heads(vb, B_KV_HEADS).transpose(0, 2, 1, 3)
    ob, _ = banded_attention(qb, kb, vb, B_WINDOW - 1, sinks.reshape(B_KV_HEADS, B_GROUP))
    mix = jnp.concatenate([oa.transpose(0, 2, 1, 3).reshape(bsz, S, A_WIDTH),
                           ob.transpose(0, 3, 1, 2, 4).reshape(bsz, S, B_Q_WIDTH)], axis=-1)
    return mix @ w_out

def hgrn2_mixer(h, w_in, lower_bound, norm_g, w_out):
    bsz, S, _ = h.shape
    proj = h @ w_in
    q, f, i, g = jnp.split(proj, [C_K_WIDTH, 2 * C_K_WIDTH, 2 * C_K_WIDTH + C_V_WIDTH], axis=-1)
    q = jax.nn.silu(q.astype(jnp.float32))
    fg = lower_bound + (1.0 - lower_bound) * jax.nn.sigmoid(f.astype(jnp.float32))
    k = 1.0 - fg
    logf = jnp.log(fg)
    nc = S // C_CHUNK
    def chunked(t, dim):
        return t.reshape(bsz, nc, C_CHUNK, C_HEADS, dim).transpose(1, 0, 3, 2, 4)
    qc = chunked(q, C_KEY_DIM)
    kc = chunked(k, C_KEY_DIM)
    vc = chunked(i.astype(jnp.float32), C_VAL_DIM)
    bc = jnp.cumsum(chunked(logf, C_KEY_DIM), axis=3)
    causal = jnp.tril(jnp.ones((C_CHUNK, C_CHUNK), dtype=bool))

    def step(state, xs):
        qt, kt, vt, bt = xs
        diff = bt[:, :, :, None, :] - bt[:, :, None, :, :]
        decay = jnp.exp(jnp.where(causal[:, :, None], diff, -jnp.inf))
        att = jnp.einsum('bhtk,bhsk,bhtsk->bhts', qt, kt, decay)
        o = jnp.einsum('bhts,bhsv->bhtv', att, vt) + jnp.einsum('bhtk,bhkv->bhtv', qt * jnp.exp(bt), state)
        b_last = bt[:, :, -1:, :]
        state = jnp.exp(b_last[:, :, 0, :])[..., None] * state + \
            jnp.einsum('bhsk,bhsv->bhkv', kt * jnp.exp(b_last - bt), vt)
        return state, o

    init = jnp.zeros((bsz, C_HEADS, C_KEY_DIM, C_VAL_DIM), jnp.float32)
    _, o = lax.scan(step, init, (qc, kc, vc, bc))
    o = o.transpose(1, 0, 3, 2, 4).reshape(bsz, S, C_HEADS, C_VAL_DIM)
    o = o * lax.rsqrt(jnp.mean(o * o, axis=-1, keepdims=True) + EPS)
    o = o.reshape(bsz, S, C_V_WIDTH) * norm_g.astype(jnp.float32) * jax.nn.silu(g.astype(jnp.float32))
    return o.astype(h.dtype) @ w_out

def swiglu(h, w_gate, w_up, w_down):
    return (jax.nn.silu(h @ w_gate) * (h @ w_up)) @ w_down

def moe_swiglu(h, w_router, w_gate, w_up, w_down):
    bsz, S, D = h.shape
    N = bsz * S
    t = h.reshape(N, D)
    logits = (t @ w_router).astype(jnp.float32)
    top_v, top_e = lax.top_k(logits, TOP_K)
    gates = jax.nn.softmax(top_v, axis=-1)
    e_flat = top_e.reshape(-1).astype(jnp.int32)
    g_flat = gates.reshape(-1)
    tok_flat = jnp.arange(N * TOP_K, dtype=jnp.int32) // TOP_K
    order = jnp.argsort(e_flat)
    e_sorted = e_flat[order]
    tok_sorted = tok_flat[order]
    g_sorted = g_flat[order]
    sizes = jnp.bincount(e_flat, length=N_EXPERTS).astype(jnp.int32)
    padded = ((sizes + MOE_BLOCK - 1) // MOE_BLOCK) * MOE_BLOCK
    start = jnp.cumsum(sizes) - sizes
    pend = jnp.cumsum(padded)
    pstart = pend - padded
    dest = pstart[e_sorted] + (jnp.arange(N * TOP_K, dtype=jnp.int32) - start[e_sorted])
    P = N * TOP_K + N_EXPERTS * MOE_BLOCK
    nblk = P // MOE_BLOCK
    buf = jnp.zeros((P, D), t.dtype).at[dest].set(t[tok_sorted])
    blk_e = jnp.minimum(jnp.searchsorted(pend, jnp.arange(nblk, dtype=jnp.int32) * MOE_BLOCK, side='right'),
                        N_EXPERTS - 1).astype(jnp.int32)

    def expert_block(args):
        xb, e = args
        return (jax.nn.silu(xb @ w_gate[e]) * (xb @ w_up[e])) @ w_down[e]

    yb = lax.map(expert_block, (buf.reshape(nblk, MOE_BLOCK, D), blk_e))
    y = yb.reshape(P, D)[dest] * g_sorted[:, None].astype(t.dtype)
    out = jax.ops.segment_sum(y, tok_sorted, num_segments=N)
    return out.reshape(bsz, S, D)

def setup_inputs(seed: int = 0) -> dict:
    key = jax.random.key(seed)
    ks = jax.random.split(key, 24)
    nrm = lambda k, shape, fan_in: jax.random.normal(k, shape, jnp.float32) * (fan_in ** -0.5)
    x = jax.random.normal(ks[0], (BATCH, SEQ, D_MODEL), jnp.float32)
    offsets = jax.random.randint(ks[1], (BATCH, 1), 0, 1024, dtype=jnp.int32)
    positions = offsets + jnp.arange(SEQ, dtype=jnp.int32)[None, :]
    g_mix = 1.0 + 0.02 * jax.random.normal(ks[2], (DEPTH, D_MODEL), jnp.float32)
    g_ffn = 1.0 + 0.02 * jax.random.normal(ks[3], (DEPTH, D_MODEL), jnp.float32)
    g_final = 1.0 + 0.02 * jax.random.normal(ks[4], (D_MODEL,), jnp.float32)
    w_in_attn = nrm(ks[5], (N_EVEN, D_MODEL, IN_ATTN), D_MODEL)
    w_out_attn = nrm(ks[6], (N_EVEN, MIX_ATTN, D_MODEL), MIX_ATTN)
    attn_sinks = 0.5 * jax.random.normal(ks[7], (N_EVEN, B_Q_HEADS), jnp.float32)
    w_in_rec = nrm(ks[8], (N_ODD, D_MODEL, IN_REC), D_MODEL)
    rec_lower_bounds = 0.5 * jax.random.normal(ks[9], (DEPTH, C_K_WIDTH), jnp.float32)
    rec_norm_g = 1.0 + 0.02 * jax.random.normal(ks[10], (N_ODD, C_V_WIDTH), jnp.float32)
    w_out_rec = nrm(ks[11], (N_ODD, C_V_WIDTH, D_MODEL), C_V_WIDTH)
    w_gate_dense = nrm(ks[12], (N_EVEN, D_MODEL, D_FF), D_MODEL)
    w_up_dense = nrm(ks[13], (N_EVEN, D_MODEL, D_FF), D_MODEL)
    w_down_dense = nrm(ks[14], (N_EVEN, D_FF, D_MODEL), D_FF)
    w_router = nrm(ks[15], (N_ODD, D_MODEL, N_EXPERTS), D_MODEL)
    w_gate_moe = nrm(ks[16], (N_ODD, N_EXPERTS, D_MODEL, D_FF), D_MODEL)
    w_up_moe = nrm(ks[17], (N_ODD, N_EXPERTS, D_MODEL, D_FF), D_MODEL)
    w_down_moe = nrm(ks[18], (N_ODD, N_EXPERTS, D_FF, D_MODEL), D_FF)
    return {"x": x, "positions": positions, "g_mix": g_mix, "g_ffn": g_ffn, "g_final": g_final,
            "w_in_attn": w_in_attn, "w_out_attn": w_out_attn, "attn_sinks": attn_sinks,
            "w_in_rec": w_in_rec, "rec_lower_bounds": rec_lower_bounds, "rec_norm_g": rec_norm_g,
            "w_out_rec": w_out_rec, "w_gate_dense": w_gate_dense, "w_up_dense": w_up_dense,
            "w_down_dense": w_down_dense, "w_router": w_router, "w_gate_moe": w_gate_moe,
            "w_up_moe": w_up_moe, "w_down_moe": w_down_moe}

def reference(x, positions, g_mix, g_ffn, g_final, w_in_attn, w_out_attn, attn_sinks, w_in_rec,
              rec_lower_bounds, rec_norm_g, w_out_rec, w_gate_dense, w_up_dense, w_down_dense,
              w_router, w_gate_moe, w_up_moe, w_down_moe):
    inv_freq = jnp.power(ROPE_THETA, -jnp.arange(0, ROT_DIM, 2, dtype=jnp.float32) / ROT_DIM)
    ang = positions.astype(jnp.float32)[..., None] * inv_freq
    cos = jnp.cos(ang)[:, :, None, :]
    sin = jnp.sin(ang)[:, :, None, :]
    lb = jax.nn.softmax(rec_lower_bounds.astype(jnp.float32), axis=0)
    lb_table = jnp.cumsum(lb, axis=0) - lb[0]
    for layer in range(DEPTH):
        j = layer // 2
        h = rms_norm(x, g_mix[layer])
        if layer % 2 == 0:
            x = x + attn_mixer(h, w_in_attn[j], attn_sinks[j], w_out_attn[j], cos, sin)
            x = x + swiglu(rms_norm(x, g_ffn[layer]), w_gate_dense[j], w_up_dense[j], w_down_dense[j])
        else:
            x = x + hgrn2_mixer(h, w_in_rec[j], lb_table[layer], rec_norm_g[j], w_out_rec[j])
            x = x + moe_swiglu(rms_norm(x, g_ffn[layer]), w_router[j], w_gate_moe[j], w_up_moe[j], w_down_moe[j])
    return rms_norm(x, g_final)


_drawn_inputs = setup_inputs


def setup_inputs(seed=0):
    import zlib

    import numpy as np

    out = dict(_drawn_inputs(seed))
    spreads = {}
    factors = {'g_final': 2.871, 'attn_sinks': 6.487, 'rec_norm_g': 2.722}
    for name, (base, spread) in spreads.items():
        noise = np.random.default_rng([zlib.crc32(name.encode()), seed]).standard_normal(out[name].shape)
        drawn = base * np.exp(spread * noise) if base else spread * noise
        out[name] = __import__('jax').numpy.asarray(drawn.astype(out[name].dtype))
    for name, factor in factors.items():
        out[name] = (out[name] * factor).astype(out[name].dtype)
    return out
```

```python
from contextlib import ExitStack

import numpy as np

import concourse.bass as bass
from concourse import mybir

ALU = mybir.AluOpType
ACT = mybir.ActivationFunctionType
AX = mybir.AxisListType
F32 = mybir.dt.float32
F32R = mybir.dt.float32r
I32 = mybir.dt.int32
U32 = mybir.dt.uint32
U8 = mybir.dt.uint8

P = 128
TT = 2
TOK = P * TT
D = 1024
KC = D // P
EPS = 1e-6
HD = 64
AH, BH, KVH = 8, 8, 2
WIN_A, WIN_B = 128, 127
ROT = 16
THETA = 500000.0
CH = 8
FF = 3584
NE = 8
CAP = 128
UNIT = 2048
BLK = 512
RAW = 6
SPL = 3
FB = FF // BLK
FCH = FF // P
FFN_UNITS = 4 * FB + FCH // 2
LEAD = RAW + SPL
BIG = 3.0e38
SCALE = HD ** -0.5

GATE, UP, TR, YB = 0, 2, 4, 6


class Tally:

    def __init__(self):
        self.count, self.per, self.var = {}, {}, None

    def at(self, key, less=0):
        c = self.count.get(key, 0) - less
        p = self.per.get(key, 0)
        return c if self.var is None or not p else self.var * p + c

    def step(self, key, by=1):
        self.count[key] = self.count.get(key, 0) + by
        return self.at(key)

    def enter(self, var, per):
        self.var, self.per, self.start = var, per, dict(self.count)

    def leave(self, rounds):
        for k in set(self.count) | set(self.per):
            got = self.count.get(k, 0) - self.start.get(k, 0)
            assert got == self.per.get(k, 0), (k, got, self.per.get(k, 0))
        self.count, self.var = dict(self.start), rounds


def spread(ap, dim, n):
    shape = list(ap.shape)
    assert shape[dim] == 1
    shape[dim] = n
    return ap.broadcast_to(shape)


def col_blocks(w, c0, n):
    v = w.rearrange("(k p) f -> p k f", p=P)
    return [v[:, h * 4:h * 4 + 4, c0:c0 + n] for h in range(2)]


def build(nc, x, positions, g_mix, g_ffn, g_final, w_in_attn, w_out_attn, attn_sinks, w_in_rec,
          rec_lower_bounds, rec_norm_g, w_out_rec, w_gate_dense, w_up_dense, w_down_dense,
          w_router, w_gate_moe, w_up_moe, w_down_moe, out):
    ctx = ExitStack()
    with ctx:
        def sb(name, shape, dt=F32):
            return ctx.enter_context(nc.sbuf_tensor(name, shape, dt))

        def sem(name):
            return ctx.enter_context(nc.semaphore(name))

        raw = sb("raw", [P, RAW, UNIT])
        w_hi = sb("w_hi", [P, SPL, UNIT], F32R)
        w_lo = sb("w_lo", [P, SPL, UNIT], F32R)
        X = sb("X", [P, TT, D])
        U = sb("U", [P, TT, D])
        t_hi = sb("t_hi", [P, KC, TOK], F32R)
        t_lo = sb("t_lo", [P, KC, TOK], F32R)
        h_hi = sb("h_hi", [P, 2, BLK], F32R)
        h_lo = sb("h_lo", [P, 2, BLK], F32R)
        work = sb("work", [P, 15360])
        ident = sb("ident", [P, P])
        tri = sb("tri", [P, P])
        ones = sb("ones", [P, P])
        slots = sb("slots", [P, P])
        iota8 = sb("iota8", [P, 8])
        lev_mask = sb("lev_mask", [P, 8, P], U8)
        col = sb("col", [P, 56])
        lbc = sb("lbc", [P, 8, 8])
        gfr = sb("gfr", [1, D + 8])
        sk8 = sb("sk8", [P, 8])
        posi = sb("posi", [P, TT], I32)
        posf = sb("posf", [P, TT])
        rope = sb("rope", [P, 8, TT, 8])
        ss = sb("ss", [P, 8])
        ss16 = sb("ss16", [P, 3, TT, CH])
        epsc = sb("epsc", [P, 2])
        wr = sb("wr", [P, KC, NE])
        wr_hi = sb("wr_hi", [P, KC, NE], F32R)
        wr_lo = sb("wr_lo", [P, KC, NE], F32R)
        att = sb("att", [P, 3, 16])
        rt = sb("rt", [P, 12, TT, 8])
        rti = sb("rti", [P, TT, 8], U32)
        cols = sb("cols", [P, TT, 2 * NE + 1])
        gates = sb("gates", [P, TT, 2 * NE + 1])
        cur = sb("cur", [P, 4])
        cnt = sb("cnt", [P, 2])
        nrounds = sb("nrounds", [P, 1], I32)

        bank = [ctx.enter_context(nc.psum_tensor(f"bank{i}", [P, BLK], F32)) for i in range(8)]

        def w_at(a, n):
            return work[:, a:a + n]

        NH = 2 * AH + BH + 2 * KVH + AH
        proj = w_at(0, TT * NH * HD).rearrange("p (t h d) -> p t h d", t=TT, h=NH)
        qkT = w_at(4608, 13 * TOK).rearrange("p (c n) -> p c n", c=13)
        sc = w_at(7936, 3 * 384).rearrange("p (s n) -> p s n", s=3)
        pT = w_at(9088, 2 * 384).rearrange("p (s n) -> p s n", s=2)
        rp = w_at(9856, 4 * TT * 26 * 8).rearrange("p (s t h d) -> p s t h d", s=4, t=TT, h=26)
        mi = w_at(0, 3 * 384).bitcast(I32).rearrange("p (s n) -> p s n", s=3)
        mf = w_at(1152, 5 * 384).rearrange("p (s n) -> p s n", s=5)
        biasA = w_at(14592, 384)
        biasB = w_at(14976, 384)
        rows = work[0:56, 14400:14400 + P]
        qT = w_at(0, 2048)
        kT = w_at(2048, 2048)
        bT = w_at(4096, 2048)
        ex = w_at(6144, 2048).rearrange("p (s n) -> p s n", s=2)
        wl = w_at(8192, 2048).rearrange("p (s n) -> p s n", s=2)
        aT = w_at(10240, 2048)
        aX = w_at(12288, 1024)
        V = w_at(13312, 2048).rearrange("p (t n) -> p t n", t=TT)
        reset = w_at(12288, 512)
        sq = w_at(6144, 2048).rearrange("p (s n) -> p s n", s=4)
        H = w_at(0, TT * FF).rearrange("p (t f) -> p t f", t=TT)
        Y = w_at(7168, D)
        G = w_at(8192, TOK).rearrange("p (t c) -> p t c", t=TT)
        GT = w_at(8448, TOK)
        S = w_at(8704, TOK).rearrange("p (t c) -> p t c", t=TT)
        gf = w_at(9216, D)
        outb = w_at(0, TT * D).rearrange("p (t n) -> p t n", t=TT)

        def proj_place(nb, t, src):
            first = (0, AH, 28, 2 * AH, 2 * AH + BH)[nb]
            if nb == 3:
                return (proj[:, t, first:first + 8, :].rearrange("p (j a) d -> p a j d", a=2),
                        src[:].rearrange("p (a j d) -> p a j d", a=2, j=4))
            h = 4 if nb == 4 else 8
            return proj[:, t, first:first + h, :], src[:, 0:h * HD].rearrange("p (h d) -> p h d", h=h)

        x_in, small_in, pos_in = sem("x_in"), sem("small_in"), sem("pos_in")
        row_in, wr_in = sem("row_in"), sem("wr_in")
        loaded = [sem(f"loaded{i}") for i in range(RAW)]
        hi_done, lo_done = sem("hi_done"), sem("lo_done")
        unit_done = sem("unit_done")
        full = [sem(f"full{i}") for i in range(8)]
        free = [sem(f"free{i}") for i in range(8)]
        pool_seq, act_seq, dve_seq = sem("pool_seq"), sem("act_seq"), sem("dve_seq")
        consts = sem("consts")
        sq_done = sem("sq_done")
        u_done = sem("u_done")
        th_done = sem("th_done")
        rope_r, rope_s = sem("rope_r"), sem("rope_s")
        lb_e = sem("lb_e")
        lb_d = sem("lb_d")
        roped = sem("roped")
        mx_ready, ex_ready, rl_ready = sem("mx_ready"), sem("ex_ready"), sem("rl_ready")
        p_ready, pv_done, oh_done = sem("p_ready"), sem("pv_done"), sem("oh_done")
        sg_done, fg_done, ln_done = sem("sg_done"), sem("fg_done"), sem("ln_done")
        scan_done = sem("scan_done")
        diff_done, e_done, wl_done = sem("diff_done"), sem("e_done"), sem("wl_done")
        osq_done, oss_done, ostd_done = sem("osq_done"), sem("oss_done"), sem("ostd_done")
        hh_done = sem("hh_done")
        wr_hi_d, wr_split = sem("wr_hi_d"), sem("wr_split")
        rt_d, rt_e = sem("rt_d"), sem("rt_e")
        mask_done, rounds_in = sem("mask_done"), sem("rounds_in")
        s_done, g_ready = sem("s_done"), sem("g_ready")
        out_done, stored = sem("out_done"), sem("stored")

        wa = w_in_attn[0]
        wrr = w_in_rec[0]
        stream = []
        for nb in range(4):
            stream += col_blocks(wa, nb * BLK, BLK)
        stream += [wa.rearrange("(k p) f -> p k f", p=P)[:, :, 4 * BLK:4 * BLK + 256]]
        for nb in range(2):
            stream += col_blocks(w_out_attn[0], nb * BLK, BLK)
        for b in range(FB):
            stream += col_blocks(w_gate_dense[0], b * BLK, BLK) + col_blocks(w_up_dense[0], b * BLK, BLK)
        down = w_down_dense[0].rearrange("(u k p) n -> p u k n", p=P, k=2)
        stream += [down[:, u] for u in range(FCH // 2)]
        narrow = wrr.rearrange("(k p) f -> p k f", p=P)
        for first in (D, 0):
            stream += [narrow[:, :, first + 256 * j:first + 256 * j + 256] for j in range(4)]
        for first in (2 * D, 3 * D):
            for nb in range(2):
                stream += col_blocks(wrr, first + nb * BLK, BLK)
        for nb in range(2):
            stream += col_blocks(w_out_rec[0], nb * BLK, BLK)
        U0 = len(stream)
        assert FFN_UNITS % RAW == 0 and FFN_UNITS % SPL == 0

        FILLS = {GATE: 4, GATE + 1: 3 + 1, UP: 4, UP + 1: 3 + 1, TR: 2 + 1 + 4, TR + 1: 2 + 3, YB: 1, YB + 1: 1}
        FULLS = {GATE + 1: 1, UP + 1: 1, TR: 7, TR + 1: 5}
        ROUND = dict([(f"fill{b}", c) for b, c in FILLS.items()] + [(f"full{b}", c) for b, c in FULLS.items()],
                     unit=FFN_UNITS)

        block = ctx.enter_context(nc.Block())

        @block.sync
        def _(sp):
            n = Tally()
            xv = x[0].rearrange("(t p) d -> p t d", p=P)
            for t in range(TT):
                sp.dma_start(X[:, t, :], xv[:, t, :]).then_inc(x_in, 16)

            def load(src, k):
                seen = n.step("unit")
                if k >= RAW:
                    sp.wait_ge(lo_done, n.at("unit", RAW))
                shape = src.shape
                dst = raw[:, k % RAW, :]
                if len(shape) == 4:
                    dst = dst.rearrange("p (e k n) -> p e k n", e=1, k=shape[2])
                else:
                    dst = dst.rearrange("p (k n) -> p k n", k=shape[1])
                sp.dma_start(dst, src).then_inc(loaded[k % RAW], 16)

            for k, src in enumerate(stream):
                load(src, k)

            gv = w_gate_moe[0].rearrange("e (k p) f -> p e k f", p=P)
            uv = w_up_moe[0].rearrange("e (k p) f -> p e k f", p=P)
            dv = w_down_moe[0].rearrange("e (u k p) n -> p e u k n", p=P, k=2)

            def expert_unit(u, e):
                if u >= 4 * FB:
                    return dv[:, bass.ds(e, 1), u - 4 * FB]
                b, h = u // 4, u % 2
                return (gv, uv)[u % 4 // 2][:, bass.ds(e, 1), 4 * h:4 * h + 4, b * BLK:(b + 1) * BLK]

            for u in range(LEAD):
                load(expert_unit(u, 0), U0 + u)
            sp.wait_ge(rounds_in, 1)
            nr = sp.value_load(nrounds[0:1, 0:1], min_val=NE, max_val=2 * NE)
            with sp.Fori(0, nr) as i:
                n.enter(i, {"unit": FFN_UNITS})
                for u in range(LEAD, FFN_UNITS + LEAD):
                    e = (i + 1) % NE if u >= FFN_UNITS else i % NE if u < 4 * FB else (i + NE) % NE
                    load(expert_unit(u % FFN_UNITS, e), U0 + u)
                n.leave(nr)
            for r in range(RAW):
                sp.wait_ge(loaded[r], nr * (16 * FFN_UNITS // RAW) + 16 * len(range(r, U0 + LEAD, RAW)))

            ov = out[0].rearrange("(t p) d -> p t d", p=P)
            for t in range(TT):
                sp.wait_ge(out_done, t + 1)
                sp.dma_start(ov[:, t, :], outb[:, t, :]).then_inc(stored, 16)
            sp.wait_ge(stored, 16 * TT)

        @block.gpsimd
        def _(pool):
            pool.memset(ident[:], 0.0).then_inc(pool_seq, 1)
            pool.memset(tri[:], 1.0).then_inc(pool_seq, 1)
            pool.memset(ones[:], 1.0).then_inc(consts, 1)
            pool.memset(epsc[:, 0:1], EPS).then_inc(consts, 1)
            pool.memset(epsc[:, 1:2], float(np.pi / 2)).then_inc(consts, 1)
            pool.wait_ge(pool_seq, 2)
            pool.affine_select(out=ident[:], in_=ident[:], compare_op=ALU.not_equal, fill=1.0, base=0,
                               pattern=[[-1, P]], channel_multiplier=1).then_inc(consts, 1)
            pool.affine_select(out=tri[:], in_=tri[:], compare_op=ALU.is_gt, fill=0.0, base=0,
                               pattern=[[1, P]], channel_multiplier=-1).then_inc(consts, 1)
            pool.iota(slots[:], pattern=[[1, P]], base=0, channel_multiplier=0,
                      allow_small_or_imprecise_dtypes=True).then_inc(consts, 1)
            pool.iota(iota8[:], pattern=[[1, 8]], base=0, channel_multiplier=0,
                      allow_small_or_imprecise_dtypes=True).then_inc(consts, 1)
            pool.iota(mi[:, 0, 0:P], pattern=[[-1, P]], base=0, channel_multiplier=1).then_inc(consts, 1)
            pool.iota(mi[:, 0, P:3 * P], pattern=[[-1, TOK]], base=P, channel_multiplier=1).then_inc(consts, 1)
            pool.iota(mi[:, 1, 0:P], pattern=[[0, P]], base=0, channel_multiplier=1).then_inc(consts, 1)
            pool.iota(mi[:, 1, P:2 * P], pattern=[[1, P]], base=0, channel_multiplier=0).then_inc(consts, 1)
            pool.iota(mi[:, 1, 2 * P:3 * P], pattern=[[1, P]], base=0, channel_multiplier=-1).then_inc(consts, 1)

            for h in range(AH + BH):
                pool.wait_ge(rl_ready, h + 1)
                s = h % 3
                pool.tensor_scalar(sc[:, s, 0:P], sc[:, s, 0:P], att[:, s, 6:7], None,
                                   ALU.mult).then_inc(p_ready, 1)
                pool.tensor_scalar(sc[:, s, P:3 * P], sc[:, s, P:3 * P], att[:, s, 7:8], None,
                                   ALU.mult).then_inc(p_ready, 1)

            pool.wait_ge(scan_done, 4)
            for idx in range(16):
                lev, hf = idx // 2, idx % 2
                half = P >> lev
                if idx >= 2:
                    pool.wait_ge(wl_done, 2 * (idx - 1))
                bv = bT[:, hf * 1024:(hf + 1) * 1024].rearrange("p (n two h) -> p n two h", two=2, h=half)
                ev = ex[:, idx % 2, :].rearrange("p (n two h) -> p n two h", two=2, h=half)
                mid = spread(bv[:, :, 0, half - 1:half], 2, half)
                pool.tensor_tensor(ev[:, :, 0, :], mid, bv[:, :, 0, :], ALU.subtract).then_inc(diff_done, 1)
                if lev == 0:
                    pool.tensor_copy(ev[:, :, 1, :], bv[:, :, 1, :]).then_inc(diff_done, 1)
                else:
                    pool.tensor_tensor(ev[:, :, 1, :], bv[:, :, 1, :], mid, ALU.subtract).then_inc(diff_done, 1)

        @block.scalar
        def _(act):
            n = Tally()

            def link(ins):
                ins.then_inc(act_seq, 1)
                act.wait_ge(act_seq, n.step("seq"))

            def wait_full(b):
                n.step(f"fill{b}")
                act.wait_ge(full[b], n.step(f"full{b}"))

            def wait_units(k, *banks):
                saw_product(*banks)
                act.wait_ge(unit_done, unit_at(k))

            def unit_at(k):
                return k if n.var is None else n.var * FFN_UNITS + k

            def saw_product(*banks):
                for b in banks:
                    n.step(f"fill{b}")

            def drained(*banks):
                for b in banks:
                    act.wait_ge(free[b], n.at(f"fill{b}"))

            def saw(*banks):
                for b in banks:
                    n.step(f"fill{b}")
                    n.step(f"full{b}")

            def split_to(k):
                while n.count.get("u", 0) < k:
                    u = n.count["u"] = n.count.get("u", 0) + 1
                    n.step("unit")
                    r = (u - 1) % RAW
                    act.wait_ge(loaded[r], n.step(f"loaded{r}", 16))
                    if u > SPL:
                        act.wait_ge(unit_done, n.at("unit", SPL))
                    act.activation(w_hi[:, (u - 1) % SPL, :], raw[:, r, :], ACT.Copy).then_inc(hi_done, 1)

            act.dma_start(rows[0:16, :], g_mix.rearrange("l (k p) -> (l k) p", p=P)).then_inc(small_in, 16)
            act.dma_start(rows[16:32, :], g_ffn.rearrange("l (k p) -> (l k) p", p=P)).then_inc(small_in, 16)
            act.dma_start(rows[32:40, :], rec_norm_g.rearrange("l (k p) -> (l k) p", p=P)).then_inc(small_in, 16)
            act.dma_start(rows[40:56, :], rec_lower_bounds.rearrange("l (k p) -> (l k) p", p=P)).then_inc(small_in, 16)
            act.dma_start(gfr[0:1, 0:D], g_final.rearrange("(a n) -> a n", a=1)).then_inc(row_in, 16)
            act.dma_start(gfr[0:1, D:D + 8], attn_sinks).then_inc(row_in, 16)
            for t in range(TT):
                act.dma_start(posi[:, t:t + 1],
                              positions[0, t * P:(t + 1) * P].rearrange("(p o) -> p o", o=1)).then_inc(pos_in, 16)
            act.dma_start(wr[:], w_router[0].rearrange("(k p) e -> p k e", p=P)).then_inc(wr_in, 16)

            def rms(step, tiles_ready):
                tiles_ready()
                for t in range(TT):
                    link(act.activation(U[:, t, :], X[:, t, :], ACT.Square, accum_out=ss[:, t:t + 1]))
                act.activation(ss[:, 2:4], ss[:, 0:2], ACT.Sqrt, scale=1.0 / D,
                               bias=epsc[:, 0:1]).then_inc(sq_done, 1)

            def t_hi_part(gain):
                for j in range(4):
                    wait_full(j)
                    for c in range(2):
                        k = 2 * j + c
                        act.activation(t_hi[:, k, :], bank[j][:, c * TOK:(c + 1) * TOK], ACT.Copy,
                                       scale=col[:, gain + k:gain + k + 1]).then_inc(th_done, 1)

            def x_loaded():
                act.wait_ge(x_in, 16 * TT)
                act.wait_ge(consts, 12)

            def x_updated(k):
                return lambda: drained(*((YB, YB + 1, GATE, GATE + 1) if k == 2 else (0, 1, 2, 3)))

            rms(0, x_loaded)
            saw(4, 7)
            act.wait_ge(free[4], 1)
            split_to(1)
            t_hi_part(0)
            split_to(SPL)
            act.wait_ge(lb_d, 1)
            act.activation(lbc[:, 1:3, :], lbc[:, 1:3, :], ACT.Exp).then_inc(lb_e, 1)
            act.wait_ge(rope_r, 1)
            act.activation(rope[:, 5, :, :], rope[:, 3, :, :], ACT.Sin).then_inc(rope_s, 1)
            act.activation(rope[:, 6, :, :], rope[:, 4, :, :], ACT.Sin, scale=-1.0,
                           bias=epsc[:, 1:2]).then_inc(rope_s, 1)
            act.wait_ge(wr_in, 16)
            act.activation(wr_hi[:], wr[:], ACT.Copy).then_inc(wr_hi_d, 1)

            for nb in range(5):
                split_to(min(2 * nb + 2, 9) + SPL)
                b0 = 2 * nb % 8
                saw_product(b0 + 1)
                wait_units(min(2 * nb + 2, 9), b0)
                to, src = proj_place(nb, 0, bank[b0])
                act.activation(to, src, ACT.Copy).then_inc(free[b0], 1)

            split_to(9 + SPL)
            for j in range(7):
                wait_full(j)
                if j % 2 == 0:
                    c = min(2, 13 - 2 * j)
                    act.activation(qkT[:, 2 * j:2 * j + c, :],
                                   bank[j][:, 0:c * TOK].rearrange("p (c n) -> p c n", c=c),
                                   ACT.Copy).then_inc(free[j], 1)

            for s in range(AH + BH + 3):
                if s < AH + BH:
                    k, g = s % 3, s >= AH
                    saw(k)
                    act.wait_ge(mx_ready, s + 1)
                    act.activation(sc[:, k, 0:P], sc[:, k, 0:P], ACT.Exp, scale=SCALE,
                                   bias=att[:, k, 2:3], accum_out=att[:, k, 4:5]).then_inc(ex_ready, 1)
                    act.activation(sc[:, k, P:3 * P], sc[:, k, P:3 * P], ACT.Exp, scale=SCALE,
                                   bias=att[:, k, 3:4], accum_out=att[:, k, 5:6]).then_inc(ex_ready, 1)
                    if g:
                        act.activation(att[:, k, 8:10], att[:, k, 10:12], ACT.Exp,
                                       scale=SCALE).then_inc(ex_ready, 1)
                if 0 <= s - 2 < AH + BH:
                    h = s - 2
                    wait_full(3 + h % 2)
                    if h >= 2:
                        act.wait_ge(pv_done, h - 1)
                    act.activation(pT[:, h % 2, :], bank[3 + h % 2][:, 0:3 * P],
                                   ACT.Copy).then_inc(free[3 + h % 2], 1)
                if s - 3 >= 0 and (s - 3) % 2 == 1:
                    j = (s - 3) // 2
                    saw_product(5 + j % 2)
                    act.wait_ge(pv_done, 2 * j + 2)
                    act.activation(t_hi[:, j, :], bank[5 + j % 2][:, 0:TOK], ACT.Copy).then_inc(oh_done, 1)

            def out_proj(base):
                split_to(base + 4)
                saw_product(0, 1, 2, 3)

            def next_stage(k, gain, base):
                split_to(base + SPL)
                rms(k, x_updated(k))
                t_hi_part(gain)

            out_proj(9)
            next_stage(1, 16, 13)

            def ffn_dense(base):
                for b in range(FB):
                    split_to(base + 4 * b + 5)
                    wait_units(base + 4 * b + 2, GATE, GATE + 1)
                    for t in range(TT):
                        act.activation(H[:, t, b * BLK:(b + 1) * BLK], bank[GATE + t][:],
                                       ACT.Silu).then_inc(free[GATE + t], 1)
                    saw_product(UP, UP + 1)
                    if b == FB - 1:
                        for g in range(2):
                            hidden_hi(g)
                for g in range(2, 14):
                    split_to(base + 28 + g - 2 + 1 + SPL)
                    hidden_hi(g)
                split_to(base + FFN_UNITS)
                saw_product(GATE, GATE + 1, YB, YB + 1)

            def hidden_hi(g):
                wait_full(TR + g % 2)
                act.activation(h_hi[:, g % 2, :], bank[TR + g % 2][:], ACT.Copy).then_inc(hh_done, 1)

            ffn_dense(13)
            next_stage(2, 8, 55)

            for j in range(4):
                split_to(55 + j + 1 + SPL)
                wait_units(55 + j + 1, j)
                act.activation(bT[:, j * BLK:(j + 1) * BLK], bank[j][:], ACT.Sigmoid).then_inc(free[j], 1)
            for j in range(4):
                split_to(59 + j + 1 + SPL)
                wait_units(59 + j + 1, 4 + j)
                act.activation(qT[:, j * BLK:(j + 1) * BLK], bank[4 + j][:], ACT.Silu).then_inc(free[4 + j], 1)
            for j in range(4):
                act.wait_ge(fg_done, 2 * (j + 1))
                act.activation(bT[:, j * BLK:(j + 1) * BLK], bT[:, j * BLK:(j + 1) * BLK],
                               ACT.Ln).then_inc(ln_done, 1)
            split_to(67 + SPL)
            saw_product(0, 1, 2, 3)
            for nb in range(2):
                split_to(67 + 2 * nb + 2 + SPL)
                wait_units(67 + 2 * nb + 2, 4 + 2 * nb, 5 + 2 * nb)
                for t in range(TT):
                    act.activation(U[:, t, nb * BLK:(nb + 1) * BLK], bank[4 + 2 * nb + t][:],
                                   ACT.Silu).then_inc(free[4 + 2 * nb + t], 1)
            for idx in range(16):
                act.wait_ge(diff_done, 2 * (idx + 1))
                act.activation(ex[:, idx % 2, :], ex[:, idx % 2, :], ACT.Exp).then_inc(e_done, 1)
            for f in range(2 + 32):
                saw(f % 8)
            for f in range(4):
                b = (34 + f) % 8
                wait_full(b)
                act.activation(sq[:, f, :], bank[b][:], ACT.Square).then_inc(osq_done, 1)
            act.wait_ge(oss_done, 4)
            act.activation(ss16[:, 1, :, :], ss16[:, 0, :, :], ACT.Sqrt, scale=1.0 / P,
                           bias=epsc[:, 0:1]).then_inc(ostd_done, 1)
            t_hi_part(32)
            out_proj(71)
            next_stage(3, 24, U0)

            saw(4, 5)
            act.wait_ge(rt_d, 1)
            act.activation(rt[:, 5, :, 0:1], rt[:, 4, :, 0:1], ACT.Exp).then_inc(rt_e, 1)

            def gather_hi():
                for m, b in enumerate((GATE + 1, UP + 1)):
                    wait_full(b)
                    for c in range(4):
                        k = 4 * m + c
                        act.activation(t_hi[:, k, 0:CAP], bank[b][:, c * P:(c + 1) * P], ACT.Copy,
                                       scale=col[:, 24 + k:25 + k]).then_inc(th_done, 1)

            def y_copy():
                for m in range(2):
                    act.activation(Y[:, m * BLK:(m + 1) * BLK], bank[YB + m][:], ACT.Copy).then_inc(free[YB + m], 1)

            for m in range(2):
                wait_full(6 + m)
                act.activation(gf[:, m * BLK:(m + 1) * BLK], bank[6 + m][:], ACT.Copy).then_inc(free[6 + m], 1)
            gather_hi()
            wait_full(YB)
            wait_full(YB + 1)
            nr = act.value_load(nrounds[0:1, 0:1], min_val=NE, max_val=2 * NE)
            with act.Fori(0, nr) as i:
                n.enter(i, dict(ROUND, **{f"loaded{r}": 16 * FFN_UNITS // RAW for r in range(RAW)}))
                wait_units(U0, YB, YB + 1)
                y_copy()
                for b in range(FB):
                    if b == 3:
                        split_to(U0 + 4 * b + 3)
                        wait_full(TR)
                        act.activation(GT[:], bank[TR][:, 0:TOK], ACT.Copy).then_inc(free[TR], 1)
                    split_to(U0 + 4 * b + 5)
                    wait_units(U0 + 4 * b + 2, GATE + b % 2)
                    act.activation(H[:, 0, b * BLK:(b + 1) * BLK], bank[GATE + b % 2][:],
                                   ACT.Silu).then_inc(free[GATE + b % 2], 1)
                    saw_product(UP + b % 2)
                    if b < 2:
                        saw(TR, TR + 1)
                for g in range(2):
                    hidden_hi(g)
                split_to(U0 + 28 + SPL)
                gather_hi()
                for g in range(2, 7):
                    split_to(U0 + 28 + 2 * (g - 2) + 2 + SPL)
                    hidden_hi(g)
                split_to(U0 + FFN_UNITS + SPL)
                n.count["u"] = U0 + SPL
                n.leave(nr)
            act.wait_ge(unit_done, nr * FFN_UNITS + U0)
            y_copy()
            saw(TR, TR + 1, TR, TR + 1)
            drained(TR, TR + 1)
            for t in range(TT):
                link(act.activation(U[:, t, :], X[:, t, :], ACT.Square, accum_out=ss[:, t:t + 1]))
            act.activation(ss[:, 2:4], ss[:, 0:2], ACT.Sqrt, scale=1.0 / D, bias=epsc[:, 0:1]).then_inc(sq_done, 1)

        @block.vector
        def _(dve):
            n = Tally()

            def link(ins):
                ins.then_inc(dve_seq, 1)
                dve.wait_ge(dve_seq, n.step("seq"))

            def wait_full(b):
                n.step(f"fill{b}")
                dve.wait_ge(full[b], n.step(f"full{b}"))

            def wait_units(k, *banks):
                saw_product(*banks)
                dve.wait_ge(unit_done, unit_at(k))

            def unit_at(k):
                return k if n.var is None else n.var * FFN_UNITS + k

            def saw_product(*banks):
                for b in banks:
                    n.step(f"fill{b}")

            def drained(*banks):
                for b in banks:
                    dve.wait_ge(free[b], n.at(f"fill{b}"))

            def saw(*banks):
                for b in banks:
                    n.step(f"fill{b}")
                    n.step(f"full{b}")

            def split_to(k):
                while n.count.get("u", 0) < k:
                    u = n.count["u"] = n.count.get("u", 0) + 1
                    dve.wait_ge(hi_done, n.step("unit"))
                    s, r = (u - 1) % SPL, (u - 1) % RAW
                    dve.tensor_tensor(w_lo[:, s, :], raw[:, r, :], w_hi[:, s, :].bitcast(F32),
                                      ALU.subtract).then_inc(lo_done, 1)

            def normalise(k):
                dve.wait_ge(sq_done, k + 1)
                link(dve.reciprocal(ss[:, 4:6], ss[:, 2:4]))
                for t in range(TT):
                    dve.tensor_scalar(U[:, t, :], X[:, t, :], ss[:, 4 + t:5 + t], None,
                                      ALU.mult).then_inc(u_done, 1)

            def t_lo_part(gain):
                for j in range(4):
                    wait_full(j)
                    dve.wait_ge(th_done, n.step("th", 2))
                    for c in range(2):
                        k = 2 * j + c
                        ins = dve.scalar_tensor_tensor(
                            t_lo[:, k, :], bank[j][:, c * TOK:(c + 1) * TOK], col[:, gain + k:gain + k + 1],
                            t_hi[:, k, :].bitcast(F32), ALU.mult, ALU.subtract)
                        if c == 1:
                            ins.then_inc(free[j], 1)

            dve.wait_ge(consts, 12)
            dist = mi[:, 0, :]
            f = [mf[:, i, :] for i in range(5)]
            link(dve.tensor_copy(f[0], dist))
            link(dve.tensor_scalar(mi[:, 2, :], dist, 3, None, ALU.bitwise_and))
            link(dve.tensor_scalar(f[1], mi[:, 2, :], 0, None, ALU.is_equal))
            link(dve.tensor_scalar(mi[:, 2, :], dist, 15, None, ALU.bitwise_and))
            link(dve.tensor_scalar(f[2], mi[:, 2, :], 0, None, ALU.is_equal))
            link(dve.tensor_tensor(f[1], f[1], f[2], ALU.add))
            link(dve.tensor_scalar(f[2], f[0], float(WIN_A), None, ALU.is_le))
            link(dve.tensor_tensor(f[1], f[1], f[2], ALU.add))
            link(dve.tensor_scalar(f[2], f[0], 0.0, None, ALU.is_ge))
            link(dve.tensor_tensor(f[1], f[1], f[2], ALU.mult))
            link(dve.tensor_scalar(f[3], f[1], 0.0, -BIG, ALU.is_equal, ALU.mult))
            link(dve.tensor_scalar(f[4], f[1], 2.0, float(8 * np.log(2.0)), ALU.is_equal, ALU.mult))
            link(dve.tensor_tensor(f[3], f[3], f[4], ALU.add))
            link(dve.tensor_scalar(f[4], f[1], 3.0, float(8 * np.log(3.0)), ALU.is_equal, ALU.mult))
            link(dve.tensor_tensor(biasA[:], f[3], f[4], ALU.add))
            link(dve.tensor_scalar(f[4], f[0], float(WIN_B), None, ALU.is_le))
            link(dve.tensor_tensor(f[4], f[4], f[2], ALU.mult))
            link(dve.tensor_scalar(biasB[:], f[4], -1.0, BIG, ALU.add, ALU.mult))
            link(dve.tensor_tensor(mi[:, 2, 0:P], mi[:, 1, 0:P], mi[:, 1, P:2 * P], ALU.bitwise_xor))
            link(dve.tensor_copy(f[0][:, 0:P], mi[:, 2, 0:P]))
            link(dve.tensor_scalar(f[1][:, 0:P], mi[:, 1, 2 * P:3 * P], 0.0, 1e9, ALU.is_lt, ALU.mult))
            link(dve.tensor_tensor(f[0][:, 0:P], f[0][:, 0:P], f[1][:, 0:P], ALU.add))
            for lev in range(8):
                link(dve.tensor_scalar(lev_mask[:, lev, :], f[0][:, 0:P], float(P >> lev), None, ALU.is_lt))

            saw(4, 7)
            normalise(0)
            dve.wait_ge(full[4], 1)
            dve.tensor_copy(col[:], bank[4][:, 0:56]).then_inc(free[4], 1)
            dve.wait_ge(free[4], 1)
            dve.wait_ge(full[7], 1)
            dve.tensor_scalar(sk8[:], bank[7][:, 0:8], 1.0 / SCALE, None, ALU.mult).then_inc(free[7], 1)
            split_to(1)
            t_lo_part(0)
            split_to(SPL)

            link(dve.tensor_tensor(lbc[:, 0, :], col[:, 40:48], col[:, 48:56], ALU.max))
            link(dve.tensor_tensor(lbc[:, 1, :], col[:, 40:48], lbc[:, 0, :], ALU.subtract))
            dve.tensor_tensor(lbc[:, 2, :], col[:, 48:56], lbc[:, 0, :], ALU.subtract).then_inc(lb_d, 1)
            dve.wait_ge(pos_in, 16 * TT)
            link(dve.tensor_copy(posf[:], posi[:]))
            inv = [float(np.float32(THETA) ** np.float32(-2.0 * j / ROT)) for j in range(ROT // 2)]
            for j in range(ROT // 2):
                dve.memset(rope[:, 0, 0, j:j + 1], inv[j]).then_inc(dve_seq, 1)
                n.step("seq")
            dve.wait_ge(dve_seq, n.at("seq"))
            ang = rope[:, 1]
            for t in range(TT):
                link(dve.tensor_scalar(ang[:, t, :], rope[:, 0, 0, :], posf[:, t:t + 1], None, ALU.mult))
            turn, red = rope[:, 2], rope[:, 3]
            magic = 1.5 * 2.0 ** 23
            c1 = 6.28125
            c2 = float(np.float32(round((2 * np.pi - c1) * 2 ** 20) / 2 ** 20))
            c3 = 2 * np.pi - c1 - c2
            link(dve.tensor_scalar(turn, ang, float(1 / (2 * np.pi)), magic, ALU.mult, ALU.add))
            link(dve.tensor_scalar(turn, turn, -magic, None, ALU.add))
            link(dve.scalar_tensor_tensor(red, turn, -c1, ang, ALU.mult, ALU.add))
            link(dve.scalar_tensor_tensor(red, turn, -c2, red, ALU.mult, ALU.add))
            link(dve.scalar_tensor_tensor(red, turn, -c3, red, ALU.mult, ALU.add))
            link(dve.tensor_scalar(red, red, 3.1415925, -3.1415925, ALU.min, ALU.max))
            dve.scalar_tensor_tensor(rope[:, 4], red, -1.0, red, ALU.mult, ALU.max).then_inc(rope_r, 1)
            dve.wait_ge(lb_e, 1)
            link(dve.tensor_tensor(lbc[:, 3, :], lbc[:, 1, :], lbc[:, 2, :], ALU.add))
            link(dve.reciprocal(lbc[:, 4, :], lbc[:, 3, :]))
            link(dve.tensor_tensor(lbc[:, 1, :], lbc[:, 1, :], lbc[:, 4, :], ALU.mult))
            link(dve.tensor_tensor(lbc[:, 2, :], lbc[:, 2, :], lbc[:, 4, :], ALU.mult))
            link(dve.tensor_tensor(lbc[:, 3, :], lbc[:, 1, :], lbc[:, 2, :], ALU.add))
            link(dve.tensor_tensor(lbc[:, 5, :], lbc[:, 3, :], lbc[:, 1, :], ALU.subtract))
            link(dve.tensor_scalar(lbc[:, 6, :], lbc[:, 5, :], -1.0, 1.0, ALU.mult, ALU.add))
            dve.wait_ge(wr_hi_d, 1)
            dve.tensor_tensor(wr_lo[:], wr[:], wr_hi[:].bitcast(F32), ALU.subtract).then_inc(wr_split, 1)

            for nb in range(5):
                split_to(min(2 * nb + 2, 9) + SPL)
                b0 = 2 * nb % 8
                saw_product(b0)
                wait_units(min(2 * nb + 2, 9), b0 + 1)
                to, src = proj_place(nb, 1, bank[b0 + 1])
                dve.tensor_copy(to, src).then_inc(free[b0 + 1], 1)

            dve.wait_ge(rope_s, 2)
            drained(*range(8))
            x1, x2 = proj[:, :, 0:26, 0:8], proj[:, :, 0:26, 8:16]
            sin = spread(rope[:, 5].rearrange("p t (o d) -> p t o d", o=1), 2, 26)
            cos = spread(rope[:, 6].rearrange("p t (o d) -> p t o d", o=1), 2, 26)
            r = [rp[:, i] for i in range(4)]
            dve.tensor_tensor(r[0], x1, cos, ALU.mult).then_inc(dve_seq, 1)
            dve.tensor_tensor(r[1], x2, sin, ALU.mult).then_inc(dve_seq, 1)
            dve.tensor_tensor(r[2], x2, cos, ALU.mult).then_inc(dve_seq, 1)
            dve.tensor_tensor(r[3], x1, sin, ALU.mult).then_inc(dve_seq, 1)
            n.step("seq", 4)
            dve.wait_ge(dve_seq, n.at("seq"))
            dve.tensor_tensor(x1, r[0], r[1], ALU.subtract).then_inc(roped, 1)
            dve.tensor_tensor(x2, r[2], r[3], ALU.add).then_inc(roped, 1)

            split_to(9 + SPL)
            for j in range(7):
                wait_full(j)
                if j % 2 == 1:
                    dve.tensor_copy(qkT[:, 2 * j:2 * j + 2, :],
                                    bank[j][:].rearrange("p (c n) -> p c n", c=2)).then_inc(free[j], 1)

            for s in range(AH + BH + 3):
                if s < AH + BH:
                    k, g = s % 3, s >= AH
                    if s >= 3:
                        dve.wait_ge(full[3 + (s - 3) % 2], n.at(f"full{3 + (s - 3) % 2}"))
                    wait_full(k)
                    bias = biasB if g else biasA
                    dve.tensor_tensor_reduce(out=sc[:, k, 0:P], in0=bank[k][:, 0:P], in1=bias[:, 0:P], scale=1.0,
                                             scalar=-BIG, op0=ALU.add, op1=ALU.max,
                                             accum_out=att[:, k, 0:1]).then_inc(dve_seq, 1)
                    dve.tensor_tensor_reduce(out=sc[:, k, P:3 * P], in0=bank[k][:, P:3 * P], in1=bias[:, P:3 * P],
                                             scale=1.0, scalar=-BIG, op0=ALU.add, op1=ALU.max,
                                             accum_out=att[:, k, 1:2]).then_inc(free[k], 1)
                    n.step("seq")
                    dve.wait_ge(dve_seq, n.at("seq"))
                    dve.wait_ge(free[k], n.at(f"fill{k}"))
                    if g:
                        hb = s - AH
                        skc = spread(sk8[:, hb:hb + 1], 1, 2)
                        link(dve.tensor_tensor(att[:, k, 0:2], att[:, k, 0:2], skc, ALU.max))
                        link(dve.tensor_tensor(att[:, k, 10:12], skc, att[:, k, 0:2], ALU.subtract))
                    dve.tensor_scalar(att[:, k, 2:4], att[:, k, 0:2], -SCALE, None, ALU.mult).then_inc(mx_ready, 1)
                if 0 <= s - 1 < AH + BH:
                    h = s - 1
                    k, g = h % 3, h >= AH
                    dve.wait_ge(ex_ready, n.step("ex", 3 if g else 2))
                    if g:
                        link(dve.tensor_tensor(att[:, k, 4:6], att[:, k, 4:6], att[:, k, 8:10], ALU.add))
                    dve.reciprocal(att[:, k, 6:8], att[:, k, 4:6]).then_inc(rl_ready, 1)
                if 0 <= s - 2 < AH + BH:
                    saw(3 + (s - 2) % 2)
                if s - 3 >= 0 and (s - 3) % 2 == 1:
                    j = (s - 3) // 2
                    saw_product(5 + j % 2)
                    dve.wait_ge(oh_done, j + 1)
                    dve.tensor_tensor(t_lo[:, j, :], bank[5 + j % 2][:, 0:TOK], t_hi[:, j, :].bitcast(F32),
                                      ALU.subtract).then_inc(free[5 + j % 2], 1)

            def out_proj(base):
                split_to(base + 4)
                for nb in range(2):
                    wait_units(base + 2 * nb + 2, 2 * nb, 2 * nb + 1)
                    for t in range(TT):
                        dve.tensor_tensor(X[:, t, nb * BLK:(nb + 1) * BLK], X[:, t, nb * BLK:(nb + 1) * BLK],
                                          bank[2 * nb + t][:], ALU.add).then_inc(free[2 * nb + t], 1)

            def hidden_lo(g):
                wait_full(TR + g % 2)
                dve.wait_ge(hh_done, n.step("hh"))
                dve.tensor_tensor(h_lo[:, g % 2, :], bank[TR + g % 2][:], h_hi[:, g % 2, :].bitcast(F32),
                                  ALU.subtract).then_inc(free[TR + g % 2], 1)

            out_proj(9)
            split_to(13 + SPL)
            normalise(1)
            t_lo_part(16)

            def h_block(b, t, up_bank, gate_bank):
                drained(gate_bank)
                hb = H[:, t, b * BLK:(b + 1) * BLK]
                dve.tensor_tensor(hb, hb, bank[up_bank][:], ALU.mult).then_inc(free[up_bank], 1)

            base = 13
            for b in range(FB):
                if b == FB - 1:
                    split_to(base + 4 * b + 5)
                    for g in range(2):
                        hidden_lo(g)
                split_to(base + 4 * b + 7)
                saw_product(GATE, GATE + 1)
                wait_units(base + 4 * b + 4, UP, UP + 1)
                for t in range(TT):
                    h_block(b, t, UP + t, GATE + t)
            for g in range(2, 14):
                split_to(base + 28 + g - 2 + 1 + SPL)
                hidden_lo(g)
            split_to(base + FFN_UNITS)
            ybank = (YB, YB + 1, GATE, GATE + 1)
            wait_units(base + FFN_UNITS, *ybank)
            for t in range(TT):
                for nb in range(2):
                    b = ybank[2 * t + nb]
                    dve.tensor_tensor(X[:, t, nb * BLK:(nb + 1) * BLK], X[:, t, nb * BLK:(nb + 1) * BLK],
                                      bank[b][:], ALU.add).then_inc(free[b], 1)
            split_to(55 + SPL)
            normalise(2)
            t_lo_part(8)

            dve.memset(reset[:], 1.0).then_inc(dve_seq, 1)
            n.step("seq")
            dve.wait_ge(dve_seq, n.at("seq"))
            link(dve.memset(reset[:].rearrange("p (n c) -> p n c", c=P)[:, :, 0:1], 0.0))
            for j in range(4):
                split_to(55 + j + 1 + SPL)
                saw_product(j)
                drained(j)
                for c in range(2):
                    hd = 2 * j + c
                    fc = bT[:, hd * TOK:(hd + 1) * TOK]
                    link(dve.tensor_scalar(fc, fc, lbc[:, 6, hd:hd + 1], lbc[:, 5, hd:hd + 1], ALU.mult, ALU.add))
                    dve.tensor_scalar(kT[:, hd * TOK:(hd + 1) * TOK], fc, -1.0, 1.0, ALU.mult,
                                      ALU.add).then_inc(fg_done, 1)
            for j in range(4):
                split_to(59 + j + 1 + SPL)
                saw_product(4 + j)
            for j in range(4):
                dve.wait_ge(ln_done, j + 1)
                bj = bT[:, j * BLK:(j + 1) * BLK]
                dve.tensor_tensor_scan(bj, reset[:], bj, 0.0, ALU.mult, ALU.add).then_inc(scan_done, 1)
            for nb in range(2):
                split_to(63 + 2 * nb + 2 + SPL)
                wait_units(63 + 2 * nb + 2, 2 * nb, 2 * nb + 1)
                for t in range(TT):
                    b = 2 * nb + t
                    dve.tensor_copy(V[:, t, nb * BLK:(nb + 1) * BLK], bank[b][:]).then_inc(free[b], 1)
            split_to(71 + SPL)
            saw_product(4, 5, 6, 7)
            link(dve.memset(aT[:], 0.0))

            fill = [0]
            last_write = {}

            def collect(idx):
                lev, hf = idx // 2, idx % 2
                for m in range(1 if lev == 0 else 2):
                    b = fill[0] % 8
                    fill[0] += 1
                    wait_full(b)
                    if lev == 0:
                        dve.tensor_copy(aX[:, hf * BLK:(hf + 1) * BLK], bank[b][:]).then_inc(free[b], 1)
                    else:
                        mask = spread(lev_mask[:, lev - 1:lev, :], 1, 4)
                        o = aT[:, hf * 1024 + m * BLK:hf * 1024 + (m + 1) * BLK]
                        if lev > 1:
                            dve.wait_ge(free[last_write[hf, m][0]], last_write[hf, m][1])
                        dve.copy_predicated(o.rearrange("p (n c) -> p n c", c=P), mask,
                                            bank[b][:].rearrange("p (n c) -> p n c", c=P)).then_inc(free[b], 1)
                        last_write[hf, m] = b, n.at(f"fill{b}")

            for idx in range(16):
                hf, lev = idx % 2, idx // 2
                half = P >> lev
                dve.wait_ge(e_done, idx + 1)
                sl = slice(hf * 1024, (hf + 1) * 1024)
                kv = kT[:, sl].rearrange("p (n two h) -> p n two h", two=2, h=half)
                qv = qT[:, sl].rearrange("p (n two h) -> p n two h", two=2, h=half)
                ev = ex[:, idx % 2, :].rearrange("p (n two h) -> p n two h", two=2, h=half)
                wv = wl[:, idx % 2, :].rearrange("p (n two h) -> p n two h", two=2, h=half)
                dve.tensor_tensor(wv[:, :, 0, :], kv[:, :, 0, :], ev[:, :, 0, :], ALU.mult).then_inc(wl_done, 1)
                dve.tensor_tensor(wv[:, :, 1, :], qv[:, :, 1, :], ev[:, :, 1, :], ALU.mult).then_inc(wl_done, 1)
                if idx >= 1:
                    collect(idx - 1)
            for idx in range(15, 18):
                collect(idx)

            for f4 in range(4):
                t, hf = f4 // 2, f4 % 2
                saw((34 + f4) % 8)
                dve.wait_ge(osq_done, f4 + 1)
                dve.reduce_sum(ss16[:, 0, t, 4 * hf:4 * hf + 4],
                               sq[:, f4, :].rearrange("p (h v) -> p h v", h=4), AX.X).then_inc(oss_done, 1)
            dve.wait_ge(ostd_done, 1)
            link(dve.reciprocal(ss16[:, 2, :, :], ss16[:, 1, :, :]))
            for f4 in range(4):
                t, hf = f4 // 2, f4 % 2
                b = (34 + f4) % 8
                for c in range(4):
                    hd = 4 * hf + c
                    uv = U[:, t, hd * P:(hd + 1) * P]
                    ins = dve.scalar_tensor_tensor(uv, bank[b][:, c * P:(c + 1) * P], ss16[:, 2, t, hd:hd + 1],
                                                   uv, ALU.mult, ALU.mult)
                ins.then_inc(free[b], 1)
            t_lo_part(32)
            out_proj(71)
            split_to(U0 + SPL)
            normalise(3)
            t_lo_part(24)

            R = [rt[:, i] for i in range(12)]
            wait_full(4)
            dve.tensor_copy(R[0], bank[4][:, 0:16].rearrange("p (t e) -> p t e", t=TT)).then_inc(free[4], 1)
            drained(4)
            for t in range(TT):
                link(dve.max(R[1][:, t, :], R[0][:, t, :]))
                link(dve.max_index(rti[:, t, :], R[1][:, t, :], R[0][:, t, :]))
            link(dve.tensor_copy(R[2], rti[:]))
            dve.tensor_tensor(R[4][:, :, 0:1], R[1][:, :, 1:2], R[1][:, :, 0:1], ALU.subtract).then_inc(rt_d, 1)
            for t in range(TT):
                link(dve.tensor_scalar(R[6][:, t, :], iota8[:], R[2][:, t, 0:1], None, ALU.is_equal))
                link(dve.tensor_scalar(R[7][:, t, :], iota8[:], R[2][:, t, 1:2], None, ALU.is_equal))
            dve.tensor_tensor(R[8], R[6], R[7], ALU.add).then_inc(mask_done, 1)
            dve.wait_ge(rt_e, 1)
            link(dve.tensor_scalar(R[4][:, :, 1:2], R[5][:, :, 0:1], 1.0, None, ALU.add))
            link(dve.reciprocal(R[4][:, :, 2:3], R[4][:, :, 1:2]))
            link(dve.tensor_tensor(R[4][:, :, 3:4], R[5][:, :, 0:1], R[4][:, :, 2:3], ALU.mult))
            for t in range(TT):
                link(dve.tensor_scalar(R[9][:, t, :], R[6][:, t, :], R[4][:, t, 2:3], None, ALU.mult))
                link(dve.scalar_tensor_tensor(gates[:, t, 0:NE], R[7][:, t, :], R[4][:, t, 3:4], R[9][:, t, :],
                                              ALU.mult, ALU.add))
            link(dve.tensor_copy(gates[:, :, NE:2 * NE], gates[:, :, 0:NE]))
            link(dve.memset(gates[:, :, 2 * NE:2 * NE + 1], 0.0))
            wait_full(5)
            pos = bank[5][:, 0:16].rearrange("p (t e) -> p t e", t=TT)
            link(dve.tensor_scalar(R[10], pos, 1.0, None, ALU.add))
            link(dve.tensor_tensor(R[10], R[10], R[8], ALU.mult))
            link(dve.tensor_scalar(cols[:, :, 0:NE], R[10], -1.0, None, ALU.add))
            link(dve.tensor_scalar(cols[:, :, NE:2 * NE], R[10], -1.0 - CAP, None, ALU.add))
            link(dve.memset(cols[:, :, 2 * NE:2 * NE + 1], -1.0))
            dve.reduce_max(cnt[:, 0:1], bank[5][:, 16:24], AX.X).then_inc(free[5], 1)
            drained(5)
            link(dve.tensor_scalar(cnt[:, 1:2], cnt[:, 0:1], float(CAP), float(NE), ALU.is_gt, ALU.mult))
            link(dve.tensor_scalar(nrounds[:], cnt[:, 1:2], float(NE), None, ALU.add))
            dve.memset(GT[:], 0.0).then_inc(rounds_in, 1)

            def round_slots(i):
                link(dve.tensor_copy(cur[:, 0:2].rearrange("p (t o) -> p t o", o=1), cols[:, :, bass.ds(i, 1)]))
                link(dve.tensor_copy(cur[:, 2:4].rearrange("p (t o) -> p t o", o=1), gates[:, :, bass.ds(i, 1)]))
                for t in range(TT):
                    dve.tensor_scalar(S[:, t, :], slots[:], cur[:, t:t + 1], None, ALU.is_equal).then_inc(s_done, 1)
                n.step("s", 2)

            def gather_lo():
                for m, b in enumerate((GATE + 1, UP + 1)):
                    wait_full(b)
                    dve.wait_ge(th_done, n.step("th", 4))
                    for c in range(4):
                        k = 4 * m + c
                        ins = dve.scalar_tensor_tensor(
                            t_lo[:, k, 0:CAP], bank[b][:, c * P:(c + 1) * P], col[:, 24 + k:25 + k],
                            t_hi[:, k, 0:CAP].bitcast(F32), ALU.mult, ALU.subtract)
                    ins.then_inc(free[b], 1)

            def scatter_add(t):
                for m in range(2):
                    wait_full(TR + m)
                    dve.tensor_tensor(X[:, t, m * BLK:(m + 1) * BLK], X[:, t, m * BLK:(m + 1) * BLK],
                                      bank[TR + m][:], ALU.add).then_inc(free[TR + m], 1)

            dve.wait_ge(rounds_in, 1)
            round_slots(0)
            gather_lo()
            saw(YB, YB + 1, YB, YB + 1)
            nr = dve.value_load(nrounds[0:1, 0:1], min_val=NE, max_val=2 * NE)
            with dve.Fori(0, nr) as i:
                n.enter(i, dict(ROUND, seq=2, s=2, th=8, hh=7))
                dve.wait_ge(s_done, n.at("s"))
                for t in range(TT):
                    dve.tensor_scalar(G[:, t, :], S[:, t, :], cur[:, 2 + t:3 + t], None, ALU.mult).then_inc(g_ready, 1)
                saw_product(YB, YB + 1)
                for b in range(FB):
                    if b == FB - 1:
                        split_to(U0 + 4 * b + 5)
                        for g in range(2):
                            hidden_lo(g)
                    split_to(U0 + 4 * b + 7)
                    saw_product(GATE + b % 2)
                    wait_units(U0 + 4 * b + 4, UP + b % 2)
                    h_block(b, 0, UP + b % 2, GATE + b % 2)
                    if b < 2:
                        scatter_add(b)
                    if b == 3:
                        saw(TR)
                        dve.wait_ge(full[TR], n.at(f"full{TR}"))
                        round_slots(i + 1)
                gather_lo()
                for g in range(2, 7):
                    split_to(U0 + 28 + 2 * (g - 2) + 2 + SPL)
                    hidden_lo(g)
                split_to(U0 + FFN_UNITS + SPL)
                n.count["u"] = U0 + SPL
                n.leave(nr)
            for t in range(TT):
                scatter_add(t)
            drained(TR, TR + 1)
            dve.wait_ge(sq_done, 5)
            link(dve.reciprocal(ss[:, 4:6], ss[:, 2:4]))
            for t in range(TT):
                dve.scalar_tensor_tensor(outb[:, t, :], X[:, t, :], ss[:, 4 + t:5 + t], gf[:], ALU.mult,
                                         ALU.mult).then_inc(out_done, 1)

        @block.tensor
        def _(pe):
            n = Tally()

            def open_bank(b):
                last = n.at(f"fill{b}")
                n.step(f"fill{b}")
                if not (isinstance(last, int) and last == 0):
                    pe.wait_ge(free[b], last)

            def drained(*banks):
                for b in banks:
                    pe.wait_ge(free[b], n.at(f"fill{b}"))

            def unit():
                s = n.count.get("u", 0) % SPL
                n.count["u"] = n.count.get("u", 0) + 1
                pe.wait_ge(lo_done, n.step("unit"))
                return s

            def triple(o, lh, ll, rh, rl, start, stop):
                pe.matmul(o, lh, rh, start=start, stop=False)
                pe.matmul(o, lh, rl, start=False, stop=False)
                return pe.matmul(o, ll, rh, start=False, stop=stop)

            def transposes(gains_of_u):
                pe.wait_ge(u_done, gains_of_u)
                for j in range(4):
                    open_bank(j)
                    for c in range(2):
                        for t in range(TT):
                            k = 2 * j + c
                            last = pe.transpose(bank[j][:, c * TOK + t * P:c * TOK + (t + 1) * P],
                                                U[:, t, k * P:(k + 1) * P], ident[:])
                    last.then_inc(full[j], 1)

            def cols_block(banks, tiles, n_cols=BLK, units=2, ready=()):
                for b in banks:
                    open_bank(b)
                per = KC // units
                for h in range(units):
                    s = unit()
                    for t in range(tiles):
                        for k in range(per):
                            kk = h * per + k
                            wsl = slice(k * n_cols, (k + 1) * n_cols)
                            last = triple(bank[banks[t]][:, 0:n_cols], t_hi[:, kk, t * P:(t + 1) * P],
                                          t_lo[:, kk, t * P:(t + 1) * P], w_hi[:, s, wsl], w_lo[:, s, wsl],
                                          kk == 0, kk == KC - 1)
                    last.then_inc(unit_done, 1)

            pe.wait_ge(consts, 12)
            pe.wait_ge(small_in, 64)
            open_bank(4)
            pe.transpose(bank[4][:, 0:56], rows[:], ident[0:56, 0:56]).then_inc(full[4], 1)
            pe.wait_ge(row_in, 32)
            open_bank(7)
            pe.matmul(bank[7][:, 0:8], ones[0:1, :], gfr[0:1, D:D + 8], start=True, stop=True).then_inc(full[7], 1)

            transposes(2)
            drained(0, 1, 2, 3)
            for nb in range(4):
                cols_block([2 * nb, 2 * nb + 1], TT)
            cols_block([0, 1], TT, 256, 1)

            pe.wait_ge(roped, 2)
            for j in range(7):
                open_bank(j)
                for c in range(min(2, 13 - 2 * j)):
                    for t in range(TT):
                        hp = 2 * (2 * j + c)
                        last = pe.transpose(bank[j][:, c * TOK + t * P:c * TOK + (t + 1) * P],
                                            proj[:, t, hp:hp + 2, :].rearrange("p h d -> p (h d)"), ident[:])
                last.then_inc(full[j], 1)
            drained(*range(7))

            for s in range(AH + BH + 3):
                if s < AH + BH:
                    h = s
                    if h < AH:
                        qc, kc, half = h // 2, 4 + h // 2, h % 2
                    else:
                        qc, kc, half = 8 + (h - AH) % 4, 12, (h - AH) // 4
                    pr = slice(half * HD, (half + 1) * HD)
                    b = h % 3
                    open_bank(b)
                    pe.matmul(bank[b][:, 0:P], qkT[pr, qc, 0:P], qkT[pr, kc, 0:P], start=True, stop=True)
                    pe.matmul(bank[b][:, P:3 * P], qkT[pr, qc, P:TOK], qkT[pr, kc, :], start=True,
                              stop=True).then_inc(full[b], 1)
                if 0 <= s - 2 < AH + BH:
                    h = s - 2
                    b = 3 + h % 2
                    pe.wait_ge(p_ready, 2 * (h + 1))
                    open_bank(b)
                    for m in range(3):
                        src = (0, 1, 2)[m]
                        last = pe.transpose(bank[b][:, m * P:(m + 1) * P], sc[:, h % 3, src * P:(src + 1) * P],
                                            ident[:])
                    last.then_inc(full[b], 1)
                if 0 <= s - 3 < AH + BH:
                    h = s - 3
                    b = 5 + (h // 2) % 2
                    vh = 28 + h if h < AH else 26 + (h - AH) // 4
                    drained(3 + h % 2)
                    if h % 2 == 0:
                        open_bank(b)
                    o = bank[b][(h % 2) * HD:(h % 2 + 1) * HD, :]
                    pe.matmul(o[:, 0:TOK], proj[:, 0, vh, :], pT[:, h % 2, 0:TOK], start=True, stop=False)
                    pe.matmul(o[:, P:TOK], proj[:, 1, vh, :], pT[:, h % 2, TOK:3 * P], start=False,
                              stop=True).then_inc(pv_done, 1)
            drained(5, 6)

            for nb in range(2):
                cols_block([2 * nb, 2 * nb + 1], TT)

            def hidden_transposes(g, tiles):
                open_bank(TR + g % 2)
                per = 4 // tiles
                for c in range(per):
                    for t in range(tiles):
                        f0 = (g * per + c) * P
                        last = pe.transpose(bank[TR + g % 2][:, (c * tiles + t) * P:(c * tiles + t + 1) * P],
                                            H[:, t, f0:f0 + P], ident[:])
                last.then_inc(full[TR + g % 2], 1)

            def down_units(g, tiles, ybanks, groups):
                drained(TR + g % 2)
                per = 4 // tiles
                for u in range(per // 2):
                    s = unit()
                    for c in range(2):
                        cc = u * 2 + c
                        for t in range(tiles):
                            for m in range(2):
                                hs = slice((cc * tiles + t) * P, (cc * tiles + t + 1) * P)
                                ws = slice(c * D + m * BLK, c * D + (m + 1) * BLK)
                                fin = g == groups - 1 and cc == per - 1
                                last = triple(bank[ybanks[2 * t + m]][:], h_hi[:, g % 2, hs], h_lo[:, g % 2, hs],
                                              w_hi[:, s, ws], w_lo[:, s, ws], g == 0 and cc == 0, fin)
                    last.then_inc(unit_done, 1)

            transposes(4)
            drained(0, 1, 2, 3)
            for b in range(FB):
                cols_block([GATE, GATE + 1], TT)
                cols_block([UP, UP + 1], TT)
                if b == FB - 2:
                    for g in range(2):
                        hidden_transposes(g, TT)
            for b in (YB, YB + 1, GATE, GATE + 1):
                open_bank(b)
            for g in range(14):
                down_units(g, TT, (YB, YB + 1, GATE, GATE + 1), 14)
                if g + 2 < 14:
                    if g + 2 == 12:
                        drained(UP, UP + 1)
                    hidden_transposes(g + 2, TT)

            transposes(6)
            drained(0, 1, 2, 3)
            for first in (0, 4):
                for j in range(4):
                    open_bank(first + j)
                    s = unit()
                    for c in range(2):
                        for k in range(KC):
                            ws = slice(k * 256 + c * P, k * 256 + (c + 1) * P)
                            last = triple(bank[first + j][:, c * TOK:(c + 1) * TOK], w_hi[:, s, ws], w_lo[:, s, ws],
                                          t_hi[:, k, :], t_lo[:, k, :], k == 0, k == KC - 1)
                    last.then_inc(unit_done, 1)
            for first in (0, 4):
                for nb in range(2):
                    cols_block([first + 2 * nb, first + 2 * nb + 1], TT)
            fill = 0
            for idx in range(18):
                lev, hf = idx // 2, idx % 2
                if lev < 8:
                    pe.wait_ge(wl_done, 2 * (idx + 1))
                for m in range(1 if lev == 0 else 2):
                    b = fill % 8
                    fill += 1
                    open_bank(b)
                    for c in range(4):
                        if lev == 0:
                            src = wl[:, idx % 2, c * TOK:(c + 1) * TOK]
                            lhs, rhs = src[:, 0:P], src[:, P:TOK]
                        elif lev < 8:
                            lhs = rhs = wl[:, idx % 2, (m * 4 + c) * P:(m * 4 + c + 1) * P]
                        else:
                            at = hf * 1024 + (m * 4 + c) * P
                            lhs, rhs = kT[:, at:at + P], qT[:, at:at + P]
                        last = pe.matmul(bank[b][:, c * P:(c + 1) * P], lhs, rhs, start=True, stop=True)
                    last.then_inc(full[b], 1)
            drained(*range(8))
            for t in range(TT):
                for hf in range(2):
                    b = fill % 8
                    fill += 1
                    open_bank(b)
                    for c in range(4):
                        hd = 4 * hf + c
                        o = bank[b][:, c * P:(c + 1) * P]
                        vs = slice(hd * P, (hd + 1) * P)
                        if t == 1:
                            pe.matmul(o, aX[:, vs], V[:, 0, vs], start=True, stop=False)
                        last = pe.matmul(o, aT[:, hd * TOK + t * P:hd * TOK + (t + 1) * P], V[:, t, vs],
                                         start=t == 0, stop=True)
                    last.then_inc(full[b], 1)
            drained(2, 3, 4, 5)
            transposes(6)
            drained(0, 1, 2, 3)
            for nb in range(2):
                cols_block([2 * nb, 2 * nb + 1], TT)

            transposes(8)
            drained(0, 1, 2, 3)
            pe.wait_ge(wr_split, 1)
            open_bank(4)
            for t in range(TT):
                for k in range(KC):
                    o = bank[4][:, t * NE:(t + 1) * NE]
                    th, tl = t_hi[:, k, t * P:(t + 1) * P], t_lo[:, k, t * P:(t + 1) * P]
                    pe.matmul(o, th, wr_hi[:, k, :], start=k == 0, stop=False)
                    pe.matmul(o, th, wr_lo[:, k, :], start=False, stop=False)
                    pe.matmul(o, tl, wr_hi[:, k, :], start=False, stop=False)
                    last = pe.matmul(o, tl, wr_lo[:, k, :], start=False, stop=k == KC - 1)
            last.then_inc(full[4], 1)
            for m in range(2):
                open_bank(6 + m)
                pe.matmul(bank[6 + m][:], ones[0:1, :], gfr[0:1, m * BLK:(m + 1) * BLK], start=True,
                          stop=True).then_inc(full[6 + m], 1)
            open_bank(5)
            pe.wait_ge(mask_done, 1)
            m0, m1 = rt[:, 8, 0, :], rt[:, 8, 1, :]
            pe.matmul(bank[5][:, 0:8], tri[:], m0, start=True, stop=True)
            pe.matmul(bank[5][:, 8:16], tri[:], m1, start=True, stop=False)
            pe.matmul(bank[5][:, 8:16], ones[:], m0, start=False, stop=True)
            pe.matmul(bank[5][:, 16:24], ones[:], m0, start=True, stop=False)
            pe.matmul(bank[5][:, 16:24], ones[:], m1, start=False, stop=True).then_inc(full[5], 1)
            pe.wait_ge(rounds_in, 1)
            nr = pe.value_load(nrounds[0:1, 0:1], min_val=NE, max_val=2 * NE)

            def gather():
                pe.wait_ge(s_done, n.step("s", 2))
                for m, b in enumerate((GATE + 1, UP + 1)):
                    open_bank(b)
                    for c in range(4):
                        k = 4 * m + c
                        for t in range(TT):
                            last = pe.matmul(bank[b][:, c * P:(c + 1) * P], U[:, t, k * P:(k + 1) * P],
                                             S[:, t, :], start=t == 0, stop=t == TT - 1)
                    last.then_inc(full[b], 1)

            def scatter(t):
                for m in range(2):
                    open_bank(TR + m)
                    pe.matmul(bank[TR + m][:], GT[:, t * P:(t + 1) * P], Y[:, m * BLK:(m + 1) * BLK],
                              start=True, stop=True).then_inc(full[TR + m], 1)

            gather()
            for m in range(2):
                open_bank(YB + m)
                pe.matmul(bank[YB + m][:], GT[:, 0:P], U[:, 0, 0:BLK], start=True, stop=True).then_inc(full[YB + m], 1)
            with pe.Fori(0, nr) as i:
                n.enter(i, {k: c for k, c in dict(ROUND, s=2, g=2).items() if k[:4] != "full"})
                drained(GATE + 1, UP + 1)
                for b in range(FB):
                    cols_block([GATE + b % 2], 1)
                    cols_block([UP + b % 2], 1)
                    if b < 2:
                        if b == 0:
                            drained(YB, YB + 1)
                        scatter(b)
                    if b == 2:
                        pe.wait_ge(g_ready, n.step("g", 2))
                        open_bank(TR)
                        for t in range(TT):
                            last = pe.transpose(bank[TR][:, t * P:(t + 1) * P], G[:, t, :], ident[:])
                        last.then_inc(full[TR], 1)
                    if b == FB - 2:
                        for g in range(2):
                            hidden_transposes(g, 1)
                gather()
                open_bank(YB)
                open_bank(YB + 1)
                for g in range(7):
                    down_units(g, 1, (YB, YB + 1), 7)
                    if g + 2 < 7:
                        if g + 2 == 6:
                            drained(UP)
                        hidden_transposes(g + 2, 1)
                n.count["u"] = U0
                n.leave(nr)
            drained(YB, YB + 1)
            scatter(0)
            scatter(1)


_INS = ["x", "positions", "g_mix", "g_ffn", "g_final", "w_in_attn", "w_out_attn", "attn_sinks", "w_in_rec",
        "rec_lower_bounds", "rec_norm_g", "w_out_rec", "w_gate_dense", "w_up_dense", "w_down_dense",
        "w_router", "w_gate_moe", "w_up_moe", "w_down_moe"]


def kernel(**inputs):
    import numpy as _np
    import concourse.bacc as _bacc
    from concourse import mybir as _mybir
    from concourse.bass_utils import run_bass_kernel_spmd as _run

    nc = _bacc.Bacc("TRN2", target_bir_lowering=False, num_devices=1)
    arrays, args = {}, []
    for name in _INS:
        a = _np.ascontiguousarray(inputs[name])
        arrays[f"in_{name}_dram"] = a
        args.append(nc.dram_tensor(f"in_{name}_dram", a.shape, _mybir.dt.from_np(a.dtype), kind="ExternalInput").ap())
    shape = inputs["x"].shape
    out = nc.dram_tensor("out_0_dram", shape, _mybir.dt.float32, kind="ExternalOutput").ap()
    build(nc, *args, out)
    r = _run(nc, [arrays], core_ids=[0])
    return r.results[0]["out_0_dram"]
```

```python
from contextlib import ExitStack

import numpy as np

import concourse.bass as bass
from concourse import mybir

ALU = mybir.AluOpType
ACT = mybir.ActivationFunctionType
AX = mybir.AxisListType
F32 = mybir.dt.float32
F32R = mybir.dt.float32r
I32 = mybir.dt.int32
U32 = mybir.dt.uint32
U8 = mybir.dt.uint8

P = 128
TT = 2
TOK = P * TT
D = 1024
KC = D // P
EPS = 1e-6
HD = 64
AH, BH, KVH = 8, 8, 2
WIN_A, WIN_B = 128, 127
ROT = 16
THETA = 500000.0
CH = 8
FF = 3584
NE = 8
CAP = 128
UNIT = 2048
BLK = 512
RAW = 6
SPL = 3
FB = FF // BLK
FCH = FF // P
FFN_UNITS = 4 * FB + FCH // 2
LEAD = RAW + SPL
LEVELS = 7
BIG = 3.0e38
SCALE = HD ** -0.5

GATE, UP, TR, YB = 0, 2, 4, 6
TB = (4, 5, 2, 3)
OB = (0, 1, 6, 7)
SB, PB, VB = (0, 1), 2, (4, 5)
QKT = (0, 1, 2, 3, 6, 7, 3)
OUT_A = ((3, 6), (7, 0))
FILLER = {0: (6, 0), 1: (6, 1), 2: (7, 0), 3: (7, 1), 4: (8, 0), 5: (8, 1),
          12: (9, 0), 13: (9, 1), 14: (10, 0), 16: (10, 1)}
OUT_R = ((0, 1), (2, 3))
SPLIT_AT = {3: 10, 5: 11, 7: 12, 15: 13}


class Tally:

    def __init__(self):
        self.count, self.per, self.var = {}, {}, None

    def at(self, key, less=0):
        c = self.count.get(key, 0) - less
        p = self.per.get(key, 0)
        return c if self.var is None or not p else self.var * p + c

    def step(self, key, by=1):
        self.count[key] = self.count.get(key, 0) + by
        return self.at(key)

    def enter(self, var, per):
        self.var, self.per, self.start = var, per, dict(self.count)

    def leave(self, rounds):
        for k in set(self.count) | set(self.per):
            got = self.count.get(k, 0) - self.start.get(k, 0)
            assert got == self.per.get(k, 0), (k, got, self.per.get(k, 0))
        self.count, self.var = dict(self.start), rounds


def spread(ap, dim, n):
    shape = list(ap.shape)
    assert shape[dim] == 1
    shape[dim] = n
    return ap.broadcast_to(shape)


def col_blocks(w, c0, n):
    v = w.rearrange("(k p) f -> p k f", p=P)
    return [v[:, h * 4:h * 4 + 4, c0:c0 + n] for h in range(2)]


def build(nc, x, positions, g_mix, g_ffn, g_final, w_in_attn, w_out_attn, attn_sinks, w_in_rec,
          rec_lower_bounds, rec_norm_g, w_out_rec, w_gate_dense, w_up_dense, w_down_dense,
          w_router, w_gate_moe, w_up_moe, w_down_moe, out):
    ctx = ExitStack()
    with ctx:
        def sb(name, shape, dt=F32):
            return ctx.enter_context(nc.sbuf_tensor(name, shape, dt))

        def sem(name):
            return ctx.enter_context(nc.semaphore(name))

        raw = sb("raw", [P, RAW, UNIT])
        w_hi = sb("w_hi", [P, SPL, UNIT], F32R)
        w_lo = sb("w_lo", [P, SPL, UNIT], F32R)
        X = sb("X", [P, TT, D])
        U = sb("U", [P, TT, D])
        t_hi = sb("t_hi", [P, KC, TOK], F32R)
        t_lo = sb("t_lo", [P, KC, TOK], F32R)
        h_hi = sb("h_hi", [P, 2, BLK], F32R)
        h_lo = sb("h_lo", [P, 2, BLK], F32R)
        work = sb("work", [P, 15360])
        ident = sb("ident", [P, P])
        tri = sb("tri", [P, P])
        ones = sb("ones", [P, P])
        slots = sb("slots", [P, P])
        iota8 = sb("iota8", [P, 8])
        lev_mask = sb("lev_mask", [P, LEVELS, P], U8)
        col = sb("col", [P, 56])
        lbc = sb("lbc", [P, 8, 8])
        gfr = sb("gfr", [1, D + 8])
        sk8 = sb("sk8", [P, 8])
        posi = sb("posi", [P, TT], I32)
        posf = sb("posf", [P, TT])
        rope = sb("rope", [P, 8, TT, 8])
        ss = sb("ss", [P, 5, 8])
        rs_row = sb("rs_row", [P, TOK])
        ss16 = sb("ss16", [P, 3, TT, CH])
        dg = sb("dg", [P, CH * TT])
        epsc = sb("epsc", [P, 3])
        wr = sb("wr", [P, KC, NE])
        wr_hi = sb("wr_hi", [P, KC, NE], F32R)
        wr_lo = sb("wr_lo", [P, KC, NE], F32R)
        att = sb("att", [P, 3, 16])
        rt = sb("rt", [P, 12, TT, 8])
        rti = sb("rti", [P, TT, 8], U32)
        cols = sb("cols", [P, TT, 2 * NE + 1])
        gates = sb("gates", [P, TT, 2 * NE + 1])
        cur = sb("cur", [P, 4])
        cnt = sb("cnt", [P, 2])
        nrounds = sb("nrounds", [P, 1], I32)

        bank = [ctx.enter_context(nc.psum_tensor(f"bank{i}", [P, BLK], F32)) for i in range(8)]

        def w_at(a, n):
            return work[:, a:a + n]

        NH = 2 * AH + BH + 2 * KVH + AH
        proj = w_at(0, TT * NH * HD).rearrange("p (t h d) -> p t h d", t=TT, h=NH)
        qkT = w_at(4608, 13 * TOK).rearrange("p (c n) -> p c n", c=13)
        sc = w_at(7936, 3 * 384).rearrange("p (s n) -> p s n", s=3)
        pT = w_at(9088, 2 * 384).rearrange("p (s n) -> p s n", s=2)
        rp = w_at(9856, 4 * TT * 26 * 8).rearrange("p (s t h d) -> p s t h d", s=4, t=TT, h=26)
        mi = w_at(4608, 3 * 384).bitcast(I32).rearrange("p (s n) -> p s n", s=3)
        mf = w_at(4608 + 1152, 5 * 384).rearrange("p (s n) -> p s n", s=5)
        biasA = w_at(14592, 384)
        biasB = w_at(14976, 384)
        rows = work[0:56, 14400:14400 + P]
        qT = w_at(0, 2048)
        kT = w_at(2048, 2048)
        fT = w_at(4096, 2048)
        aT = w_at(8192, 2048)
        aX = w_at(10240, 1024)
        V = w_at(11264, 2048).rearrange("p (t n) -> p t n", t=TT)
        sq = w_at(0, 2048).rearrange("p (s n) -> p s n", s=4)
        tot = [fT] + [w_at(6144 + 2048 - (4096 >> i), 2048 >> i) for i in range(1, LEVELS)]
        xr, xr2 = w_at(13312, P), w_at(13440, P)
        H = w_at(0, TT * FF).rearrange("p (t f) -> p t f", t=TT)
        Y = w_at(7168, D)
        G = w_at(8192, TOK).rearrange("p (t c) -> p t c", t=TT)
        GT = w_at(8448, TOK)
        S = w_at(8704, TOK).rearrange("p (t c) -> p t c", t=TT)
        gf = w_at(9216, D)
        outb = w_at(0, TT * D).rearrange("p (t n) -> p t n", t=TT)

        def outputs_at(t_part, h_part, j):
            return t_part[:, j, :] if j >= AH // 2 else h_part[:, j // 2, j % 2 * TOK:(j % 2 + 1) * TOK]

        def proj_place(nb, t, src):
            first = (0, AH, 28, 2 * AH, 2 * AH + BH)[nb]
            if nb == 3:
                return (proj[:, t, first:first + 8, :].rearrange("p (j a) d -> p a j d", a=2),
                        src[:].rearrange("p (a j d) -> p a j d", a=2, j=4))
            h = 4 if nb == 4 else 8
            return proj[:, t, first:first + h, :], src[:, 0:h * HD].rearrange("p (h d) -> p h d", h=h)

        x_in, small_in, pos_in = sem("x_in"), sem("small_in"), sem("pos_in")
        row_in, wr_in = sem("row_in"), sem("wr_in")
        loaded = [sem(f"loaded{i}") for i in range(RAW)]
        hi_done, lo_done = sem("hi_done"), sem("lo_done")
        unit_done = sem("unit_done")
        full = [sem(f"full{i}") for i in range(8)]
        free = [sem(f"free{i}") for i in range(8)]
        pool_seq, act_seq, dve_seq = sem("pool_seq"), sem("act_seq"), sem("dve_seq")
        consts = sem("consts")
        sq_done = sem("sq_done")
        rs_done = sem("rs_done")
        u_done = sem("u_done")
        sg_done = sem("sg_done")
        row_done = sem("row_done")
        th_done = sem("th_done")
        rope_r, rope_s = sem("rope_r"), sem("rope_s")
        rope_m = sem("rope_m")
        lb_e = sem("lb_e")
        lb_d = sem("lb_d")
        roped = sem("roped")
        mx_ready, ex_ready = sem("mx_ready"), sem("ex_ready")
        p_ready, pv_done, oh_done = sem("p_ready"), sem("pv_done"), sem("oh_done")
        fg_done = sem("fg_done")
        qk_done = sem("qk_done")
        tot_done = sem("tot_done")
        qp_done = sem("qp_done")
        lev_done = sem("lev_done")
        kr_done = sem("kr_done")
        osq_done, oss_done, ostd_done = sem("osq_done"), sem("oss_done"), sem("ostd_done")
        hh_done = sem("hh_done")
        wr_hi_d, wr_split = sem("wr_hi_d"), sem("wr_split")
        rt_d, rt_e = sem("rt_d"), sem("rt_e")
        mask_done, rounds_in = sem("mask_done"), sem("rounds_in")
        s_done, g_ready = sem("s_done"), sem("g_ready")
        out_done, stored = sem("out_done"), sem("stored")

        wa = w_in_attn[0]
        wrr = w_in_rec[0]
        stream = []
        for nb in range(4):
            stream += col_blocks(wa, nb * BLK, BLK)
        stream += [wa.rearrange("(k p) f -> p k f", p=P)[:, :, 4 * BLK:4 * BLK + 256]]
        out_a = [col_blocks(w_out_attn[0], nb * BLK, BLK) for nb in range(2)]
        stream += [out_a[nb][h] for h in range(2) for nb in range(2)]
        for b in range(FB):
            stream += col_blocks(w_gate_dense[0], b * BLK, BLK) + col_blocks(w_up_dense[0], b * BLK, BLK)
        down = w_down_dense[0].rearrange("(u k p) n -> p u k n", p=P, k=2)
        stream += [down[:, u] for u in range(FCH // 2)]
        narrow = wrr.rearrange("(k p) f -> p k f", p=P)
        for first in (D, 0):
            stream += [narrow[:, :, first + 256 * j:first + 256 * j + 256] for j in range(4)]
        for first in (2 * D, 3 * D):
            for nb in range(2):
                stream += col_blocks(wrr, first + nb * BLK, BLK)
        for nb in range(2):
            stream += col_blocks(w_out_rec[0], nb * BLK, BLK)
        U0 = len(stream)
        assert FFN_UNITS % RAW == 0 and FFN_UNITS % SPL == 0

        FILLS = {GATE: 4, GATE + 1: 3 + 1, UP: 4, UP + 1: 3 + 1, TR: 2 + 1 + 4, TR + 1: 2 + 3, YB: 1, YB + 1: 1}
        FULLS = {GATE + 1: 1, UP + 1: 1, TR: 7, TR + 1: 5}
        ROUND = dict([(f"fill{b}", c) for b, c in FILLS.items()] + [(f"full{b}", c) for b, c in FULLS.items()],
                     unit=FFN_UNITS)

        def level_bank(i, hf):
            return 4 + (1 + 2 * i + hf) % 4

        block = ctx.enter_context(nc.Block())

        @block.sync
        def _(sp):
            n = Tally()
            xv = x[0].rearrange("(t p) d -> p t d", p=P)
            for t in range(TT):
                sp.dma_start(X[:, t, :], xv[:, t, :]).then_inc(x_in, 16)

            def load(src, k):
                seen = n.step("unit")
                if k >= RAW:
                    sp.wait_ge(lo_done, n.at("unit", RAW))
                shape = src.shape
                dst = raw[:, k % RAW, :]
                if len(shape) == 4:
                    dst = dst.rearrange("p (e k n) -> p e k n", e=1, k=shape[2])
                else:
                    dst = dst.rearrange("p (k n) -> p k n", k=shape[1])
                sp.dma_start(dst, src).then_inc(loaded[k % RAW], 16)

            for k, src in enumerate(stream):
                load(src, k)

            gv = w_gate_moe[0].rearrange("e (k p) f -> p e k f", p=P)
            uv = w_up_moe[0].rearrange("e (k p) f -> p e k f", p=P)
            dv = w_down_moe[0].rearrange("e (u k p) n -> p e u k n", p=P, k=2)

            def expert_unit(u, e):
                if u >= 4 * FB:
                    return dv[:, bass.ds(e, 1), u - 4 * FB]
                b, h = u // 4, u % 2
                return (gv, uv)[u % 4 // 2][:, bass.ds(e, 1), 4 * h:4 * h + 4, b * BLK:(b + 1) * BLK]

            for u in range(LEAD):
                load(expert_unit(u, 0), U0 + u)
            sp.wait_ge(rounds_in, 1)
            nr = sp.value_load(nrounds[0:1, 0:1], min_val=NE, max_val=2 * NE)
            with sp.Fori(0, nr) as i:
                n.enter(i, {"unit": FFN_UNITS})
                for u in range(LEAD, FFN_UNITS + LEAD):
                    e = (i + 1) % NE if u >= FFN_UNITS else i % NE if u < 4 * FB else (i + NE) % NE
                    load(expert_unit(u % FFN_UNITS, e), U0 + u)
                n.leave(nr)
            for r in range(RAW):
                sp.wait_ge(loaded[r], nr * (16 * FFN_UNITS // RAW) + 16 * len(range(r, U0 + LEAD, RAW)))

            ov = out[0].rearrange("(t p) d -> p t d", p=P)
            for t in range(TT):
                sp.wait_ge(out_done, t + 1)
                sp.dma_start(ov[:, t, :], outb[:, t, :]).then_inc(stored, 16)
            sp.wait_ge(stored, 16 * TT)

        @block.gpsimd
        def _(pool):
            pool.memset(ident[:], 0.0).then_inc(pool_seq, 1)
            pool.memset(tri[:], 1.0).then_inc(pool_seq, 1)
            pool.memset(ones[:], 1.0).then_inc(consts, 1)
            pool.memset(epsc[:, 0:1], EPS).then_inc(consts, 1)
            pool.memset(epsc[:, 1:2], float(np.pi / 2)).then_inc(consts, 1)
            pool.wait_ge(pool_seq, 2)
            pool.affine_select(out=ident[:], in_=ident[:], compare_op=ALU.not_equal, fill=1.0, base=0,
                               pattern=[[-1, P]], channel_multiplier=1).then_inc(consts, 1)
            pool.affine_select(out=tri[:], in_=tri[:], compare_op=ALU.is_gt, fill=0.0, base=0,
                               pattern=[[1, P]], channel_multiplier=-1).then_inc(consts, 1)
            pool.iota(slots[:], pattern=[[1, P]], base=0, channel_multiplier=0,
                      allow_small_or_imprecise_dtypes=True).then_inc(consts, 1)
            pool.iota(iota8[:], pattern=[[1, 8]], base=0, channel_multiplier=0,
                      allow_small_or_imprecise_dtypes=True).then_inc(consts, 1)
            pool.iota(mi[:, 0, 0:P], pattern=[[-1, P]], base=0, channel_multiplier=1).then_inc(consts, 1)
            pool.iota(mi[:, 0, P:3 * P], pattern=[[-1, TOK]], base=P, channel_multiplier=1).then_inc(consts, 1)
            pool.iota(mi[:, 1, 0:P], pattern=[[0, P]], base=0, channel_multiplier=1).then_inc(consts, 1)
            pool.iota(mi[:, 1, P:2 * P], pattern=[[1, P]], base=0, channel_multiplier=0).then_inc(consts, 1)
            pool.iota(mi[:, 1, 2 * P:3 * P], pattern=[[1, P]], base=0, channel_multiplier=-1).then_inc(consts, 1)

            for hf in range(2):
                pool.wait_ge(fg_done, 4 * (hf + 1))
                for lev in range(1, LEVELS):
                    w = 1024 >> (lev - 1)
                    below = tot[lev - 1][:, hf * w:(hf + 1) * w].rearrange("p (n two) -> p n two", two=2)
                    if lev > 1:
                        pool.wait_ge(tot_done, hf * (LEVELS - 1) + lev - 1)
                    pool.tensor_tensor(tot[lev][:, hf * w // 2:(hf + 1) * w // 2], below[:, :, 0],
                                       below[:, :, 1], ALU.mult).then_inc(tot_done, 1)
            pool.wait_ge(tot_done, 2 * (LEVELS - 1))
            for lev in range(LEVELS):
                for hf in range(2):
                    half = 1 << lev
                    pool.wait_ge(lev_done, 2 * lev + hf + 1)
                    kv = kT[:, hf * 1024:(hf + 1) * 1024].rearrange("p (n two h) -> p n two h", two=2, h=half)
                    tv = tot[lev][:, hf * (1024 >> lev):(hf + 1) * (1024 >> lev)].rearrange(
                        "p (n two o) -> p n two o", two=2, o=1)
                    pool.tensor_tensor(kv[:, :, 0, :], kv[:, :, 0, :], spread(tv[:, :, 1, :], 2, half),
                                       ALU.mult).then_inc(kr_done, 1)

        @block.scalar
        def _(act):
            n = Tally()

            def link(ins):
                ins.then_inc(act_seq, 1)
                act.wait_ge(act_seq, n.step("seq"))

            def wait_full(b):
                n.step(f"fill{b}")
                act.wait_ge(full[b], n.step(f"full{b}"))

            def wait_units(k, *banks):
                saw_product(*banks)
                act.wait_ge(unit_done, unit_at(k))

            def unit_at(k):
                return k if n.var is None else n.var * FFN_UNITS + k

            def saw_product(*banks):
                for b in banks:
                    n.step(f"fill{b}")

            def drained(*banks):
                for b in banks:
                    act.wait_ge(free[b], n.at(f"fill{b}"))

            def saw(*banks):
                for b in banks:
                    n.step(f"fill{b}")
                    n.step(f"full{b}")

            def split_to(k):
                while n.count.get("u", 0) < k:
                    u = n.count["u"] = n.count.get("u", 0) + 1
                    n.step("unit")
                    r = (u - 1) % RAW
                    act.wait_ge(loaded[r], n.step(f"loaded{r}", 16))
                    if u > SPL:
                        act.wait_ge(unit_done, n.at("unit", SPL))
                    act.activation(w_hi[:, (u - 1) % SPL, :], raw[:, r, :], ACT.Copy).then_inc(hi_done, 1)

            act.dma_start(rows[0:16, :], g_mix.rearrange("l (k p) -> (l k) p", p=P)).then_inc(small_in, 16)
            act.dma_start(rows[16:32, :], g_ffn.rearrange("l (k p) -> (l k) p", p=P)).then_inc(small_in, 16)
            act.dma_start(rows[32:40, :], rec_norm_g.rearrange("l (k p) -> (l k) p", p=P)).then_inc(small_in, 16)
            act.dma_start(rows[40:56, :], rec_lower_bounds.rearrange("l (k p) -> (l k) p", p=P)).then_inc(small_in, 16)
            act.dma_start(gfr[0:1, 0:D], g_final.rearrange("(a n) -> a n", a=1)).then_inc(row_in, 16)
            act.dma_start(gfr[0:1, D:D + 8], attn_sinks).then_inc(row_in, 16)
            for t in range(TT):
                act.dma_start(posi[:, t:t + 1],
                              positions[0, t * P:(t + 1) * P].rearrange("(p o) -> p o", o=1)).then_inc(pos_in, 16)
            act.dma_start(wr[:], w_router[0].rearrange("(k p) e -> p k e", p=P)).then_inc(wr_in, 16)

            def rms(k):
                for t in range(TT):
                    link(act.activation(U[:, t, :], X[:, t, :], ACT.Square, accum_out=ss[:, k, t:t + 1]))
                act.activation(ss[:, k, 2:4], ss[:, k, 0:2], ACT.Sqrt, scale=1.0 / D,
                               bias=epsc[:, 0:1]).then_inc(sq_done, 1)

            def t_hi_part(gain):
                for j in range(4):
                    wait_full(TB[j])
                    for c in range(2):
                        k = 2 * j + c
                        act.activation(t_hi[:, k, :], bank[TB[j]][:, c * TOK:(c + 1) * TOK], ACT.Copy,
                                       scale=col[:, gain + k:gain + k + 1]).then_inc(th_done, 1)

            saw(4, 7)
            act.wait_ge(free[4], 1)
            t_hi_part(0)
            split_to(SPL)
            act.wait_ge(x_in, 16 * TT)
            rms(0)
            act.wait_ge(lb_d, 1)
            act.activation(lbc[:, 1:3, :], lbc[:, 1:3, :], ACT.Exp).then_inc(lb_e, 1)
            act.wait_ge(rope_r, 1)
            act.activation(rope[:, 5, :, :], rope[:, 3, :, :], ACT.Sin).then_inc(rope_s, 1)
            act.activation(rope[:, 6, :, :], rope[:, 4, :, :], ACT.Sin, scale=-1.0,
                           bias=epsc[:, 1:2]).then_inc(rope_s, 1)
            act.wait_ge(wr_in, 16)
            act.activation(wr_hi[:], wr[:], ACT.Copy).then_inc(wr_hi_d, 1)

            def place(nb, b):
                to, src = proj_place(nb, 0, bank[b])
                act.activation(to, src, ACT.Copy, scale=ss[:, 0, 4:5]).then_inc(free[b], 1)

            def qk_copy(j):
                c = min(2, 13 - 2 * j)
                act.activation(qkT[:, 2 * j:2 * j + c, :],
                               bank[QKT[j]][:, 0:c * TOK].rearrange("p (c n) -> p c n", c=c),
                               ACT.Copy).then_inc(free[QKT[j]], 1)

            for nb in range(2):
                split_to(2 * nb + 2 + SPL)
                saw_product(2 * nb + 1)
                wait_units(2 * nb + 2, 2 * nb)
                if nb == 0:
                    act.wait_ge(rs_done, 1)
                place(nb, 2 * nb)
            split_to(5 + SPL)
            for j in range(4):
                wait_full(QKT[j])
                if j % 2 == 0:
                    qk_copy(j)
            split_to(6 + SPL)
            saw_product(5)
            wait_units(6, 4)
            place(2, 4)

            for s in range(AH + BH + 3):
                if s == AH:
                    for j in range(4, 7):
                        wait_full(QKT[j])
                        if j % 2 == 0:
                            qk_copy(j)
                if s - 3 >= 0 and (s - 3) % 2 == 1:
                    j = (s - 3) // 2
                    saw_product(VB[j % 2])
                    act.wait_ge(pv_done, 2 * j + 2)
                    act.activation(outputs_at(t_hi, h_hi, j), bank[VB[j % 2]][:, 0:TOK], ACT.Copy).then_inc(oh_done, 1)
                if s < AH + BH:
                    k, g = s % 3, s >= AH
                    saw(SB[s % 2])
                    act.wait_ge(mx_ready, s + 1)
                    act.activation(sc[:, k, 0:P], sc[:, k, 0:P], ACT.Exp, scale=SCALE,
                                   bias=att[:, k, 2:3], accum_out=att[:, k, 4:5]).then_inc(ex_ready, 1)
                    act.activation(sc[:, k, P:3 * P], sc[:, k, P:3 * P], ACT.Exp, scale=SCALE,
                                   bias=att[:, k, 3:4], accum_out=att[:, k, 5:6]).then_inc(ex_ready, 1)
                    if g:
                        act.activation(att[:, k, 8:10], att[:, k, 10:12], ACT.Exp,
                                       scale=SCALE).then_inc(ex_ready, 1)
                if 0 <= s - 2 < AH + BH:
                    h = s - 2
                    wait_full(PB)
                    if h >= 2:
                        act.wait_ge(pv_done, h - 1)
                    act.activation(pT[:, h % 2, :], bank[PB][:, 0:3 * P], ACT.Copy).then_inc(free[PB], 1)
                if s == 4:
                    saw_product(7)
                    wait_units(8, 6)
                    place(3, 6)
                if s == 6:
                    wait_units(9, 3)
                    for t in range(TT):
                        to, src = proj_place(4, t, bank[3][:, t * 256:(t + 1) * 256])
                        ins = act.activation(to, src, ACT.Copy, scale=ss[:, 0, 4 + t:5 + t])
                    ins.then_inc(free[3], 1)
                if s in SPLIT_AT:
                    split_to(SPLIT_AT[s])

            def out_proj(base, banks):
                split_to(base + 4)
                saw_product(*banks[0], *banks[1])

            def next_stage(k, gain, base, x_banks):
                split_to(base + 2)
                t_hi_part(gain)
                split_to(base + SPL)
                drained(*x_banks)
                rms(k)
                act.wait_ge(rs_done, k + 1)

            out_proj(9, OUT_A)
            next_stage(1, 16, 13, OUT_A[0] + OUT_A[1])

            def ffn_dense(base):
                for b in range(FB):
                    split_to(base + 4 * b + 5)
                    wait_units(base + 4 * b + 2, GATE, GATE + 1)
                    for t in range(TT):
                        act.activation(H[:, t, b * BLK:(b + 1) * BLK], bank[GATE + t][:], ACT.Silu,
                                       scale=ss[:, 1, 4 + t:5 + t]).then_inc(free[GATE + t], 1)
                    saw_product(UP, UP + 1)
                    if b == FB - 1:
                        for g in range(2):
                            hidden_hi(g)
                for g in range(2, 14):
                    split_to(base + 28 + g - 2 + 1 + SPL)
                    hidden_hi(g)
                split_to(base + FFN_UNITS)
                saw_product(GATE, GATE + 1, YB, YB + 1)

            def hidden_hi(g):
                wait_full(TR + g % 2)
                act.activation(h_hi[:, g % 2, :], bank[TR + g % 2][:], ACT.Copy).then_inc(hh_done, 1)

            ffn_dense(13)
            next_stage(2, 8, 55, (YB, YB + 1, GATE, GATE + 1))

            saw(7)
            for j in range(4):
                split_to(55 + j + 1 + SPL)
                saw_product(j)
                drained(j)
                act.activation(fT[:, j * BLK:(j + 1) * BLK], fT[:, j * BLK:(j + 1) * BLK],
                               ACT.Sigmoid).then_inc(sg_done, 1)
            for j in range(4):
                split_to(59 + j + 1 + SPL)
                saw_product(4 + j)
                drained(4 + j)
                act.activation(qT[:, j * BLK:(j + 1) * BLK], qT[:, j * BLK:(j + 1) * BLK],
                               ACT.Silu).then_inc(sg_done, 1)
            for nb in range(4):
                split_to(63 + 2 * nb + 2 + SPL)
                wait_units(63 + 2 * nb + 2, 2 * nb % 4, 2 * nb % 4 + 1)
                cs = slice(nb % 2 * BLK, (nb % 2 + 1) * BLK)
                for t in range(TT):
                    act.activation((V if nb < 2 else U)[:, t, cs], bank[2 * nb % 4 + t][:],
                                   ACT.Copy if nb < 2 else ACT.Silu,
                                   scale=ss[:, 2, 4 + t:5 + t]).then_inc(free[2 * nb % 4 + t], 1)
            saw(4)
            for i in range(LEVELS + 1):
                saw_product(level_bank(i, 0), level_bank(i, 1))
            def o_rms(f4):
                t, hf = f4 // 2, f4 % 2
                act.wait_ge(oss_done, f4 + 1)
                act.activation(ss16[:, 1, t, 4 * hf:4 * hf + 4], ss16[:, 0, t, 4 * hf:4 * hf + 4], ACT.Sqrt,
                               scale=1.0 / P, bias=epsc[:, 0:1]).then_inc(ostd_done, 1)

            act.activation(epsc[:, 2:3], epsc[:, 0:1], ACT.Sqrt)
            for f4, b in enumerate(OB):
                wait_full(b)
                act.activation(sq[:, f4, :], bank[b][:], ACT.Square).then_inc(osq_done, 1)
                if f4:
                    o_rms(f4 - 1)
            o_rms(3)
            t_hi_part(32)
            out_proj(71, OUT_R)
            next_stage(3, 24, U0, OUT_R[0] + OUT_R[1])

            saw(4, 5)
            act.wait_ge(rt_d, 1)
            act.activation(rt[:, 5, :, 0:1], rt[:, 4, :, 0:1], ACT.Exp).then_inc(rt_e, 1)

            def gather_hi():
                for m, b in enumerate((GATE + 1, UP + 1)):
                    wait_full(b)
                    for c in range(4):
                        k = 4 * m + c
                        act.activation(t_hi[:, k, 0:CAP], bank[b][:, c * P:(c + 1) * P], ACT.Copy,
                                       scale=col[:, 24 + k:25 + k]).then_inc(th_done, 1)

            def y_copy():
                for m in range(2):
                    act.activation(Y[:, m * BLK:(m + 1) * BLK], bank[YB + m][:], ACT.Copy).then_inc(free[YB + m], 1)

            for m in range(2):
                wait_full(6 + m)
                act.activation(gf[:, m * BLK:(m + 1) * BLK], bank[6 + m][:], ACT.Copy).then_inc(free[6 + m], 1)
            gather_hi()
            wait_full(YB)
            wait_full(YB + 1)
            nr = act.value_load(nrounds[0:1, 0:1], min_val=NE, max_val=2 * NE)
            with act.Fori(0, nr) as i:
                n.enter(i, dict(ROUND, **{f"loaded{r}": 16 * FFN_UNITS // RAW for r in range(RAW)}))
                wait_units(U0, YB, YB + 1)
                y_copy()
                for b in range(FB):
                    if b == 3:
                        split_to(U0 + 4 * b + 3)
                        wait_full(TR)
                        act.activation(GT[:], bank[TR][:, 0:TOK], ACT.Copy).then_inc(free[TR], 1)
                    split_to(U0 + 4 * b + 5)
                    wait_units(U0 + 4 * b + 2, GATE + b % 2)
                    act.activation(H[:, 0, b * BLK:(b + 1) * BLK], bank[GATE + b % 2][:],
                                   ACT.Silu).then_inc(free[GATE + b % 2], 1)
                    saw_product(UP + b % 2)
                    if b < 2:
                        saw(TR, TR + 1)
                for g in range(2):
                    hidden_hi(g)
                split_to(U0 + 28 + SPL)
                gather_hi()
                for g in range(2, 7):
                    split_to(U0 + 28 + 2 * (g - 2) + 2 + SPL)
                    hidden_hi(g)
                split_to(U0 + FFN_UNITS + SPL)
                n.count["u"] = U0 + SPL
                n.leave(nr)
            act.wait_ge(unit_done, nr * FFN_UNITS + U0)
            y_copy()
            saw(TR, TR + 1, TR, TR + 1)
            drained(TR, TR + 1)
            for t in range(TT):
                link(act.activation(U[:, t, :], X[:, t, :], ACT.Square, accum_out=ss[:, 4, t:t + 1]))
            act.activation(ss[:, 4, 2:4], ss[:, 4, 0:2], ACT.Sqrt, scale=1.0 / D,
                           bias=epsc[:, 0:1]).then_inc(sq_done, 1)

        @block.vector
        def _(dve):
            n = Tally()

            def link(ins):
                ins.then_inc(dve_seq, 1)
                dve.wait_ge(dve_seq, n.step("seq"))

            def wait_full(b):
                n.step(f"fill{b}")
                dve.wait_ge(full[b], n.step(f"full{b}"))

            def wait_units(k, *banks):
                saw_product(*banks)
                dve.wait_ge(unit_done, unit_at(k))

            def unit_at(k):
                return k if n.var is None else n.var * FFN_UNITS + k

            def saw_product(*banks):
                for b in banks:
                    n.step(f"fill{b}")

            def drained(*banks):
                for b in banks:
                    dve.wait_ge(free[b], n.at(f"fill{b}"))

            def saw(*banks):
                for b in banks:
                    n.step(f"fill{b}")
                    n.step(f"full{b}")

            def split_to(k):
                while n.count.get("u", 0) < k:
                    u = n.count["u"] = n.count.get("u", 0) + 1
                    dve.wait_ge(hi_done, n.step("unit"))
                    s, r = (u - 1) % SPL, (u - 1) % RAW
                    dve.tensor_tensor(w_lo[:, s, :], raw[:, r, :], w_hi[:, s, :].bitcast(F32),
                                      ALU.subtract).then_inc(lo_done, 1)

            def inverse_rms(k):
                dve.wait_ge(sq_done, k + 1)
                dve.reciprocal(ss[:, k, 4:6], ss[:, k, 2:4]).then_inc(rs_done, 1)
                dve.wait_ge(rs_done, k + 1)

            def t_lo_part(gain):
                for j in range(4):
                    wait_full(TB[j])
                    dve.wait_ge(th_done, n.step("th", 2))
                    for c in range(2):
                        k = 2 * j + c
                        ins = dve.scalar_tensor_tensor(
                            t_lo[:, k, :], bank[TB[j]][:, c * TOK:(c + 1) * TOK], col[:, gain + k:gain + k + 1],
                            t_hi[:, k, :].bitcast(F32), ALU.mult, ALU.subtract)
                        if c == 1:
                            ins.then_inc(free[TB[j]], 1)

            dve.wait_ge(consts, 12)
            dist = mi[:, 0, :]
            f = [mf[:, i, :] for i in range(5)]
            link(dve.tensor_copy(f[0], dist))
            link(dve.tensor_scalar(mi[:, 2, :], dist, 3, None, ALU.bitwise_and))
            link(dve.tensor_scalar(f[1], mi[:, 2, :], 0, None, ALU.is_equal))
            link(dve.tensor_scalar(mi[:, 2, :], dist, 15, None, ALU.bitwise_and))
            link(dve.tensor_scalar(f[2], mi[:, 2, :], 0, None, ALU.is_equal))
            link(dve.tensor_tensor(f[1], f[1], f[2], ALU.add))
            link(dve.tensor_scalar(f[2], f[0], float(WIN_A), None, ALU.is_le))
            link(dve.tensor_tensor(f[1], f[1], f[2], ALU.add))
            link(dve.tensor_scalar(f[2], f[0], 0.0, None, ALU.is_ge))
            link(dve.tensor_tensor(f[1], f[1], f[2], ALU.mult))
            saw(4, 7)
            dve.wait_ge(full[4], 1)
            dve.tensor_copy(col[:], bank[4][:, 0:56]).then_inc(free[4], 1)
            dve.wait_ge(free[4], 1)
            t_lo_part(0)
            split_to(SPL)
            inverse_rms(0)

            def bias_masks():
                link(dve.tensor_scalar(f[3], f[1], 0.0, -BIG, ALU.is_equal, ALU.mult))
                link(dve.tensor_scalar(f[4], f[1], 2.0, float(8 * np.log(2.0)), ALU.is_equal, ALU.mult))
                link(dve.tensor_tensor(f[3], f[3], f[4], ALU.add))
                link(dve.tensor_scalar(f[4], f[1], 3.0, float(8 * np.log(3.0)), ALU.is_equal, ALU.mult))
                link(dve.tensor_tensor(biasA[:], f[3], f[4], ALU.add))
                link(dve.tensor_scalar(f[4], f[0], float(WIN_B), None, ALU.is_le))
                link(dve.tensor_tensor(f[4], f[4], f[2], ALU.mult))
                link(dve.tensor_scalar(biasB[:], f[4], -1.0, BIG, ALU.add, ALU.mult))
                link(dve.tensor_tensor(mi[:, 2, 0:P], mi[:, 1, 0:P], mi[:, 1, P:2 * P], ALU.bitwise_xor))
                link(dve.tensor_copy(f[0][:, 0:P], mi[:, 2, 0:P]))
                link(dve.tensor_scalar(f[1][:, 0:P], mi[:, 1, 2 * P:3 * P], 0.0, 1e9, ALU.is_lt, ALU.mult))
                link(dve.tensor_tensor(xr[:], f[0][:, 0:P], f[1][:, 0:P], ALU.add))

            link(dve.tensor_tensor(lbc[:, 0, :], col[:, 40:48], col[:, 48:56], ALU.max))
            link(dve.tensor_tensor(lbc[:, 1, :], col[:, 40:48], lbc[:, 0, :], ALU.subtract))
            dve.tensor_tensor(lbc[:, 2, :], col[:, 48:56], lbc[:, 0, :], ALU.subtract).then_inc(lb_d, 1)
            dve.wait_ge(pos_in, 16 * TT)
            link(dve.tensor_copy(posf[:], posi[:]))
            inv = [float(np.float32(THETA) ** np.float32(-2.0 * j / ROT)) for j in range(ROT // 2)]
            for j in range(ROT // 2):
                dve.memset(rope[:, 0, 0, j:j + 1], inv[j]).then_inc(dve_seq, 1)
                n.step("seq")
            dve.wait_ge(dve_seq, n.at("seq"))
            ang = rope[:, 1]
            for t in range(TT):
                link(dve.tensor_scalar(ang[:, t, :], rope[:, 0, 0, :], posf[:, t:t + 1], None, ALU.mult))
            turn, red = rope[:, 2], rope[:, 3]
            magic = 1.5 * 2.0 ** 23
            c1 = 6.28125
            c2 = float(np.float32(round((2 * np.pi - c1) * 2 ** 20) / 2 ** 20))
            c3 = 2 * np.pi - c1 - c2
            link(dve.tensor_scalar(turn, ang, float(1 / (2 * np.pi)), magic, ALU.mult, ALU.add))
            link(dve.tensor_scalar(turn, turn, -magic, None, ALU.add))
            link(dve.scalar_tensor_tensor(red, turn, -c1, ang, ALU.mult, ALU.add))
            link(dve.scalar_tensor_tensor(red, turn, -c2, red, ALU.mult, ALU.add))
            link(dve.scalar_tensor_tensor(red, turn, -c3, red, ALU.mult, ALU.add))
            link(dve.tensor_scalar(red, red, 3.1415925, -3.1415925, ALU.min, ALU.max))
            dve.scalar_tensor_tensor(rope[:, 4], red, -1.0, red, ALU.mult, ALU.max).then_inc(rope_r, 1)
            dve.wait_ge(lb_e, 1)
            link(dve.tensor_tensor(lbc[:, 3, :], lbc[:, 1, :], lbc[:, 2, :], ALU.add))
            link(dve.reciprocal(lbc[:, 4, :], lbc[:, 3, :]))
            link(dve.tensor_tensor(lbc[:, 1, :], lbc[:, 1, :], lbc[:, 4, :], ALU.mult))
            link(dve.tensor_tensor(lbc[:, 2, :], lbc[:, 2, :], lbc[:, 4, :], ALU.mult))
            link(dve.tensor_tensor(lbc[:, 3, :], lbc[:, 1, :], lbc[:, 2, :], ALU.add))
            link(dve.tensor_tensor(lbc[:, 5, :], lbc[:, 3, :], lbc[:, 1, :], ALU.subtract))
            link(dve.tensor_scalar(lbc[:, 6, :], lbc[:, 5, :], -1.0, 1.0, ALU.mult, ALU.add))
            dve.wait_ge(wr_hi_d, 1)
            dve.tensor_tensor(wr_lo[:], wr[:], wr_hi[:].bitcast(F32), ALU.subtract).then_inc(wr_split, 1)

            def place(nb, b):
                to, src = proj_place(nb, 1, bank[b])
                dve.tensor_scalar(to, src, ss[:, 0, 5:6], None, ALU.mult).then_inc(free[b], 1)

            def rotate(h0, h1, steps):
                x1, x2 = proj[:, :, h0:h1, 0:8], proj[:, :, h0:h1, 8:16]
                sin = spread(rope[:, 5].rearrange("p t (o d) -> p t o d", o=1), 2, h1 - h0)
                cos = spread(rope[:, 6].rearrange("p t (o d) -> p t o d", o=1), 2, h1 - h0)
                r = [rp[:, i, :, h0:h1, :] for i in range(4)]
                dve.tensor_tensor(r[0], x1, cos, ALU.mult).then_inc(rope_m, 1)
                dve.tensor_tensor(r[1], x2, sin, ALU.mult).then_inc(rope_m, 1)
                dve.tensor_tensor(r[2], x2, cos, ALU.mult).then_inc(rope_m, 1)
                dve.tensor_tensor(r[3], x1, sin, ALU.mult).then_inc(rope_m, 1)
                dve.wait_ge(rope_m, steps + 4)
                dve.tensor_tensor(x1, r[0], r[1], ALU.subtract).then_inc(roped, 1)
                dve.tensor_tensor(x2, r[2], r[3], ALU.add).then_inc(roped, 1)

            def qk_copy(j):
                dve.tensor_copy(qkT[:, 2 * j:2 * j + 2, :],
                                bank[QKT[j]][:].rearrange("p (c n) -> p c n", c=2)).then_inc(free[QKT[j]], 1)

            for nb in range(2):
                split_to(2 * nb + 2 + SPL)
                saw_product(2 * nb)
                wait_units(2 * nb + 2, 2 * nb + 1)
                place(nb, 2 * nb + 1)
                if nb == 0:
                    bias_masks()
            dve.wait_ge(rope_s, 2)
            drained(0, 1, 2, 3)
            rotate(0, 2 * AH, 0)
            split_to(5 + SPL)
            for j in range(4):
                wait_full(QKT[j])
                if j % 2 == 1:
                    qk_copy(j)
            split_to(6 + SPL)
            saw_product(4)
            wait_units(6, 5)
            place(2, 5)
            dve.wait_ge(full[7], 1)
            dve.tensor_scalar(sk8[:], bank[7][:, 0:8], 1.0 / SCALE, None, ALU.mult).then_inc(free[7], 1)

            for s in range(AH + BH + 3):
                if s == AH:
                    for j in range(4, 7):
                        wait_full(QKT[j])
                        if j % 2 == 1:
                            qk_copy(j)
                if s < AH + BH:
                    k, g = s % 3, s >= AH
                    if s >= 3:
                        dve.wait_ge(full[PB], n.at(f"full{PB}"))
                    wait_full(SB[s % 2])
                    bias, b = biasB if g else biasA, SB[s % 2]
                    dve.tensor_tensor_reduce(out=sc[:, k, 0:P], in0=bank[b][:, 0:P], in1=bias[:, 0:P], scale=1.0,
                                             scalar=-BIG, op0=ALU.add, op1=ALU.max,
                                             accum_out=att[:, k, 0:1]).then_inc(dve_seq, 1)
                    dve.tensor_tensor_reduce(out=sc[:, k, P:3 * P], in0=bank[b][:, P:3 * P], in1=bias[:, P:3 * P],
                                             scale=1.0, scalar=-BIG, op0=ALU.add, op1=ALU.max,
                                             accum_out=att[:, k, 1:2]).then_inc(free[b], 1)
                    n.step("seq")
                    dve.wait_ge(dve_seq, n.at("seq"))
                    drained(b)
                    if g:
                        hb = s - AH
                        skc = spread(sk8[:, hb:hb + 1], 1, 2)
                        if s == AH:
                            dve.wait_ge(free[7], 1)
                        link(dve.tensor_tensor(att[:, k, 0:2], att[:, k, 0:2], skc, ALU.max))
                        link(dve.tensor_tensor(att[:, k, 10:12], skc, att[:, k, 0:2], ALU.subtract))
                    dve.tensor_scalar(att[:, k, 2:4], att[:, k, 0:2], -SCALE, None, ALU.mult).then_inc(mx_ready, 1)
                if 0 <= s - 1 < AH + BH:
                    h = s - 1
                    k, g = h % 3, h >= AH
                    dve.wait_ge(ex_ready, n.step("ex", 3 if g else 2))
                    if g:
                        link(dve.tensor_tensor(att[:, k, 4:6], att[:, k, 4:6], att[:, k, 8:10], ALU.add))
                    link(dve.reciprocal(att[:, k, 6:8], att[:, k, 4:6]))
                    dve.tensor_scalar(sc[:, k, 0:P], sc[:, k, 0:P], att[:, k, 6:7], None, ALU.mult).then_inc(p_ready, 1)
                    dve.tensor_scalar(sc[:, k, P:3 * P], sc[:, k, P:3 * P], att[:, k, 7:8], None,
                                      ALU.mult).then_inc(p_ready, 1)
                if 0 <= s - 2 < AH + BH:
                    saw(PB)
                if s - 3 >= 0 and (s - 3) % 2 == 1:
                    j = (s - 3) // 2
                    saw_product(VB[j % 2])
                    dve.wait_ge(oh_done, j + 1)
                    dve.tensor_tensor(outputs_at(t_lo, h_lo, j), bank[VB[j % 2]][:, 0:TOK],
                                      outputs_at(t_hi, h_hi, j).bitcast(F32), ALU.subtract).then_inc(free[VB[j % 2]], 1)
                if s == 4:
                    saw_product(6)
                    wait_units(8, 7)
                    place(3, 7)
                if s == 6:
                    saw_product(3)
                    drained(3, 6, 7)
                    rotate(2 * AH, 2 * AH + BH + KVH, 4)
                if s - 1 in SPLIT_AT:
                    split_to(SPLIT_AT[s - 1])

            def out_proj(base, banks, last):
                split_to(base + 4)
                for nb in range(2):
                    wait_units(base + last[nb] + 1, *banks[nb])
                    for t in range(TT):
                        add_to_x(t, nb, banks[nb][t])
                    if nb == 0:
                        split_to(base + 4 + 2)

            def add_to_x(t, nb, b):
                xb = X[:, t, nb * BLK:(nb + 1) * BLK]
                dve.tensor_tensor(xb, xb, bank[b][:], ALU.add).then_inc(free[b], 1)

            def hidden_lo(g):
                wait_full(TR + g % 2)
                dve.wait_ge(hh_done, n.step("hh"))
                dve.tensor_tensor(h_lo[:, g % 2, :], bank[TR + g % 2][:], h_hi[:, g % 2, :].bitcast(F32),
                                  ALU.subtract).then_inc(free[TR + g % 2], 1)

            out_proj(9, OUT_A, (2, 3))
            t_lo_part(16)
            split_to(13 + SPL)
            inverse_rms(1)

            def h_block(b, t, up_bank, gate_bank, rs=None):
                drained(gate_bank)
                hb = H[:, t, b * BLK:(b + 1) * BLK]
                if rs is None:
                    dve.tensor_tensor(hb, hb, bank[up_bank][:], ALU.mult).then_inc(free[up_bank], 1)
                else:
                    dve.scalar_tensor_tensor(hb, bank[up_bank][:], rs, hb, ALU.mult, ALU.mult).then_inc(free[up_bank], 1)

            base = 13
            for b in range(FB):
                if b == 1:
                    for lev in range(LEVELS):
                        link(dve.tensor_scalar(xr2[:], xr[:], float(1 << lev), None, ALU.is_ge))
                        link(dve.scalar_tensor_tensor(lev_mask[:, lev, :], xr[:], float(2 << lev), xr2[:], ALU.is_lt,
                                                      ALU.mult))
                if b == FB - 1:
                    split_to(base + 4 * b + 5)
                    for g in range(2):
                        hidden_lo(g)
                split_to(base + 4 * b + 7)
                saw_product(GATE, GATE + 1)
                wait_units(base + 4 * b + 4, UP, UP + 1)
                for t in range(TT):
                    h_block(b, t, UP + t, GATE + t, ss[:, 1, 4 + t:5 + t])
            for g in range(2, 14):
                split_to(base + 28 + g - 2 + 1 + SPL)
                hidden_lo(g)
            split_to(base + FFN_UNITS + 2)
            ybank = (YB, YB + 1, GATE, GATE + 1)
            wait_units(base + FFN_UNITS, *ybank)
            for nb in range(2):
                for t in range(TT):
                    add_to_x(t, nb, ybank[2 * t + nb])
            t_lo_part(8)
            split_to(55 + SPL)
            inverse_rms(2)
            for t in range(TT):
                dve.tensor_scalar(rs_row[:, t * P:(t + 1) * P], ident[:], ss[:, 2, 4 + t:5 + t], None,
                                  ALU.mult).then_inc(row_done, 1)
            wait_full(7)
            dve.tensor_copy(rs_row[:], bank[7][:, 0:TOK]).then_inc(free[7], 1)
            drained(7)

            def scale_rows(to, base, j, b):
                wait_units(base + j + 1, b)
                dve.tensor_tensor(to[:, j * BLK:(j + 1) * BLK].rearrange("p (c n) -> p c n", c=2),
                                  bank[b][:].rearrange("p (c n) -> p c n", c=2),
                                  spread(rs_row[:].rearrange("p (c n) -> p c n", c=1), 1, 2),
                                  ALU.mult).then_inc(free[b], 1)

            for j in range(4):
                split_to(55 + j + 1 + SPL)
                scale_rows(fT, 55, j, j)
                dve.wait_ge(sg_done, j + 1)
                for c in range(2):
                    hd = 2 * j + c
                    fc = fT[:, hd * TOK:(hd + 1) * TOK]
                    link(dve.tensor_scalar(fc, fc, lbc[:, 6, hd:hd + 1], lbc[:, 5, hd:hd + 1], ALU.mult, ALU.add))
                    dve.tensor_scalar(kT[:, hd * TOK:(hd + 1) * TOK], fc, -1.0, 1.0, ALU.mult,
                                      ALU.add).then_inc(fg_done, 1)
            for j in range(4):
                split_to(59 + j + 1 + SPL)
                scale_rows(qT, 59, j, 4 + j)
                dve.wait_ge(sg_done, 4 + j + 1)
                js = slice(j * BLK, (j + 1) * BLK)
                dve.tensor_tensor(aT[:, js], qT[:, js], kT[:, js], ALU.mult).then_inc(qk_done, 1)
                dve.wait_ge(qk_done, j + 1)
                dve.wait_ge(fg_done, 2 * (j + 1))
                dve.tensor_tensor(qT[:, js], qT[:, js], fT[:, js], ALU.mult).then_inc(qp_done, 1)
            def own():
                wait_full(4)
                dve.tensor_copy(dg[:], bank[4][:, 0:CH * TT]).then_inc(free[4], 1)
                drained(4)
                link(dve.tensor_tensor(aT[:].rearrange("p (n c) -> p n c", c=P),
                                       spread(ident[:].rearrange("p (o c) -> p o c", o=1), 1, CH * TT),
                                       spread(dg[:].rearrange("p (n o) -> p n o", o=1), 2, P), ALU.mult))

            def level(i, hf):
                lb = level_bank(i, hf)
                saw_product(lb)
                dve.wait_ge(lev_done, 2 * i + hf + 1)
                if i == LEVELS:
                    dve.tensor_copy(aX[:, hf * BLK:(hf + 1) * BLK], bank[lb][:]).then_inc(free[lb], 1)
                    return
                half = 1 << i
                qv = qT[:, hf * 1024:(hf + 1) * 1024].rearrange("p (n two h) -> p n two h", two=2, h=half)
                tv = tot[i][:, hf * (1024 >> i):(hf + 1) * (1024 >> i)].rearrange(
                    "p (n two o) -> p n two o", two=2, o=1)
                dve.tensor_tensor(qv[:, :, 1, :], qv[:, :, 1, :], spread(tv[:, :, 0, :], 2, half),
                                  ALU.mult).then_inc(qp_done, 1)
                at = aT[:, hf * 1024:(hf + 1) * 1024].rearrange("p (a n two h) -> p a n two h", a=8, two=2, h=half)
                mk = lev_mask[:, i, :].rearrange("p (a n two h) -> p a n two h", a=1, two=2, h=half)
                pb = bank[lb][:].rearrange("p (a n h) -> p a n h", a=8, h=half)
                if i:
                    drained(level_bank(i - 1, hf))
                dve.copy_predicated(at[:, :, :, 1, :], spread(mk[:, :, :, 1, :], 1, 8), pb).then_inc(free[lb], 1)

            dve.wait_ge(tot_done, 2 * (LEVELS - 1))
            for u in range(8):
                if u == 7:
                    level(LEVELS - 1, 0)
                    level(LEVELS - 1, 1)
                split_to(63 + u + 1 + SPL)
                if u % 2:
                    saw_product(u // 2 % 2 * 2, u // 2 % 2 * 2 + 1)
                if u == 0:
                    own()
                else:
                    for hf in range(2):
                        level(u - 1 if u < 7 else LEVELS, hf)

            def o_sums(f4):
                t, hf = f4 // 2, f4 % 2
                saw(OB[f4])
                dve.wait_ge(osq_done, f4 + 1)
                dve.reduce_sum(ss16[:, 0, t, 4 * hf:4 * hf + 4],
                               sq[:, f4, :].rearrange("p (h v) -> p h v", h=4), AX.X).then_inc(oss_done, 1)

            def o_scaled(f4):
                t, hf = f4 // 2, f4 % 2
                dve.wait_ge(ostd_done, f4 + 1)
                hs = slice(4 * hf, 4 * hf + 4)
                link(dve.reciprocal(ss16[:, 2, t, hs], ss16[:, 1, t, hs]))
                for c in range(4):
                    hd = 4 * hf + c
                    uv = U[:, t, hd * P:(hd + 1) * P]
                    ins = dve.scalar_tensor_tensor(uv, bank[OB[f4]][:, c * P:(c + 1) * P], ss16[:, 2, t, hd:hd + 1],
                                                   uv, ALU.mult, ALU.mult)
                ins.then_inc(free[OB[f4]], 1)

            o_sums(0)
            for f4 in range(4):
                if f4 < 3:
                    o_sums(f4 + 1)
                o_scaled(f4)
            t_lo_part(32)
            out_proj(71, OUT_R, (1, 3))
            t_lo_part(24)
            split_to(U0 + SPL)
            inverse_rms(3)
            for t in range(TT):
                dve.tensor_scalar(U[:, t, :], X[:, t, :], ss[:, 3, 4 + t:5 + t], None, ALU.mult).then_inc(u_done, 1)

            R = [rt[:, i] for i in range(12)]
            wait_full(4)
            dve.tensor_copy(R[0], bank[4][:, 0:16].rearrange("p (t e) -> p t e", t=TT)).then_inc(free[4], 1)
            drained(4)
            for t in range(TT):
                link(dve.max(R[1][:, t, :], R[0][:, t, :]))
                link(dve.max_index(rti[:, t, :], R[1][:, t, :], R[0][:, t, :]))
            link(dve.tensor_copy(R[2], rti[:]))
            link(dve.tensor_tensor(R[4][:, :, 0:1], R[1][:, :, 1:2], R[1][:, :, 0:1], ALU.subtract))
            dve.tensor_tensor(R[4][:, :, 0:1], R[4][:, :, 0:1], ss[:, 3, 4:6].rearrange("p (t o) -> p t o", o=1),
                              ALU.mult).then_inc(rt_d, 1)
            for t in range(TT):
                link(dve.tensor_scalar(R[6][:, t, :], iota8[:], R[2][:, t, 0:1], None, ALU.is_equal))
                link(dve.tensor_scalar(R[7][:, t, :], iota8[:], R[2][:, t, 1:2], None, ALU.is_equal))
            dve.tensor_tensor(R[8], R[6], R[7], ALU.add).then_inc(mask_done, 1)
            dve.wait_ge(rt_e, 1)
            link(dve.tensor_scalar(R[4][:, :, 1:2], R[5][:, :, 0:1], 1.0, None, ALU.add))
            link(dve.reciprocal(R[4][:, :, 2:3], R[4][:, :, 1:2]))
            link(dve.tensor_tensor(R[4][:, :, 3:4], R[5][:, :, 0:1], R[4][:, :, 2:3], ALU.mult))
            for t in range(TT):
                link(dve.tensor_scalar(R[9][:, t, :], R[6][:, t, :], R[4][:, t, 2:3], None, ALU.mult))
                link(dve.scalar_tensor_tensor(gates[:, t, 0:NE], R[7][:, t, :], R[4][:, t, 3:4], R[9][:, t, :],
                                              ALU.mult, ALU.add))
            link(dve.tensor_copy(gates[:, :, NE:2 * NE], gates[:, :, 0:NE]))
            link(dve.memset(gates[:, :, 2 * NE:2 * NE + 1], 0.0))
            wait_full(5)
            pos = bank[5][:, 0:16].rearrange("p (t e) -> p t e", t=TT)
            link(dve.tensor_scalar(R[10], pos, 1.0, None, ALU.add))
            link(dve.tensor_tensor(R[10], R[10], R[8], ALU.mult))
            link(dve.tensor_scalar(cols[:, :, 0:NE], R[10], -1.0, None, ALU.add))
            link(dve.tensor_scalar(cols[:, :, NE:2 * NE], R[10], -1.0 - CAP, None, ALU.add))
            link(dve.memset(cols[:, :, 2 * NE:2 * NE + 1], -1.0))
            dve.reduce_max(cnt[:, 0:1], bank[5][:, 16:24], AX.X).then_inc(free[5], 1)
            drained(5)
            link(dve.tensor_scalar(cnt[:, 1:2], cnt[:, 0:1], float(CAP), float(NE), ALU.is_gt, ALU.mult))
            link(dve.tensor_scalar(nrounds[:], cnt[:, 1:2], float(NE), None, ALU.add))
            dve.memset(GT[:], 0.0).then_inc(rounds_in, 1)

            def round_slots(i):
                link(dve.tensor_copy(cur[:, 0:2].rearrange("p (t o) -> p t o", o=1), cols[:, :, bass.ds(i, 1)]))
                link(dve.tensor_copy(cur[:, 2:4].rearrange("p (t o) -> p t o", o=1), gates[:, :, bass.ds(i, 1)]))
                for t in range(TT):
                    dve.tensor_scalar(S[:, t, :], slots[:], cur[:, t:t + 1], None, ALU.is_equal).then_inc(s_done, 1)
                n.step("s", 2)

            def gather_lo():
                for m, b in enumerate((GATE + 1, UP + 1)):
                    wait_full(b)
                    dve.wait_ge(th_done, n.step("th", 4))
                    for c in range(4):
                        k = 4 * m + c
                        ins = dve.scalar_tensor_tensor(
                            t_lo[:, k, 0:CAP], bank[b][:, c * P:(c + 1) * P], col[:, 24 + k:25 + k],
                            t_hi[:, k, 0:CAP].bitcast(F32), ALU.mult, ALU.subtract)
                    ins.then_inc(free[b], 1)

            def scatter_add(t):
                for m in range(2):
                    wait_full(TR + m)
                    dve.tensor_tensor(X[:, t, m * BLK:(m + 1) * BLK], X[:, t, m * BLK:(m + 1) * BLK],
                                      bank[TR + m][:], ALU.add).then_inc(free[TR + m], 1)

            dve.wait_ge(rounds_in, 1)
            round_slots(0)
            gather_lo()
            saw(YB, YB + 1, YB, YB + 1)
            nr = dve.value_load(nrounds[0:1, 0:1], min_val=NE, max_val=2 * NE)
            with dve.Fori(0, nr) as i:
                n.enter(i, dict(ROUND, seq=2, s=2, th=8, hh=7))
                dve.wait_ge(s_done, n.at("s"))
                for t in range(TT):
                    dve.tensor_scalar(G[:, t, :], S[:, t, :], cur[:, 2 + t:3 + t], None, ALU.mult).then_inc(g_ready, 1)
                saw_product(YB, YB + 1)
                for b in range(FB):
                    if b == FB - 1:
                        split_to(U0 + 4 * b + 5)
                        for g in range(2):
                            hidden_lo(g)
                    split_to(U0 + 4 * b + 7)
                    saw_product(GATE + b % 2)
                    wait_units(U0 + 4 * b + 4, UP + b % 2)
                    h_block(b, 0, UP + b % 2, GATE + b % 2)
                    if b < 2:
                        scatter_add(b)
                    if b == 3:
                        saw(TR)
                        dve.wait_ge(full[TR], n.at(f"full{TR}"))
                        round_slots(i + 1)
                gather_lo()
                for g in range(2, 7):
                    split_to(U0 + 28 + 2 * (g - 2) + 2 + SPL)
                    hidden_lo(g)
                split_to(U0 + FFN_UNITS + SPL)
                n.count["u"] = U0 + SPL
                n.leave(nr)
            for t in range(TT):
                scatter_add(t)
            drained(TR, TR + 1)
            inverse_rms(4)
            for t in range(TT):
                dve.scalar_tensor_tensor(outb[:, t, :], X[:, t, :], ss[:, 4, 4 + t:5 + t], gf[:], ALU.mult,
                                         ALU.mult).then_inc(out_done, 1)

        @block.tensor
        def _(pe):
            n = Tally()

            def open_bank(b):
                last = n.at(f"fill{b}")
                n.step(f"fill{b}")
                if not (isinstance(last, int) and last == 0):
                    pe.wait_ge(free[b], last)

            def drained(*banks):
                for b in banks:
                    pe.wait_ge(free[b], n.at(f"fill{b}"))

            def unit():
                s = n.count.get("u", 0) % SPL
                n.count["u"] = n.count.get("u", 0) + 1
                pe.wait_ge(lo_done, n.step("unit"))
                return s

            def triple(o, lh, ll, rh, rl, start, stop):
                pe.matmul(o, lh, rh, start=start, stop=False)
                pe.matmul(o, lh, rl, start=False, stop=False)
                return pe.matmul(o, ll, rh, start=False, stop=stop)

            def transposes(rows_of, halves=((), ())):
                for j in range(4):
                    if j % 2 == 0:
                        drained(*halves[j // 2])
                    open_bank(TB[j])
                    for c in range(2):
                        for t in range(TT):
                            k = 2 * j + c
                            last = pe.transpose(bank[TB[j]][:, c * TOK + t * P:c * TOK + (t + 1) * P],
                                                rows_of[:, t, k * P:(k + 1) * P], ident[:])
                    last.then_inc(full[TB[j]], 1)

            def split_ready(h):
                drained(*TB[2 * h:2 * h + 2])

            def cols_block(banks, tiles, n_cols=BLK, units=2, fresh=False):
                for b in banks:
                    open_bank(b)
                for h in range(units):
                    if fresh:
                        split_ready(h)
                    col_unit(banks, tiles, h, units, n_cols)

            def col_unit(banks, tiles, h, units, n_cols=BLK):
                s = unit()
                for t in range(tiles):
                    last = col_half(banks, t, h, units, s, n_cols)
                last.then_inc(unit_done, 1)

            def col_half(banks, t, h, units, s, n_cols=BLK, mixed=False):
                per = KC // units
                for k in range(per):
                    kk = h * per + k
                    wsl = slice(k * n_cols, (k + 1) * n_cols)
                    a_hi, a_lo = t_hi[:, kk, :], t_lo[:, kk, :]
                    if mixed:
                        a_hi, a_lo = outputs_at(t_hi, h_hi, kk), outputs_at(t_lo, h_lo, kk)
                    last = triple(bank[banks[t]][:, 0:n_cols], a_hi[:, t * P:(t + 1) * P],
                                  a_lo[:, t * P:(t + 1) * P], w_hi[:, s, wsl], w_lo[:, s, wsl],
                                  kk == 0, kk == KC - 1)
                return last

            pe.wait_ge(consts, 12)
            pe.wait_ge(small_in, 64)
            open_bank(4)
            pe.transpose(bank[4][:, 0:56], rows[:], ident[0:56, 0:56]).then_inc(full[4], 1)
            pe.wait_ge(row_in, 32)
            open_bank(7)
            pe.matmul(bank[7][:, 0:8], ones[0:1, :], gfr[0:1, D:D + 8], start=True, stop=True).then_inc(full[7], 1)

            pe.wait_ge(x_in, 16 * TT)
            transposes(X)
            def qk_transposes(j):
                open_bank(QKT[j])
                for c in range(min(2, 13 - 2 * j)):
                    for t in range(TT):
                        hp = 2 * (2 * j + c)
                        last = pe.transpose(bank[QKT[j]][:, c * TOK + t * P:c * TOK + (t + 1) * P],
                                            proj[:, t, hp:hp + 2, :].rearrange("p h d -> p (h d)"), ident[:])
                last.then_inc(full[QKT[j]], 1)

            for nb in range(2):
                cols_block([2 * nb, 2 * nb + 1], TT, fresh=nb == 0)
            open_bank(4)
            open_bank(5)
            col_unit([4, 5], TT, 0, 2)
            pe.wait_ge(roped, 2)
            for j in range(4):
                qk_transposes(j)
            col_unit([4, 5], TT, 1, 2)

            def filler(s):
                u, t = FILLER[s]
                if t == 0:
                    slot[0] = unit()
                if u in (6, 7):
                    if u == 6:
                        open_bank(6 + t)
                    last = col_half([6, 7], t, u - 6, 2, slot[0])
                elif u == 8:
                    if t == 0:
                        open_bank(3)
                    for k in range(KC):
                        ws = slice(k * 256, (k + 1) * 256)
                        last = triple(bank[3][:, t * 256:(t + 1) * 256], t_hi[:, k, t * P:(t + 1) * P],
                                      t_lo[:, k, t * P:(t + 1) * P], w_hi[:, slot[0], ws], w_lo[:, slot[0], ws],
                                      k == 0, k == KC - 1)
                else:
                    if u == 9 and t == 0:
                        drained(*VB)
                    open_bank(OUT_A[u - 9][t])
                    last = col_half(OUT_A[u - 9], t, 0, 2, slot[0], mixed=True)
                if t == 1:
                    last.then_inc(unit_done, 1)

            def scores(h):
                if h < AH:
                    qc, kc, half = h // 2, 4 + h // 2, h % 2
                else:
                    qc, kc, half = 8 + (h - AH) % 4, 12, (h - AH) // 4
                if h == 0:
                    drained(*QKT[0:4])
                if h == AH:
                    drained(*QKT[4:7])
                pr = slice(half * HD, (half + 1) * HD)
                b = SB[h % 2]
                open_bank(b)
                pe.matmul(bank[b][:, 0:P], qkT[pr, qc, 0:P], qkT[pr, kc, 0:P], start=True, stop=True)
                pe.matmul(bank[b][:, P:3 * P], qkT[pr, qc, P:TOK], qkT[pr, kc, :], start=True,
                          stop=True).then_inc(full[b], 1)

            slot = [0]
            for s in range(AH + BH + 3):
                if s < AH + BH and s != AH:
                    scores(s)
                if 0 <= s - 3 < AH + BH:
                    h = s - 3
                    b = VB[(h // 2) % 2]
                    vh = 28 + h if h < AH else 26 + (h - AH) // 4
                    if h == 0:
                        drained(4, 5)
                    drained(PB)
                    if h % 2 == 0:
                        open_bank(b)
                    o = bank[b][(h % 2) * HD:(h % 2 + 1) * HD, :]
                    pe.matmul(o[:, 0:TOK], proj[:, 0, vh, :], pT[:, h % 2, 0:TOK], start=True, stop=False)
                    pe.matmul(o[:, P:TOK], proj[:, 1, vh, :], pT[:, h % 2, TOK:3 * P], start=False,
                              stop=True).then_inc(pv_done, 1)
                if 0 <= s - 2 < AH + BH:
                    h = s - 2
                    pe.wait_ge(p_ready, 2 * (h + 1))
                    open_bank(PB)
                    for m in range(3):
                        last = pe.transpose(bank[PB][:, m * P:(m + 1) * P], sc[:, h % 3, m * P:(m + 1) * P],
                                            ident[:])
                    last.then_inc(full[PB], 1)
                if s == AH:
                    scores(s)
                if s == AH - 1:
                    pe.wait_ge(roped, 4)
                    for j in range(4, 7):
                        qk_transposes(j)
                if s in FILLER:
                    filler(s)
            drained(*VB)
            for nb in range(2):
                col_unit(OUT_A[nb], TT, 1, 2)

            def hidden_transposes(g, tiles):
                open_bank(TR + g % 2)
                per = 4 // tiles
                for c in range(per):
                    for t in range(tiles):
                        f0 = (g * per + c) * P
                        last = pe.transpose(bank[TR + g % 2][:, (c * tiles + t) * P:(c * tiles + t + 1) * P],
                                            H[:, t, f0:f0 + P], ident[:])
                last.then_inc(full[TR + g % 2], 1)

            def down_units(g, tiles, ybanks, groups):
                drained(TR + g % 2)
                per = 4 // tiles
                for u in range(per // 2):
                    s = unit()
                    for c in range(2):
                        cc = u * 2 + c
                        for t in range(tiles):
                            for m in range(2):
                                hs = slice((cc * tiles + t) * P, (cc * tiles + t + 1) * P)
                                ws = slice(c * D + m * BLK, c * D + (m + 1) * BLK)
                                fin = g == groups - 1 and cc == per - 1
                                last = triple(bank[ybanks[2 * t + m]][:], h_hi[:, g % 2, hs], h_lo[:, g % 2, hs],
                                              w_hi[:, s, ws], w_lo[:, s, ws], g == 0 and cc == 0, fin)
                    last.then_inc(unit_done, 1)

            transposes(X, OUT_A)
            for b in range(FB):
                cols_block([GATE, GATE + 1], TT, fresh=b == 0)
                cols_block([UP, UP + 1], TT)
                if b == FB - 2:
                    for g in range(2):
                        hidden_transposes(g, TT)
            for b in (YB, YB + 1, GATE, GATE + 1):
                open_bank(b)
            for g in range(14):
                down_units(g, TT, (YB, YB + 1, GATE, GATE + 1), 14)
                if g + 2 < 14:
                    if g + 2 == 12:
                        drained(UP, UP + 1)
                    hidden_transposes(g + 2, TT)

            transposes(X, ((YB, GATE), (YB + 1, GATE + 1)))
            drained(*TB)
            for first in (0, 4):
                for j in range(4):
                    if first == 0 and j == 2:
                        pe.wait_ge(row_done, 2)
                        open_bank(7)
                        pe.matmul(bank[7][:, 0:TOK], ones[:], rs_row[:], start=True, stop=True).then_inc(full[7], 1)
                    open_bank(first + j)
                    s = unit()
                    for c in range(2):
                        for k in range(KC):
                            ws = slice(k * 256 + c * P, k * 256 + (c + 1) * P)
                            last = triple(bank[first + j][:, c * TOK:(c + 1) * TOK], w_hi[:, s, ws], w_lo[:, s, ws],
                                          t_hi[:, k, :], t_lo[:, k, :], k == 0, k == KC - 1)
                    last.then_inc(unit_done, 1)
            def level(i, hf):
                pe.wait_ge(qp_done, 4 + (2 * (i - 1) + hf + 1 if i else 0))
                if i:
                    pe.wait_ge(kr_done, 2 * (i - 1) + hf + 1)
                lb = level_bank(i, hf)
                open_bank(lb)
                if i == LEVELS:
                    for c in range(4):
                        at = (4 * hf + c) * TOK
                        last = pe.matmul(bank[lb][:, c * P:(c + 1) * P], kT[:, at:at + P], qT[:, at + P:at + TOK],
                                         start=True, stop=True)
                else:
                    half = 1 << i
                    for c in range(8):
                        at = hf * 1024 + c * P
                        qv = qT[:, at:at + P].rearrange("p (n two h) -> p n two h", two=2, h=half)
                        last = pe.matmul(bank[lb][:, c * P // 2:(c + 1) * P // 2].rearrange("p (n h) -> p n h", h=half),
                                         kT[:, at:at + P], qv[:, :, 1, :], start=True, stop=True)
                last.then_inc(lev_done, 1)

            def own_products():
                pe.wait_ge(qk_done, 4)
                open_bank(4)
                for c in range(CH * TT):
                    last = pe.matmul(bank[4][:, c:c + 1], aT[:, c * P:(c + 1) * P], ones[:, 0:1],
                                     start=True, stop=True)
                last.then_inc(full[4], 1)

            for nb in range(4):
                ba = 2 * nb % 4
                open_bank(ba)
                open_bank(ba + 1)
                for h in range(2):
                    u = 2 * nb + h
                    s = unit()
                    col_half([ba, ba + 1], 0, h, 2, s)
                    if u == 7:
                        level(LEVELS - 1, 0)
                        level(LEVELS - 1, 1)
                    col_half([ba, ba + 1], 1, h, 2, s).then_inc(unit_done, 1)
                    if u == 0:
                        own_products()
                    else:
                        for hf in range(2):
                            level(u - 1 if u < 7 else LEVELS, hf)
            for t in range(TT):
                drained(*(level_bank(LEVELS - 1 + t, hf) for hf in range(2)))
                for hf in range(2):
                    b = OB[2 * t + hf]
                    open_bank(b)
                    for c in range(4):
                        hd = 4 * hf + c
                        o = bank[b][:, c * P:(c + 1) * P]
                        vs = slice(hd * P, (hd + 1) * P)
                        if t == 1:
                            pe.matmul(o, aX[:, vs], V[:, 0, vs], start=True, stop=False)
                        last = pe.matmul(o, aT[:, hd * TOK + t * P:hd * TOK + (t + 1) * P], V[:, t, vs],
                                         start=t == 0, stop=True)
                    last.then_inc(full[b], 1)
            transposes(U, ((OB[0], OB[2]), (OB[1], OB[3])))
            for nb in range(2):
                cols_block([2 * nb, 2 * nb + 1], TT, fresh=nb == 0)

            transposes(X, OUT_R)
            drained(*TB)
            pe.wait_ge(wr_split, 1)
            open_bank(4)
            for t in range(TT):
                for k in range(KC):
                    o = bank[4][:, t * NE:(t + 1) * NE]
                    th, tl = t_hi[:, k, t * P:(t + 1) * P], t_lo[:, k, t * P:(t + 1) * P]
                    pe.matmul(o, th, wr_hi[:, k, :], start=k == 0, stop=False)
                    pe.matmul(o, th, wr_lo[:, k, :], start=False, stop=False)
                    pe.matmul(o, tl, wr_hi[:, k, :], start=False, stop=False)
                    last = pe.matmul(o, tl, wr_lo[:, k, :], start=False, stop=k == KC - 1)
            last.then_inc(full[4], 1)
            for m in range(2):
                open_bank(6 + m)
                pe.matmul(bank[6 + m][:], ones[0:1, :], gfr[0:1, m * BLK:(m + 1) * BLK], start=True,
                          stop=True).then_inc(full[6 + m], 1)
            open_bank(5)
            pe.wait_ge(mask_done, 1)
            m0, m1 = rt[:, 8, 0, :], rt[:, 8, 1, :]
            pe.matmul(bank[5][:, 0:8], tri[:], m0, start=True, stop=True)
            pe.matmul(bank[5][:, 8:16], tri[:], m1, start=True, stop=False)
            pe.matmul(bank[5][:, 8:16], ones[:], m0, start=False, stop=True)
            pe.matmul(bank[5][:, 16:24], ones[:], m0, start=True, stop=False)
            pe.matmul(bank[5][:, 16:24], ones[:], m1, start=False, stop=True).then_inc(full[5], 1)
            pe.wait_ge(rounds_in, 1)
            nr = pe.value_load(nrounds[0:1, 0:1], min_val=NE, max_val=2 * NE)

            def gather():
                pe.wait_ge(s_done, n.step("s", 2))
                if n.var is None:
                    pe.wait_ge(u_done, TT)
                for m, b in enumerate((GATE + 1, UP + 1)):
                    open_bank(b)
                    for c in range(4):
                        k = 4 * m + c
                        for t in range(TT):
                            last = pe.matmul(bank[b][:, c * P:(c + 1) * P], U[:, t, k * P:(k + 1) * P],
                                             S[:, t, :], start=t == 0, stop=t == TT - 1)
                    last.then_inc(full[b], 1)

            def scatter(t):
                for m in range(2):
                    open_bank(TR + m)
                    pe.matmul(bank[TR + m][:], GT[:, t * P:(t + 1) * P], Y[:, m * BLK:(m + 1) * BLK],
                              start=True, stop=True).then_inc(full[TR + m], 1)

            gather()
            for m in range(2):
                open_bank(YB + m)
                pe.matmul(bank[YB + m][:], GT[:, 0:P], U[:, 0, 0:BLK], start=True, stop=True).then_inc(full[YB + m], 1)
            with pe.Fori(0, nr) as i:
                n.enter(i, {k: c for k, c in dict(ROUND, s=2, g=2).items() if k[:4] != "full"})
                drained(GATE + 1, UP + 1)
                for b in range(FB):
                    cols_block([GATE + b % 2], 1)
                    cols_block([UP + b % 2], 1)
                    if b < 2:
                        if b == 0:
                            drained(YB, YB + 1)
                        scatter(b)
                    if b == 2:
                        pe.wait_ge(g_ready, n.step("g", 2))
                        open_bank(TR)
                        for t in range(TT):
                            last = pe.transpose(bank[TR][:, t * P:(t + 1) * P], G[:, t, :], ident[:])
                        last.then_inc(full[TR], 1)
                    if b == FB - 2:
                        for g in range(2):
                            hidden_transposes(g, 1)
                gather()
                open_bank(YB)
                open_bank(YB + 1)
                for g in range(7):
                    down_units(g, 1, (YB, YB + 1), 7)
                    if g + 2 < 7:
                        if g + 2 == 6:
                            drained(UP)
                        hidden_transposes(g + 2, 1)
                n.count["u"] = U0
                n.leave(nr)
            drained(YB, YB + 1)
            scatter(0)
            scatter(1)


_INS = ["x", "positions", "g_mix", "g_ffn", "g_final", "w_in_attn", "w_out_attn", "attn_sinks", "w_in_rec",
        "rec_lower_bounds", "rec_norm_g", "w_out_rec", "w_gate_dense", "w_up_dense", "w_down_dense",
        "w_router", "w_gate_moe", "w_up_moe", "w_down_moe"]


def kernel(**inputs):
    import numpy as _np
    import concourse.bacc as _bacc
    from concourse import mybir as _mybir
    from concourse.bass_utils import run_bass_kernel_spmd as _run

    nc = _bacc.Bacc("TRN2", target_bir_lowering=False, num_devices=1)
    arrays, args = {}, []
    for name in _INS:
        a = _np.ascontiguousarray(inputs[name])
        arrays[f"in_{name}_dram"] = a
        args.append(nc.dram_tensor(f"in_{name}_dram", a.shape, _mybir.dt.from_np(a.dtype), kind="ExternalInput").ap())
    shape = inputs["x"].shape
    out = nc.dram_tensor("out_0_dram", shape, _mybir.dt.float32, kind="ExternalOutput").ap()
    build(nc, *args, out)
    r = _run(nc, [arrays], core_ids=[0])
    return r.results[0]["out_0_dram"]
```

```python
from contextlib import ExitStack

import numpy as np

import concourse.bass as bass
from concourse import mybir

ALU = mybir.AluOpType
ACT = mybir.ActivationFunctionType
AX = mybir.AxisListType
F32 = mybir.dt.float32
F32R = mybir.dt.float32r
I32 = mybir.dt.int32
U32 = mybir.dt.uint32
U8 = mybir.dt.uint8

P = 128
TT = 2
TOK = P * TT
D = 1024
KC = D // P
EPS = 1e-6
HD = 64
AH, BH, KVH = 8, 8, 2
WIN_A, WIN_B = 128, 127
ROT = 16
THETA = 500000.0
CH = 8
FF = 3584
NE = 8
CAP = 128
UNIT = 2048
BLK = 512
RAW = 7
SPL = 3
FB = FF // BLK
FCH = FF // P
FFN_UNITS = 4 * FB + FCH // 2
LEAD = RAW + SPL
AHEAD = 2
LEVELS = 7
BIG = 3.0e38
SCALE = HD ** -0.5

GATE, UP, TR, YB = 0, 2, 4, 6
TB = (4, 5, 2, 3)
OB = (0, 1, 6, 7)
SB, PB, VB = (0, 1), 2, (4, 5)
QKT = (0, 1, 2, 3, 6, 7, 3)
OUT_A = ((3, 6), (7, 0))
FILLER = {0: (6, 0), 1: (6, 1), 2: (7, 0), 3: (7, 1), 4: (8, 0), 5: (8, 1),
          11: (9, 0), 12: (9, 1), 13: (10, 0), 15: (10, 1)}
SPLIT_AT = {2: 10, 4: 11, 11: 12, 13: 13}
LAST = ((TR, TR + 1), (GATE, UP))
OUT_R = ((0, 1), (2, 3))


class Tally:

    def __init__(self):
        self.count, self.per, self.var = {}, {}, None

    def at(self, key, less=0):
        c = self.count.get(key, 0) - less
        p = self.per.get(key, 0)
        return c if self.var is None or not p else self.var * p + c

    def step(self, key, by=1):
        self.count[key] = self.count.get(key, 0) + by
        return self.at(key)

    def enter(self, var, per):
        self.var, self.per, self.start = var, per, dict(self.count)

    def leave(self, rounds):
        for k in set(self.count) | set(self.per):
            got = self.count.get(k, 0) - self.start.get(k, 0)
            assert got == self.per.get(k, 0), (k, got, self.per.get(k, 0))
        self.count, self.var = dict(self.start), rounds


def spread(ap, dim, n):
    shape = list(ap.shape)
    assert shape[dim] == 1
    shape[dim] = n
    return ap.broadcast_to(shape)


def col_blocks(w, c0, n):
    v = w.rearrange("(k p) f -> p k f", p=P)
    return [v[:, h * 4:h * 4 + 4, c0:c0 + n] for h in range(2)]


def build(nc, x, positions, g_mix, g_ffn, g_final, w_in_attn, w_out_attn, attn_sinks, w_in_rec,
          rec_lower_bounds, rec_norm_g, w_out_rec, w_gate_dense, w_up_dense, w_down_dense,
          w_router, w_gate_moe, w_up_moe, w_down_moe, out):
    ctx = ExitStack()
    with ctx:
        def sb(name, shape, dt=F32):
            return ctx.enter_context(nc.sbuf_tensor(name, shape, dt))

        def sem(name):
            return ctx.enter_context(nc.semaphore(name))

        raw = sb("raw", [P, RAW, UNIT])
        w_hi = sb("w_hi", [P, SPL, UNIT], F32R)
        w_lo = sb("w_lo", [P, SPL, UNIT], F32R)
        X = sb("X", [P, TT, D])
        U = sb("U", [P, TT, D])
        t_hi = sb("t_hi", [P, KC, TOK], F32R)
        t_lo = sb("t_lo", [P, KC, TOK], F32R)
        h_hi = sb("h_hi", [P, 2, BLK], F32R)
        h_lo = sb("h_lo", [P, 2, BLK], F32R)
        work = sb("work", [P, 13312])
        ident = sb("ident", [P, P])
        tri = sb("tri", [P, P])
        ones = sb("ones", [P, P])
        slots = sb("slots", [P, P])
        iota8 = sb("iota8", [P, 8])
        lev_mask = sb("lev_mask", [P, LEVELS, P], U8)
        col = sb("col", [P, 56])
        lbc = sb("lbc", [P, 8, 8])
        sk8 = sb("sk8", [P, 8])
        posi = sb("posi", [P, TT], I32)
        posf = sb("posf", [P, TT])
        rope = sb("rope", [P, 8, TT, 8])
        ss = sb("ss", [P, 5, 8])
        rs_row = sb("rs_row", [P, TOK])
        ss16 = sb("ss16", [P, 3, TT, CH])
        dg = sb("dg", [P, CH * TT])
        epsc = sb("epsc", [P, 4])
        wr = sb("wr", [P, KC, NE])
        wr16 = sb("wr16", [P, KC, 2 * NE], F32R)
        wr_hi, wr_lo = wr16[:, :, 0:NE], wr16[:, :, NE:2 * NE]
        ST = sb("ST", [P, TOK], F32R)
        lgT = sb("lgT", [2 * NE, TOK])
        fold = sb("fold", [2 * NE, NE])
        att = sb("att", [P, 3, 16])
        rt = sb("rt", [P, 12, TT, 8])
        rti = sb("rti", [P, TT, 8], U32)
        cols = sb("cols", [P, TT, 2 * NE + 1])
        gates = sb("gates", [P, TT, 2 * NE])
        cur = sb("cur", [P, 4])
        cnt = sb("cnt", [P, 2])
        nrounds = sb("nrounds", [P, 2], I32)

        bank = [ctx.enter_context(nc.psum_tensor(f"bank{i}", [P, BLK], F32)) for i in range(8)]

        def w_at(a, n):
            return work[:, a:a + n]

        NH = 2 * AH + BH + 2 * KVH + AH
        proj = w_at(0, TT * NH * HD).rearrange("p (t h d) -> p t h d", t=TT, h=NH)
        qkT = w_at(4608, 13 * TOK).rearrange("p (c n) -> p c n", c=13)
        sc = w_at(7936, 3 * 384).rearrange("p (s n) -> p s n", s=3)
        pT = w_at(9088, 2 * 384).rearrange("p (s n) -> p s n", s=2)
        rp = w_at(9856, 4 * TT * 26 * 8).rearrange("p (s t h d) -> p s t h d", s=4, t=TT, h=26)
        mi = w_at(4608, 3 * 384).bitcast(I32).rearrange("p (s n) -> p s n", s=3)
        mf = w_at(4608 + 1152, 5 * 384).rearrange("p (s n) -> p s n", s=5)
        biasA = w_at(11520, 384)
        biasB = w_at(11904, 384)
        rows = work[0:56, 12288:12288 + P]
        qT = w_at(0, 2048)
        kT = w_at(2048, 2048)
        fT = w_at(4096, 2048)
        aT = w_at(8192, 2048)
        aX = w_at(10240, 1024)
        V = w_at(11264, 2048).rearrange("p (t n) -> p t n", t=TT)
        sq = w_at(0, 2048).rearrange("p (s n) -> p s n", s=4)
        tot = [fT] + [w_at(6144 + 2048 - (4096 >> i), 2048 >> i) for i in range(1, LEVELS)]
        xr, xr2 = w_at(12416, P), w_at(12544, P)
        H = w_at(0, TT * FF).rearrange("p (t f) -> p t f", t=TT)
        y_hi = [t_hi[:, 4 * m:4 * m + 4, CAP:2 * CAP] for m in range(2)]
        y_lo = [t_lo[:, 4 * m:4 * m + 4, CAP:2 * CAP] for m in range(2)]
        S = w_at(8704, TOK).rearrange("p (t c) -> p t c", t=TT)
        gf = w_at(9216, D)
        outb = w_at(0, TT * D).rearrange("p (t n) -> p t n", t=TT)

        def outputs_at(t_part, h_part, j):
            return t_part[:, j, :] if j >= AH // 2 else h_part[:, j // 2, j % 2 * TOK:(j % 2 + 1) * TOK]

        def proj_place(nb, t, src):
            first = (0, AH, 28, 2 * AH, 2 * AH + BH)[nb]
            if nb == 3:
                return (proj[:, t, first:first + 8, :].rearrange("p (j a) d -> p a j d", a=2),
                        src[:].rearrange("p (a j d) -> p a j d", a=2, j=4))
            h = 4 if nb == 4 else 8
            return proj[:, t, first:first + h, :], src[:, 0:h * HD].rearrange("p (h d) -> p h d", h=h)

        x_in, small_in, pos_in = sem("x_in"), sem("small_in"), sem("pos_in")
        row_in, wr_in, gf_in = sem("row_in"), sem("wr_in"), sem("gf_in")
        sinks = sem("sinks")
        loaded = [sem(f"loaded{i}") for i in range(RAW)]
        hi_done, lo_done = sem("hi_done"), sem("lo_done")
        unit_done = sem("unit_done")
        full = [sem(f"full{i}") for i in range(8)]
        free = [sem(f"free{i}") for i in range(8)]
        pool_seq, act_seq, dve_seq = sem("pool_seq"), sem("act_seq"), sem("dve_seq")
        consts = sem("consts")
        sq_done = sem("sq_done")
        rs_done = sem("rs_done")
        u_done = sem("u_done")
        sg_done = sem("sg_done")
        row_done = sem("row_done")
        th_done = sem("th_done")
        rope_r, rope_s = sem("rope_r"), sem("rope_s")
        rope_m = sem("rope_m")
        lb_e = sem("lb_e")
        lb_d = sem("lb_d")
        roped = sem("roped")
        mx_ready, ex_ready = sem("mx_ready"), sem("ex_ready")
        p_ready, pv_done, oh_done = sem("p_ready"), sem("pv_done"), sem("oh_done")
        fg_done = sem("fg_done")
        qk_done = sem("qk_done")
        tot_done = sem("tot_done")
        qp_done = sem("qp_done")
        lev_done = sem("lev_done")
        kr_done = sem("kr_done")
        osq_done, oss_done, ostd_done = sem("osq_done"), sem("oss_done"), sem("ostd_done")
        hh_done = sem("hh_done")
        wr_hi_d, wr_split = sem("wr_hi_d"), sem("wr_split")
        rt_d, rt_e = sem("rt_d"), sem("rt_e")
        mask_done, rounds_in = sem("mask_done"), sem("rounds_in")
        s_done = sem("s_done")
        yh_done = sem("yh_done")
        out_done, stored = sem("out_done"), sem("stored")

        wa = w_in_attn[0]
        wrr = w_in_rec[0]
        stream = []
        for nb in range(4):
            stream += col_blocks(wa, nb * BLK, BLK)
        stream += [wa.rearrange("(k p) f -> p k f", p=P)[:, :, 4 * BLK:4 * BLK + 256]]
        out_a = [col_blocks(w_out_attn[0], nb * BLK, BLK) for nb in range(2)]
        stream += [out_a[nb][h] for h in range(2) for nb in range(2)]
        for b in range(FB):
            stream += col_blocks(w_gate_dense[0], b * BLK, BLK) + col_blocks(w_up_dense[0], b * BLK, BLK)
        down = w_down_dense[0].rearrange("(u k p) n -> p u k n", p=P, k=2)
        stream += [down[:, u] for u in range(FCH // 2)]
        narrow = wrr.rearrange("(k p) f -> p k f", p=P)
        for first in (D, 0):
            stream += [narrow[:, :, first + 256 * j:first + 256 * j + 256] for j in range(4)]
        for first in (2 * D, 3 * D):
            for nb in range(2):
                stream += col_blocks(wrr, first + nb * BLK, BLK)
        for nb in range(2):
            stream += col_blocks(w_out_rec[0], nb * BLK, BLK)
        U0 = len(stream)
        assert FFN_UNITS % RAW == 0 and FFN_UNITS % SPL == 0

        FILLS = {GATE: 4, GATE + 1: 3 + 1, UP: 4, UP + 1: 3 + 1, TR: 2 + 1 + 4, TR + 1: 2 + 3, YB: 1, YB + 1: 1}
        FULLS = {GATE + 1: 1, UP + 1: 1, TR: 7, TR + 1: 5}
        ROUND = dict([(f"fill{b}", c) for b, c in FILLS.items()] + [(f"full{b}", c) for b, c in FULLS.items()],
                     unit=FFN_UNITS)

        def level_bank(i, hf):
            return 4 + (1 + 2 * i + hf) % 4

        block = ctx.enter_context(nc.Block())

        @block.sync
        def _(sp):
            n = Tally()
            xv = x[0].rearrange("(t p) d -> p t d", p=P)
            sp.dma_start(X[:, 0, :], xv[:, 0, :]).then_inc(x_in, 16)
            sp.dma_start(rows[0:16, :], g_mix.rearrange("l (k p) -> (l k) p", p=P)).then_inc(small_in, 16)
            sp.dma_start(rows[16:32, :], g_ffn.rearrange("l (k p) -> (l k) p", p=P)).then_inc(small_in, 16)
            sp.dma_start(X[:, 1, :], xv[:, 1, :]).then_inc(x_in, 16)
            sp.dma_start(rows[32:40, :], rec_norm_g.rearrange("l (k p) -> (l k) p", p=P)).then_inc(small_in, 16)
            sp.dma_start(rows[40:56, :], rec_lower_bounds.rearrange("l (k p) -> (l k) p", p=P)).then_inc(small_in, 16)

            def load(src, k):
                seen = n.step("unit")
                if k >= RAW:
                    sp.wait_ge(lo_done, n.at("unit", RAW))
                shape = src.shape
                dst = raw[:, k % RAW, :]
                if len(shape) == 4:
                    dst = dst.rearrange("p (e k n) -> p e k n", e=1, k=shape[2])
                else:
                    dst = dst.rearrange("p (k n) -> p k n", k=shape[1])
                sp.dma_start(dst, src).then_inc(loaded[k % RAW], 16)

            for k, src in enumerate(stream):
                load(src, k)

            gv = w_gate_moe[0].rearrange("e (k p) f -> p e k f", p=P)
            uv = w_up_moe[0].rearrange("e (k p) f -> p e k f", p=P)
            dv = w_down_moe[0].rearrange("e (u k p) n -> p e u k n", p=P, k=2)

            def expert_unit(u, e):
                if u >= 4 * FB:
                    return dv[:, bass.ds(e, 1), u - 4 * FB]
                b, h = u // 4, u % 2
                return (gv, uv)[u % 4 // 2][:, bass.ds(e, 1), 4 * h:4 * h + 4, b * BLK:(b + 1) * BLK]

            for u in range(LEAD):
                load(expert_unit(u, 0), U0 + u)
            sp.wait_ge(rounds_in, 1)
            before = sp.value_load(nrounds[0:1, 1:2], min_val=NE - 1, max_val=2 * NE - 1)
            with sp.Fori(0, before) as i:
                n.enter(i, {"unit": FFN_UNITS})
                for u in range(LEAD, FFN_UNITS + LEAD):
                    e = (i + 1) % NE if u >= FFN_UNITS else i % NE if u < 4 * FB else (i + NE) % NE
                    load(expert_unit(u % FFN_UNITS, e), U0 + u)
                n.leave(before)
            for u in range(LEAD, FFN_UNITS):
                load(expert_unit(u, NE - 1), U0 + u)
            for u in range(AHEAD):
                load(expert_unit(u, 0), U0 + FFN_UNITS + u)

            ov = out[0].rearrange("(t p) d -> p t d", p=P)
            for t in range(TT):
                sp.wait_ge(out_done, t + 1)
                sp.dma_start(ov[:, t, :], outb[:, t, :]).then_inc(stored, 16)
            sp.wait_ge(stored, 16 * TT)

        @block.gpsimd
        def _(pool):
            pool.memset(ident[:], 0.0).then_inc(pool_seq, 1)
            pool.memset(tri[:], 1.0).then_inc(pool_seq, 1)
            pool.memset(ones[:], 1.0).then_inc(consts, 1)
            pool.memset(epsc[:, 0:1], EPS).then_inc(consts, 1)
            pool.memset(epsc[:, 1:2], float(np.pi / 2)).then_inc(consts, 1)
            pool.wait_ge(pool_seq, 2)
            pool.affine_select(out=ident[:], in_=ident[:], compare_op=ALU.not_equal, fill=1.0, base=0,
                               pattern=[[-1, P]], channel_multiplier=1).then_inc(consts, 1)
            pool.affine_select(out=tri[:], in_=tri[:], compare_op=ALU.is_gt, fill=0.0, base=0,
                               pattern=[[1, P]], channel_multiplier=-1).then_inc(consts, 1)
            pool.iota(slots[:], pattern=[[1, P]], base=1, channel_multiplier=0,
                      allow_small_or_imprecise_dtypes=True).then_inc(consts, 1)
            pool.iota(iota8[:], pattern=[[1, 8]], base=0, channel_multiplier=0,
                      allow_small_or_imprecise_dtypes=True).then_inc(consts, 1)
            pool.iota(mi[:, 0, 0:P], pattern=[[-1, P]], base=0, channel_multiplier=1).then_inc(consts, 1)
            pool.iota(mi[:, 0, P:3 * P], pattern=[[-1, TOK]], base=P, channel_multiplier=1).then_inc(consts, 1)
            pool.iota(mi[:, 1, 0:P], pattern=[[0, P]], base=0, channel_multiplier=1).then_inc(consts, 1)
            pool.iota(mi[:, 1, P:2 * P], pattern=[[1, P]], base=0, channel_multiplier=0).then_inc(consts, 1)
            pool.iota(mi[:, 1, 2 * P:3 * P], pattern=[[1, P]], base=0, channel_multiplier=-1).then_inc(consts, 1)

            for hf in range(2):
                pool.wait_ge(fg_done, 4 * (hf + 1))
                for lev in range(1, LEVELS):
                    w = 1024 >> (lev - 1)
                    below = tot[lev - 1][:, hf * w:(hf + 1) * w].rearrange("p (n two) -> p n two", two=2)
                    if lev > 1:
                        pool.wait_ge(tot_done, hf * (LEVELS - 1) + lev - 1)
                    pool.tensor_tensor(tot[lev][:, hf * w // 2:(hf + 1) * w // 2], below[:, :, 0],
                                       below[:, :, 1], ALU.mult).then_inc(tot_done, 1)
            pool.wait_ge(tot_done, 2 * (LEVELS - 1))
            for lev in range(LEVELS):
                for hf in range(2):
                    half = 1 << lev
                    pool.wait_ge(lev_done, 2 * lev + hf + 1)
                    kv = kT[:, hf * 1024:(hf + 1) * 1024].rearrange("p (n two h) -> p n two h", two=2, h=half)
                    tv = tot[lev][:, hf * (1024 >> lev):(hf + 1) * (1024 >> lev)].rearrange(
                        "p (n two o) -> p n two o", two=2, o=1)
                    pool.tensor_tensor(kv[:, :, 0, :], kv[:, :, 0, :], spread(tv[:, :, 1, :], 2, half),
                                       ALU.mult).then_inc(kr_done, 1)

        @block.scalar
        def _(act):
            n = Tally()

            def link(ins):
                ins.then_inc(act_seq, 1)
                act.wait_ge(act_seq, n.step("seq"))

            def wait_full(b):
                n.step(f"fill{b}")
                act.wait_ge(full[b], n.step(f"full{b}"))

            def wait_units(k, *banks):
                saw_product(*banks)
                act.wait_ge(unit_done, unit_at(k))

            def unit_at(k):
                return k if n.var is None else n.var * FFN_UNITS + k

            def saw_product(*banks):
                for b in banks:
                    n.step(f"fill{b}")

            def drained(*banks):
                for b in banks:
                    act.wait_ge(free[b], n.at(f"fill{b}"))

            def saw(*banks):
                for b in banks:
                    n.step(f"fill{b}")
                    n.step(f"full{b}")

            def split_to(k):
                while n.count.get("u", 0) < k:
                    u = n.count["u"] = n.count.get("u", 0) + 1
                    n.step("unit")
                    r = (u - 1) % RAW
                    act.wait_ge(loaded[r], n.step(f"loaded{r}", 16))
                    if u > SPL:
                        act.wait_ge(unit_done, n.at("unit", SPL))
                    act.activation(w_hi[:, (u - 1) % SPL, :], raw[:, r, :], ACT.Copy).then_inc(hi_done, 1)

            act.dma_start(sk8[:], attn_sinks.broadcast_to([P, BH])).then_inc(row_in, 16)
            for t in range(TT):
                act.dma_start(posi[:, t:t + 1],
                              positions[0, t * P:(t + 1) * P].rearrange("(p o) -> p o", o=1)).then_inc(pos_in, 16)
            act.dma_start(wr[:], w_router[0].rearrange("(k p) e -> p k e", p=P)).then_inc(wr_in, 16)

            def rms(k):
                for t in range(TT):
                    link(act.activation(U[:, t, :], X[:, t, :], ACT.Square, accum_out=ss[:, k, t:t + 1]))
                act.activation(ss[:, k, 2:4], ss[:, k, 0:2], ACT.Sqrt, scale=1.0 / D,
                               bias=epsc[:, 0:1]).then_inc(sq_done, 1)

            def t_hi_part(gain, first=None):
                for j in range(4):
                    if j == 2 and first is not None:
                        split_to(first + 1)
                    wait_full(TB[j])
                    for c in range(2):
                        k = 2 * j + c
                        act.activation(t_hi[:, k, :], bank[TB[j]][:, c * TOK:(c + 1) * TOK], ACT.Copy,
                                       scale=col[:, gain + k:gain + k + 1]).then_inc(th_done, 1)

            saw(4)
            act.wait_ge(consts, 12)
            act.activation(epsc[:, 3:4], epsc[:, 0:1], ACT.Copy)
            act.wait_ge(free[4], 1)
            t_hi_part(0, first=0)
            split_to(SPL)
            act.wait_ge(x_in, 16 * TT)
            rms(0)
            act.wait_ge(lb_d, 1)
            act.activation(lbc[:, 1:3, :], lbc[:, 1:3, :], ACT.Exp).then_inc(lb_e, 1)
            act.wait_ge(rope_r, 1)
            act.activation(rope[:, 5, :, :], rope[:, 3, :, :], ACT.Sin).then_inc(rope_s, 1)
            act.activation(rope[:, 6, :, :], rope[:, 4, :, :], ACT.Sin, scale=-1.0,
                           bias=epsc[:, 1:2]).then_inc(rope_s, 1)
            act.wait_ge(wr_in, 16)
            act.activation(wr_hi, wr[:], ACT.Copy).then_inc(wr_hi_d, 1)

            def place(nb, b):
                to, src = proj_place(nb, 0, bank[b])
                act.activation(to, src, ACT.Copy, scale=ss[:, 0, 4:5]).then_inc(free[b], 1)

            def qk_copy(j):
                c = min(2, 13 - 2 * j)
                act.activation(qkT[:, 2 * j:2 * j + c, :],
                               bank[QKT[j]][:, 0:c * TOK].rearrange("p (c n) -> p c n", c=c),
                               ACT.Copy).then_inc(free[QKT[j]], 1)

            for nb in range(2):
                split_to(nb + 2 + SPL)
                saw_product(2 * nb + 1)
                wait_units(2 * nb + 2, 2 * nb)
                if nb == 0:
                    act.wait_ge(rs_done, 1)
                place(nb, 2 * nb)
            split_to(5 + SPL)
            for j in range(4):
                wait_full(QKT[j])
                if j % 2 == 0:
                    qk_copy(j)
            split_to(6 + SPL)
            saw_product(5)
            wait_units(6, 4)
            place(2, 4)

            for s in range(AH + BH + 3):
                if s == AH:
                    for j in range(4, 7):
                        wait_full(QKT[j])
                        if j % 2 == 0:
                            qk_copy(j)
                if s - 3 >= 0 and (s - 3) % 2 == 1:
                    j = (s - 3) // 2
                    saw_product(VB[j % 2])
                    act.wait_ge(pv_done, 2 * j + 2)
                    act.activation(outputs_at(t_hi, h_hi, j), bank[VB[j % 2]][:, 0:TOK], ACT.Copy).then_inc(oh_done, 1)
                if 0 <= s - 2 < AH + BH:
                    h = s - 2
                    wait_full(PB)
                    if h >= 2:
                        act.wait_ge(pv_done, h - 1)
                    act.activation(pT[:, h % 2, :], bank[PB][:, 0:3 * P], ACT.Copy).then_inc(free[PB], 1)
                if s < AH + BH:
                    k, g = s % 3, s >= AH
                    saw(SB[s % 2])
                    act.wait_ge(mx_ready, s + 1)
                    act.activation(sc[:, k, 0:P], sc[:, k, 0:P], ACT.Exp, scale=SCALE,
                                   bias=att[:, k, 2:3], accum_out=att[:, k, 4:5]).then_inc(ex_ready, 1)
                    act.activation(sc[:, k, P:3 * P], sc[:, k, P:3 * P], ACT.Exp, scale=SCALE,
                                   bias=att[:, k, 3:4], accum_out=att[:, k, 5:6]).then_inc(ex_ready, 1)
                    if g:
                        act.activation(att[:, k, 8:10], att[:, k, 10:12], ACT.Exp,
                                       scale=SCALE).then_inc(ex_ready, 1)
                if s == 4:
                    saw_product(7)
                    wait_units(8, 6)
                    place(3, 6)
                if s == 6:
                    wait_units(9, 3)
                    for t in range(TT):
                        to, src = proj_place(4, t, bank[3][:, t * 256:(t + 1) * 256])
                        ins = act.activation(to, src, ACT.Copy, scale=ss[:, 0, 4 + t:5 + t])
                    ins.then_inc(free[3], 1)
                if s in SPLIT_AT:
                    split_to(SPLIT_AT[s])

            def out_proj(base, banks):
                split_to(base + 4)
                saw_product(*banks[0], *banks[1])

            def next_stage(k, gain, base, x_banks):
                split_to(base + 2)
                t_hi_part(gain)
                if k < 3:
                    split_to(base + SPL)
                drained(*x_banks)
                rms(k)
                act.wait_ge(rs_done, k + 1)

            out_proj(9, OUT_A)
            next_stage(1, 16, 13, OUT_A[0] + OUT_A[1])

            def ffn_dense(base):
                for b in range(FB):
                    split_to(base + 4 * b + 5)
                    wait_units(base + 4 * b + 2, GATE, GATE + 1)
                    for t in range(TT):
                        act.activation(H[:, t, b * BLK:(b + 1) * BLK], bank[GATE + t][:], ACT.Silu,
                                       scale=ss[:, 1, 4 + t:5 + t]).then_inc(free[GATE + t], 1)
                    saw_product(UP, UP + 1)
                    if b == FB - 1:
                        for g in range(2):
                            hidden_hi(g)
                for g in range(2, 14):
                    split_to(base + 28 + g - 2 + 1 + SPL)
                    hidden_hi(g)
                split_to(base + FFN_UNITS)
                saw_product(GATE, GATE + 1, YB, YB + 1)

            def hidden_hi(g):
                wait_full(TR + g % 2)
                act.activation(h_hi[:, g % 2, :], bank[TR + g % 2][:], ACT.Copy).then_inc(hh_done, 1)

            ffn_dense(13)
            next_stage(2, 8, 55, (YB, YB + 1, GATE, GATE + 1))

            saw(7)
            for j in range(4):
                split_to(55 + j + 1 + SPL)
                saw_product(j)
                drained(j)
                act.activation(fT[:, j * BLK:(j + 1) * BLK], fT[:, j * BLK:(j + 1) * BLK],
                               ACT.Sigmoid).then_inc(sg_done, 1)
            for j in range(4):
                split_to(59 + j + 1 + SPL)
                saw_product(4 + j)
                drained(4 + j)
                act.activation(qT[:, j * BLK:(j + 1) * BLK], qT[:, j * BLK:(j + 1) * BLK],
                               ACT.Silu).then_inc(sg_done, 1)
            for nb in range(4):
                split_to(63 + min(2 * nb + 2, 7) + SPL)
                wait_units(63 + 2 * nb + 2, 2 * nb % 4, 2 * nb % 4 + 1)
                cs = slice(nb % 2 * BLK, (nb % 2 + 1) * BLK)
                for t in range(TT):
                    act.activation((V if nb < 2 else U)[:, t, cs], bank[2 * nb % 4 + t][:],
                                   ACT.Copy if nb < 2 else ACT.Silu,
                                   scale=ss[:, 2, 4 + t:5 + t]).then_inc(free[2 * nb % 4 + t], 1)
            saw(4)
            for i in range(LEVELS + 1):
                saw_product(level_bank(i, 0), level_bank(i, 1))
            def o_rms(f4):
                t, hf = f4 // 2, f4 % 2
                act.wait_ge(oss_done, f4 + 1)
                act.activation(ss16[:, 1, t, 4 * hf:4 * hf + 4], ss16[:, 0, t, 4 * hf:4 * hf + 4], ACT.Sqrt,
                               scale=1.0 / P, bias=epsc[:, 0:1]).then_inc(ostd_done, 1)

            act.activation(epsc[:, 2:3], epsc[:, 0:1], ACT.Sqrt)
            for f4, b in enumerate(OB):
                wait_full(b)
                act.activation(sq[:, f4, :], bank[b][:], ACT.Square).then_inc(osq_done, 1)
                if f4:
                    o_rms(f4 - 1)
            o_rms(3)
            t_hi_part(32)
            out_proj(71, OUT_R)
            next_stage(3, 24, U0, OUT_R[0] + OUT_R[1])

            saw(6)
            act.dma_start(gf[:], g_final.rearrange("(o n) -> o n", o=1).broadcast_to([P, D])).then_inc(gf_in, 16)
            saw(5, 4, 5)
            act.wait_ge(rt_d, 1)
            act.activation(rt[:, 5, :, 0:1], rt[:, 4, :, 0:1], ACT.Exp).then_inc(rt_e, 1)

            def gather_hi():
                for m, b in enumerate((GATE + 1, UP + 1)):
                    wait_full(b)
                    for c in range(4):
                        k = 4 * m + c
                        act.activation(t_hi[:, k, 0:CAP], bank[b][:, c * P:(c + 1) * P], ACT.Copy,
                                       scale=col[:, 24 + k:25 + k]).then_inc(th_done, 1)

            def y_copy():
                for m in range(2):
                    act.activation(y_hi[m], bank[YB + m][:].rearrange("p (c n) -> p c n", c=4), ACT.Copy).then_inc(yh_done, 1)

            gather_hi()
            act.wait_ge(rounds_in, 1)
            nr = act.value_load(nrounds[0:1, 0:1], min_val=NE, max_val=2 * NE)
            with act.Fori(0, nr) as i:
                n.enter(i, dict(ROUND, **{f"loaded{r}": 16 * FFN_UNITS // RAW for r in range(RAW)}))
                for b in range(FB):
                    if b == 3:
                        split_to(U0 + 4 * b + 3)
                        wait_full(TR)
                        act.activation(ST[:], bank[TR][:, 0:TOK], ACT.Copy).then_inc(free[TR], 1)
                    split_to(U0 + 4 * b + 5)
                    wait_units(U0 + 4 * b + 2, GATE + b % 2)
                    act.activation(H[:, 0, b * BLK:(b + 1) * BLK], bank[GATE + b % 2][:],
                                   ACT.Silu).then_inc(free[GATE + b % 2], 1)
                    saw_product(UP + b % 2)
                    if b < 2:
                        saw(TR, TR + 1)
                for g in range(2):
                    hidden_hi(g)
                split_to(U0 + 28 + SPL)
                gather_hi()
                for g in range(2, 7):
                    split_to(U0 + 28 + 2 * (g - 2) + 2 + SPL)
                    hidden_hi(g)
                split_to(U0 + FFN_UNITS + AHEAD)
                wait_units(U0 + FFN_UNITS, YB, YB + 1)
                y_copy()
                n.count["u"] = U0 + AHEAD
                n.leave(nr)
            act.activation(epsc[:, 2:3], epsc[:, 0:1], ACT.Sqrt)
            for t in range(TT):
                saw(*LAST[t])
                drained(*LAST[t])
                link(act.activation(U[:, t, :], X[:, t, :], ACT.Square, accum_out=ss[:, 4, t:t + 1]))
                act.activation(ss[:, 4, 2 + t:3 + t], ss[:, 4, t:t + 1], ACT.Sqrt, scale=1.0 / D,
                               bias=epsc[:, 0:1]).then_inc(sq_done, 1)

        @block.vector
        def _(dve):
            n = Tally()

            def link(ins):
                ins.then_inc(dve_seq, 1)
                dve.wait_ge(dve_seq, n.step("seq"))

            def wait_full(b):
                n.step(f"fill{b}")
                dve.wait_ge(full[b], n.step(f"full{b}"))

            def wait_units(k, *banks):
                saw_product(*banks)
                dve.wait_ge(unit_done, unit_at(k))

            def unit_at(k):
                return k if n.var is None else n.var * FFN_UNITS + k

            def saw_product(*banks):
                for b in banks:
                    n.step(f"fill{b}")

            def drained(*banks):
                for b in banks:
                    dve.wait_ge(free[b], n.at(f"fill{b}"))

            def saw(*banks):
                for b in banks:
                    n.step(f"fill{b}")
                    n.step(f"full{b}")

            def split_to(k):
                while n.count.get("u", 0) < k:
                    u = n.count["u"] = n.count.get("u", 0) + 1
                    dve.wait_ge(hi_done, n.step("unit"))
                    s, r = (u - 1) % SPL, (u - 1) % RAW
                    dve.tensor_tensor(w_lo[:, s, :], raw[:, r, :], w_hi[:, s, :].bitcast(F32),
                                      ALU.subtract).then_inc(lo_done, 1)

            def inverse_rms(k):
                dve.wait_ge(sq_done, k + 1)
                dve.reciprocal(ss[:, k, 4:6], ss[:, k, 2:4]).then_inc(rs_done, 1)
                dve.wait_ge(rs_done, k + 1)

            def t_lo_part(gain, first=None):
                for j in range(4):
                    if j == 2 and first is not None:
                        split_to(first + 1)
                    wait_full(TB[j])
                    dve.wait_ge(th_done, n.step("th", 2))
                    for c in range(2):
                        k = 2 * j + c
                        ins = dve.scalar_tensor_tensor(
                            t_lo[:, k, :], bank[TB[j]][:, c * TOK:(c + 1) * TOK], col[:, gain + k:gain + k + 1],
                            t_hi[:, k, :].bitcast(F32), ALU.mult, ALU.subtract)
                        if c == 1:
                            ins.then_inc(free[TB[j]], 1)

            dve.wait_ge(consts, 12)
            dist = mi[:, 0, :]
            f = [mf[:, i, :] for i in range(5)]
            link(dve.tensor_copy(f[0], dist))
            link(dve.tensor_scalar(mi[:, 2, :], dist, 3, None, ALU.bitwise_and))
            link(dve.tensor_scalar(f[1], mi[:, 2, :], 0, None, ALU.is_equal))
            link(dve.tensor_scalar(mi[:, 2, :], dist, 15, None, ALU.bitwise_and))
            link(dve.tensor_scalar(f[2], mi[:, 2, :], 0, None, ALU.is_equal))
            link(dve.tensor_tensor(f[1], f[1], f[2], ALU.add))
            link(dve.tensor_scalar(f[2], f[0], float(WIN_A), None, ALU.is_le))
            link(dve.tensor_tensor(f[1], f[1], f[2], ALU.add))
            link(dve.tensor_scalar(f[2], f[0], 0.0, None, ALU.is_ge))
            link(dve.tensor_tensor(f[1], f[1], f[2], ALU.mult))
            saw(4)
            dve.wait_ge(full[4], 1)
            dve.tensor_copy(col[:], bank[4][:, 0:56]).then_inc(free[4], 1)
            dve.wait_ge(free[4], 1)
            t_lo_part(0, first=0)
            split_to(SPL)
            inverse_rms(0)

            def bias_masks():
                link(dve.tensor_scalar(f[3], f[1], 0.0, -BIG, ALU.is_equal, ALU.mult))
                link(dve.tensor_scalar(f[4], f[1], 2.0, float(8 * np.log(2.0)), ALU.is_equal, ALU.mult))
                link(dve.tensor_tensor(f[3], f[3], f[4], ALU.add))
                link(dve.tensor_scalar(f[4], f[1], 3.0, float(8 * np.log(3.0)), ALU.is_equal, ALU.mult))
                link(dve.tensor_tensor(biasA[:], f[3], f[4], ALU.add))
                link(dve.tensor_scalar(f[4], f[0], float(WIN_B), None, ALU.is_le))
                link(dve.tensor_tensor(f[4], f[4], f[2], ALU.mult))
                link(dve.tensor_scalar(biasB[:], f[4], -1.0, BIG, ALU.add, ALU.mult))
                link(dve.tensor_tensor(mi[:, 2, 0:P], mi[:, 1, 0:P], mi[:, 1, P:2 * P], ALU.bitwise_xor))
                link(dve.tensor_copy(f[0][:, 0:P], mi[:, 2, 0:P]))
                link(dve.tensor_scalar(f[1][:, 0:P], mi[:, 1, 2 * P:3 * P], 0.0, 1e9, ALU.is_lt, ALU.mult))
                link(dve.tensor_tensor(xr[:], f[0][:, 0:P], f[1][:, 0:P], ALU.add))

            link(dve.tensor_tensor(lbc[:, 0, :], col[:, 40:48], col[:, 48:56], ALU.max))
            link(dve.tensor_tensor(lbc[:, 1, :], col[:, 40:48], lbc[:, 0, :], ALU.subtract))
            dve.tensor_tensor(lbc[:, 2, :], col[:, 48:56], lbc[:, 0, :], ALU.subtract).then_inc(lb_d, 1)
            dve.wait_ge(pos_in, 16 * TT)
            link(dve.tensor_copy(posf[:], posi[:]))
            inv = [float(np.float32(THETA) ** np.float32(-2.0 * j / ROT)) for j in range(ROT // 2)]
            for j in range(ROT // 2):
                dve.memset(rope[:, 0, 0, j:j + 1], inv[j]).then_inc(dve_seq, 1)
                n.step("seq")
            dve.wait_ge(dve_seq, n.at("seq"))
            ang = rope[:, 1]
            for t in range(TT):
                link(dve.tensor_scalar(ang[:, t, :], rope[:, 0, 0, :], posf[:, t:t + 1], None, ALU.mult))
            turn, red = rope[:, 2], rope[:, 3]
            magic = 1.5 * 2.0 ** 23
            c1 = 6.28125
            c2 = float(np.float32(round((2 * np.pi - c1) * 2 ** 20) / 2 ** 20))
            c3 = 2 * np.pi - c1 - c2
            link(dve.tensor_scalar(turn, ang, float(1 / (2 * np.pi)), magic, ALU.mult, ALU.add))
            link(dve.tensor_scalar(turn, turn, -magic, None, ALU.add))
            link(dve.scalar_tensor_tensor(red, turn, -c1, ang, ALU.mult, ALU.add))
            link(dve.scalar_tensor_tensor(red, turn, -c2, red, ALU.mult, ALU.add))
            link(dve.scalar_tensor_tensor(red, turn, -c3, red, ALU.mult, ALU.add))
            link(dve.tensor_scalar(red, red, 3.1415925, -3.1415925, ALU.min, ALU.max))
            dve.scalar_tensor_tensor(rope[:, 4], red, -1.0, red, ALU.mult, ALU.max).then_inc(rope_r, 1)
            dve.wait_ge(lb_e, 1)
            link(dve.tensor_tensor(lbc[:, 3, :], lbc[:, 1, :], lbc[:, 2, :], ALU.add))
            link(dve.reciprocal(lbc[:, 4, :], lbc[:, 3, :]))
            link(dve.tensor_tensor(lbc[:, 1, :], lbc[:, 1, :], lbc[:, 4, :], ALU.mult))
            link(dve.tensor_tensor(lbc[:, 2, :], lbc[:, 2, :], lbc[:, 4, :], ALU.mult))
            link(dve.tensor_tensor(lbc[:, 3, :], lbc[:, 1, :], lbc[:, 2, :], ALU.add))
            link(dve.tensor_tensor(lbc[:, 5, :], lbc[:, 3, :], lbc[:, 1, :], ALU.subtract))
            link(dve.tensor_scalar(lbc[:, 6, :], lbc[:, 5, :], -1.0, 1.0, ALU.mult, ALU.add))
            link(dve.tensor_tensor(fold[:], ident[0:2 * NE, 0:NE], ident[0:2 * NE, NE:2 * NE], ALU.add))
            dve.wait_ge(wr_hi_d, 1)
            dve.tensor_tensor(wr_lo, wr[:], wr_hi.bitcast(F32), ALU.subtract).then_inc(wr_split, 1)

            def place(nb, b):
                to, src = proj_place(nb, 1, bank[b])
                dve.tensor_scalar(to, src, ss[:, 0, 5:6], None, ALU.mult).then_inc(free[b], 1)

            def rotate(h0, h1, steps):
                x1, x2 = proj[:, :, h0:h1, 0:8], proj[:, :, h0:h1, 8:16]
                sin = spread(rope[:, 5].rearrange("p t (o d) -> p t o d", o=1), 2, h1 - h0)
                cos = spread(rope[:, 6].rearrange("p t (o d) -> p t o d", o=1), 2, h1 - h0)
                r = [rp[:, i, :, h0:h1, :] for i in range(4)]
                dve.tensor_tensor(r[0], x1, cos, ALU.mult).then_inc(rope_m, 1)
                dve.tensor_tensor(r[1], x2, sin, ALU.mult).then_inc(rope_m, 1)
                dve.tensor_tensor(r[2], x2, cos, ALU.mult).then_inc(rope_m, 1)
                dve.tensor_tensor(r[3], x1, sin, ALU.mult).then_inc(rope_m, 1)
                dve.wait_ge(rope_m, steps + 4)
                dve.tensor_tensor(x1, r[0], r[1], ALU.subtract).then_inc(roped, 1)
                dve.tensor_tensor(x2, r[2], r[3], ALU.add).then_inc(roped, 1)

            def qk_copy(j):
                dve.tensor_copy(qkT[:, 2 * j:2 * j + 2, :],
                                bank[QKT[j]][:].rearrange("p (c n) -> p c n", c=2)).then_inc(free[QKT[j]], 1)

            for nb in range(2):
                split_to(nb + 2 + SPL)
                saw_product(2 * nb)
                wait_units(2 * nb + 2, 2 * nb + 1)
                place(nb, 2 * nb + 1)
                if nb == 0:
                    bias_masks()
            dve.wait_ge(rope_s, 2)
            drained(0, 1, 2, 3)
            rotate(0, 2 * AH, 0)
            split_to(5 + SPL)
            for j in range(4):
                wait_full(QKT[j])
                if j % 2 == 1:
                    qk_copy(j)
            split_to(6 + SPL)
            saw_product(4)
            wait_units(6, 5)
            place(2, 5)
            dve.wait_ge(row_in, 16)
            dve.tensor_scalar(sk8[:], sk8[:], 1.0 / SCALE, None, ALU.mult).then_inc(sinks, 1)

            for s in range(AH + BH + 3):
                if s == AH:
                    for j in range(4, 7):
                        wait_full(QKT[j])
                        if j % 2 == 1:
                            qk_copy(j)
                if s < AH + BH:
                    k, g = s % 3, s >= AH
                    if s >= 3:
                        dve.wait_ge(full[PB], n.at(f"full{PB}"))
                    wait_full(SB[s % 2])
                    bias, b = biasB if g else biasA, SB[s % 2]
                    dve.tensor_tensor_reduce(out=sc[:, k, 0:P], in0=bank[b][:, 0:P], in1=bias[:, 0:P], scale=1.0,
                                             scalar=-BIG, op0=ALU.add, op1=ALU.max,
                                             accum_out=att[:, k, 0:1]).then_inc(dve_seq, 1)
                    dve.tensor_tensor_reduce(out=sc[:, k, P:3 * P], in0=bank[b][:, P:3 * P], in1=bias[:, P:3 * P],
                                             scale=1.0, scalar=-BIG, op0=ALU.add, op1=ALU.max,
                                             accum_out=att[:, k, 1:2]).then_inc(free[b], 1)
                    n.step("seq")
                    dve.wait_ge(dve_seq, n.at("seq"))
                    drained(b)
                    if g:
                        hb = s - AH
                        skc = spread(sk8[:, hb:hb + 1], 1, 2)
                        if s == AH:
                            dve.wait_ge(sinks, 1)
                        link(dve.tensor_tensor(att[:, k, 0:2], att[:, k, 0:2], skc, ALU.max))
                        link(dve.tensor_tensor(att[:, k, 10:12], skc, att[:, k, 0:2], ALU.subtract))
                    dve.tensor_scalar(att[:, k, 2:4], att[:, k, 0:2], -SCALE, None, ALU.mult).then_inc(mx_ready, 1)
                if 0 <= s - 1 < AH + BH:
                    h = s - 1
                    k, g = h % 3, h >= AH
                    dve.wait_ge(ex_ready, n.step("ex", 3 if g else 2))
                    if g:
                        link(dve.tensor_tensor(att[:, k, 4:6], att[:, k, 4:6], att[:, k, 8:10], ALU.add))
                    link(dve.reciprocal(att[:, k, 6:8], att[:, k, 4:6]))
                    dve.tensor_scalar(sc[:, k, 0:P], sc[:, k, 0:P], att[:, k, 6:7], None, ALU.mult).then_inc(p_ready, 1)
                    dve.tensor_scalar(sc[:, k, P:3 * P], sc[:, k, P:3 * P], att[:, k, 7:8], None,
                                      ALU.mult).then_inc(p_ready, 1)
                if 0 <= s - 2 < AH + BH:
                    saw(PB)
                if s - 3 >= 0 and (s - 3) % 2 == 1:
                    j = (s - 3) // 2
                    saw_product(VB[j % 2])
                    dve.wait_ge(oh_done, j + 1)
                    dve.tensor_tensor(outputs_at(t_lo, h_lo, j), bank[VB[j % 2]][:, 0:TOK],
                                      outputs_at(t_hi, h_hi, j).bitcast(F32), ALU.subtract).then_inc(free[VB[j % 2]], 1)
                if s == 4:
                    saw_product(6)
                    wait_units(8, 7)
                    place(3, 7)
                if s == 6:
                    saw_product(3)
                    drained(3, 6, 7)
                    rotate(2 * AH, 2 * AH + BH + KVH, 4)
                if s - 1 in SPLIT_AT:
                    split_to(SPLIT_AT[s - 1])

            def out_proj(base, banks, last):
                split_to(base + 4)
                for nb in range(2):
                    wait_units(base + last[nb] + 1, *banks[nb])
                    for t in range(TT):
                        add_to_x(t, nb, banks[nb][t])
                    if nb == 0:
                        split_to(base + 4 + 2)

            def add_to_x(t, nb, b):
                xb = X[:, t, nb * BLK:(nb + 1) * BLK]
                dve.tensor_tensor(xb, xb, bank[b][:], ALU.add).then_inc(free[b], 1)

            def hidden_lo(g):
                wait_full(TR + g % 2)
                dve.wait_ge(hh_done, n.step("hh"))
                dve.tensor_tensor(h_lo[:, g % 2, :], bank[TR + g % 2][:], h_hi[:, g % 2, :].bitcast(F32),
                                  ALU.subtract).then_inc(free[TR + g % 2], 1)

            out_proj(9, OUT_A, (2, 3))
            t_lo_part(16)
            split_to(13 + SPL)
            inverse_rms(1)

            def h_block(b, t, up_bank, gate_bank, rs=None):
                drained(gate_bank)
                hb = H[:, t, b * BLK:(b + 1) * BLK]
                if rs is None:
                    dve.tensor_tensor(hb, hb, bank[up_bank][:], ALU.mult).then_inc(free[up_bank], 1)
                else:
                    dve.scalar_tensor_tensor(hb, bank[up_bank][:], rs, hb, ALU.mult, ALU.mult).then_inc(free[up_bank], 1)

            base = 13
            for b in range(FB):
                if b == 1:
                    for lev in range(LEVELS):
                        link(dve.tensor_scalar(xr2[:], xr[:], float(1 << lev), None, ALU.is_ge))
                        link(dve.scalar_tensor_tensor(lev_mask[:, lev, :], xr[:], float(2 << lev), xr2[:], ALU.is_lt,
                                                      ALU.mult))
                if b == FB - 1:
                    split_to(base + 4 * b + 5)
                    for g in range(2):
                        hidden_lo(g)
                split_to(base + 4 * b + 7)
                saw_product(GATE, GATE + 1)
                wait_units(base + 4 * b + 4, UP, UP + 1)
                for t in range(TT):
                    h_block(b, t, UP + t, GATE + t, ss[:, 1, 4 + t:5 + t])
            for g in range(2, 14):
                split_to(base + 28 + g - 2 + 1 + SPL)
                hidden_lo(g)
            split_to(base + FFN_UNITS + 2)
            ybank = (YB, YB + 1, GATE, GATE + 1)
            wait_units(base + FFN_UNITS, *ybank)
            for nb in range(2):
                for t in range(TT):
                    add_to_x(t, nb, ybank[2 * t + nb])
            t_lo_part(8)
            split_to(55 + SPL)
            inverse_rms(2)
            for t in range(TT):
                dve.tensor_scalar(rs_row[:, t * P:(t + 1) * P], ident[:], ss[:, 2, 4 + t:5 + t], None,
                                  ALU.mult).then_inc(row_done, 1)
            wait_full(7)
            dve.tensor_copy(rs_row[:], bank[7][:, 0:TOK]).then_inc(free[7], 1)
            drained(7)

            def scale_rows(to, base, j, b):
                wait_units(base + j + 1, b)
                dve.tensor_tensor(to[:, j * BLK:(j + 1) * BLK].rearrange("p (c n) -> p c n", c=2),
                                  bank[b][:].rearrange("p (c n) -> p c n", c=2),
                                  spread(rs_row[:].rearrange("p (c n) -> p c n", c=1), 1, 2),
                                  ALU.mult).then_inc(free[b], 1)

            for j in range(4):
                split_to(55 + j + 1 + SPL)
                scale_rows(fT, 55, j, j)
                dve.wait_ge(sg_done, j + 1)
                for c in range(2):
                    hd = 2 * j + c
                    fc = fT[:, hd * TOK:(hd + 1) * TOK]
                    link(dve.tensor_scalar(fc, fc, lbc[:, 6, hd:hd + 1], lbc[:, 5, hd:hd + 1], ALU.mult, ALU.add))
                    dve.tensor_scalar(kT[:, hd * TOK:(hd + 1) * TOK], fc, -1.0, 1.0, ALU.mult,
                                      ALU.add).then_inc(fg_done, 1)
            for j in range(4):
                split_to(59 + j + 1 + SPL)
                scale_rows(qT, 59, j, 4 + j)
                dve.wait_ge(sg_done, 4 + j + 1)
                js = slice(j * BLK, (j + 1) * BLK)
                dve.tensor_tensor(aT[:, js], qT[:, js], kT[:, js], ALU.mult).then_inc(qk_done, 1)
                dve.wait_ge(qk_done, j + 1)
                dve.wait_ge(fg_done, 2 * (j + 1))
                dve.tensor_tensor(qT[:, js], qT[:, js], fT[:, js], ALU.mult).then_inc(qp_done, 1)
            def own():
                wait_full(4)
                dve.tensor_copy(dg[:], bank[4][:, 0:CH * TT]).then_inc(free[4], 1)
                drained(4)
                link(dve.tensor_tensor(aT[:].rearrange("p (n c) -> p n c", c=P),
                                       spread(ident[:].rearrange("p (o c) -> p o c", o=1), 1, CH * TT),
                                       spread(dg[:].rearrange("p (n o) -> p n o", o=1), 2, P), ALU.mult))

            def level(i, hf):
                lb = level_bank(i, hf)
                saw_product(lb)
                dve.wait_ge(lev_done, 2 * i + hf + 1)
                if i == LEVELS:
                    dve.tensor_copy(aX[:, hf * BLK:(hf + 1) * BLK], bank[lb][:]).then_inc(free[lb], 1)
                    return
                half = 1 << i
                qv = qT[:, hf * 1024:(hf + 1) * 1024].rearrange("p (n two h) -> p n two h", two=2, h=half)
                tv = tot[i][:, hf * (1024 >> i):(hf + 1) * (1024 >> i)].rearrange(
                    "p (n two o) -> p n two o", two=2, o=1)
                dve.tensor_tensor(qv[:, :, 1, :], qv[:, :, 1, :], spread(tv[:, :, 0, :], 2, half),
                                  ALU.mult).then_inc(qp_done, 1)
                at = aT[:, hf * 1024:(hf + 1) * 1024].rearrange("p (a n two h) -> p a n two h", a=8, two=2, h=half)
                mk = lev_mask[:, i, :].rearrange("p (a n two h) -> p a n two h", a=1, two=2, h=half)
                pb = bank[lb][:].rearrange("p (a n h) -> p a n h", a=8, h=half)
                if i:
                    drained(level_bank(i - 1, hf))
                dve.copy_predicated(at[:, :, :, 1, :], spread(mk[:, :, :, 1, :], 1, 8), pb).then_inc(free[lb], 1)

            dve.wait_ge(tot_done, 2 * (LEVELS - 1))
            for u in range(8):
                if u == 7:
                    level(LEVELS - 1, 0)
                    level(LEVELS - 1, 1)
                if u < 7:
                    split_to(63 + u + 1 + SPL)
                if u % 2:
                    saw_product(u // 2 % 2 * 2, u // 2 % 2 * 2 + 1)
                if u == 1:
                    own()
                if u:
                    for hf in range(2):
                        level(u - 1 if u < 7 else LEVELS, hf)

            def o_sums(f4):
                t, hf = f4 // 2, f4 % 2
                saw(OB[f4])
                dve.wait_ge(osq_done, f4 + 1)
                dve.reduce_sum(ss16[:, 0, t, 4 * hf:4 * hf + 4],
                               sq[:, f4, :].rearrange("p (h v) -> p h v", h=4), AX.X).then_inc(oss_done, 1)

            def o_scaled(f4):
                t, hf = f4 // 2, f4 % 2
                dve.wait_ge(ostd_done, f4 + 1)
                hs = slice(4 * hf, 4 * hf + 4)
                link(dve.reciprocal(ss16[:, 2, t, hs], ss16[:, 1, t, hs]))
                for c in range(4):
                    hd = 4 * hf + c
                    uv = U[:, t, hd * P:(hd + 1) * P]
                    ins = dve.scalar_tensor_tensor(uv, bank[OB[f4]][:, c * P:(c + 1) * P], ss16[:, 2, t, hd:hd + 1],
                                                   uv, ALU.mult, ALU.mult)
                ins.then_inc(free[OB[f4]], 1)

            o_sums(0)
            for f4 in range(4):
                if f4 < 3:
                    o_sums(f4 + 1)
                o_scaled(f4)
            t_lo_part(32)
            out_proj(71, OUT_R, (1, 3))
            t_lo_part(24)
            wait_full(6)
            dve.tensor_copy(lgT[:], bank[6][0:2 * NE, 0:TOK]).then_inc(free[6], 1)
            inverse_rms(3)

            R = [rt[:, i] for i in range(12)]
            wait_full(5)
            dve.tensor_copy(R[0], bank[5][:, 0:16].rearrange("p (t e) -> p t e", t=TT)).then_inc(free[5], 1)
            drained(5)
            for t in range(TT):
                dve.max(R[1][:, t, :], R[0][:, t, :]).then_inc(dve_seq, 1)
            n.step("seq", 2)
            dve.wait_ge(dve_seq, n.at("seq"))
            for t in range(TT):
                dve.max_index(rti[:, t, :], R[1][:, t, :], R[0][:, t, :]).then_inc(dve_seq, 1)
            n.step("seq", 2)
            dve.wait_ge(dve_seq, n.at("seq"))
            link(dve.tensor_copy(R[2], rti[:]))
            for t in range(TT):
                for r in range(2):
                    dve.tensor_scalar(R[6 + r][:, t, :], iota8[:], R[2][:, t, r:r + 1], None,
                                      ALU.is_equal).then_inc(dve_seq, 1)
            n.step("seq", 4)
            dve.wait_ge(dve_seq, n.at("seq"))
            dve.tensor_tensor(R[8], R[6], R[7], ALU.add).then_inc(mask_done, 1)
            link(dve.tensor_tensor(R[4][:, :, 0:1], R[1][:, :, 1:2], R[1][:, :, 0:1], ALU.subtract))
            dve.tensor_tensor(R[4][:, :, 0:1], R[4][:, :, 0:1], ss[:, 3, 4:6].rearrange("p (t o) -> p t o", o=1),
                              ALU.mult).then_inc(rt_d, 1)
            for t in range(TT):
                dve.tensor_scalar(U[:, t, :], X[:, t, :], ss[:, 3, 4 + t:5 + t], None, ALU.mult).then_inc(u_done, 1)
            dve.wait_ge(mask_done, 1)
            wait_full(4)
            pos = bank[4][:, 0:16].rearrange("p (t e) -> p t e", t=TT)
            dve.scalar_tensor_tensor(cols[:, :, 0:NE], pos, 1.0, R[8], ALU.add, ALU.mult).then_inc(free[4], 1)
            drained(4)
            for t in range(TT):
                dve.tensor_scalar(S[:, t, :], slots[:], cols[:, t, 0:1], None, ALU.is_equal).then_inc(s_done, 1)
            n.step("s", 2)
            wait_full(5)
            dve.reduce_max(cnt[:, 0:1], bank[5][:, 16:24], AX.X).then_inc(free[5], 1)
            drained(5)
            link(dve.tensor_scalar(cnt[:, 1:2], cnt[:, 0:1], float(CAP), float(NE), ALU.is_gt, ALU.mult))
            link(dve.tensor_scalar(nrounds[:, 0:1], cnt[:, 1:2], float(NE), None, ALU.add))
            link(dve.tensor_scalar(nrounds[:, 1:2], cnt[:, 1:2], float(NE - 1), None, ALU.add))
            dve.memset(cur[:, 2:4], 0.0).then_inc(dve_seq, 1)
            n.step("seq")
            dve.tensor_scalar(ST[:], rs_row[:], 0.0, None, ALU.mult).then_inc(rounds_in, 1)
            dve.tensor_scalar(cols[:, :, NE:2 * NE], cols[:, :, 0:NE], -float(CAP), None, ALU.add).then_inc(dve_seq, 1)
            dve.memset(cols[:, :, 2 * NE:2 * NE + 1], 0.0).then_inc(dve_seq, 1)
            n.step("seq", 2)
            dve.wait_ge(rt_e, 1)
            link(dve.tensor_scalar(R[4][:, :, 1:2], R[5][:, :, 0:1], 1.0, None, ALU.add))
            link(dve.reciprocal(R[4][:, :, 2:3], R[4][:, :, 1:2]))
            link(dve.tensor_tensor(R[4][:, :, 3:4], R[5][:, :, 0:1], R[4][:, :, 2:3], ALU.mult))
            for t in range(TT):
                link(dve.tensor_scalar(R[9][:, t, :], R[6][:, t, :], R[4][:, t, 2:3], None, ALU.mult))
                link(dve.scalar_tensor_tensor(gates[:, t, 0:NE], R[7][:, t, :], R[4][:, t, 3:4], R[9][:, t, :],
                                              ALU.mult, ALU.add))
            link(dve.tensor_copy(gates[:, :, NE:2 * NE], gates[:, :, 0:NE]))

            def round_slots(i):
                link(dve.tensor_copy(cur[:, 0:2].rearrange("p (t o) -> p t o", o=1), cols[:, :, bass.ds(i, 1)]))
                for t in range(TT):
                    dve.tensor_scalar(S[:, t, :], slots[:], cur[:, t:t + 1], None, ALU.is_equal).then_inc(s_done, 1)
                n.step("s", 2)

            def gather_lo():
                for m, b in enumerate((GATE + 1, UP + 1)):
                    wait_full(b)
                    dve.wait_ge(th_done, n.step("th", 4))
                    for c in range(4):
                        k = 4 * m + c
                        ins = dve.scalar_tensor_tensor(
                            t_lo[:, k, 0:CAP], bank[b][:, c * P:(c + 1) * P], col[:, 24 + k:25 + k],
                            t_hi[:, k, 0:CAP].bitcast(F32), ALU.mult, ALU.subtract)
                    ins.then_inc(free[b], 1)

            def y_lo_part():
                saw_product(YB, YB + 1)
                for m in range(2):
                    dve.wait_ge(yh_done, n.step("yh"))
                    dve.tensor_tensor(y_lo[m], bank[YB + m][:].rearrange("p (c n) -> p c n", c=4),
                                      y_hi[m].bitcast(F32),
                                      ALU.subtract).then_inc(free[YB + m], 1)

            def scatter_add(t, banks):
                for m, b in enumerate(banks):
                    wait_full(b)
                    xb = X[:, t, m * BLK:(m + 1) * BLK]
                    dve.scalar_tensor_tensor(xb, bank[b][:], cur[:, 2 + t:3 + t], xb, ALU.mult,
                                             ALU.add).then_inc(free[b], 1)

            gather_lo()
            dve.wait_ge(rounds_in, 1)
            nr = dve.value_load(nrounds[0:1, 0:1], min_val=NE, max_val=2 * NE)
            with dve.Fori(0, nr) as i:
                n.enter(i, dict(ROUND, seq=2, s=2, th=8, hh=7, yh=2))
                for b in range(FB):
                    if b == FB - 1:
                        split_to(U0 + 4 * b + 5)
                        for g in range(2):
                            hidden_lo(g)
                    split_to(U0 + 4 * b + 7)
                    saw_product(GATE + b % 2)
                    wait_units(U0 + 4 * b + 4, UP + b % 2)
                    h_block(b, 0, UP + b % 2, GATE + b % 2)
                    if b < 2:
                        scatter_add(b, LAST[0])
                    if b == 3:
                        saw(TR)
                        dve.wait_ge(full[TR], n.at(f"full{TR}"))
                        round_slots(i + 1)
                        link(dve.tensor_copy(cur[:, 2:4].rearrange("p (t o) -> p t o", o=1),
                                             gates[:, :, bass.ds(i, 1)]))
                gather_lo()
                for g in range(2, 7):
                    split_to(U0 + 28 + 2 * (g - 2) + 2 + SPL)
                    hidden_lo(g)
                split_to(U0 + FFN_UNITS + AHEAD)
                y_lo_part()
                n.count["u"] = U0 + AHEAD
                n.leave(nr)
            for t in range(TT):
                scatter_add(t, LAST[t])
            dve.wait_ge(gf_in, 16)
            for t in range(TT):
                drained(*LAST[t])
                dve.wait_ge(sq_done, 5 + t)
                link(dve.reciprocal(ss[:, 4, 4 + t:5 + t], ss[:, 4, 2 + t:3 + t]))
                dve.scalar_tensor_tensor(outb[:, t, :], X[:, t, :], ss[:, 4, 4 + t:5 + t], gf[:], ALU.mult,
                                         ALU.mult).then_inc(out_done, 1)

        @block.tensor
        def _(pe):
            n = Tally()

            def open_bank(b):
                last = n.at(f"fill{b}")
                n.step(f"fill{b}")
                if not (isinstance(last, int) and last == 0):
                    pe.wait_ge(free[b], last)

            def drained(*banks):
                for b in banks:
                    pe.wait_ge(free[b], n.at(f"fill{b}"))

            def unit():
                s = n.count.get("u", 0) % SPL
                n.count["u"] = n.count.get("u", 0) + 1
                pe.wait_ge(lo_done, n.step("unit"))
                return s

            def triple(o, lh, ll, rh, rl, start, stop):
                pe.matmul(o, lh, rh, start=start, stop=False)
                pe.matmul(o, lh, rl, start=False, stop=False)
                return pe.matmul(o, ll, rh, start=False, stop=stop)

            def transposes(rows_of, halves=((), ())):
                for j in range(4):
                    if j % 2 == 0:
                        drained(*halves[j // 2])
                    open_bank(TB[j])
                    for c in range(2):
                        for t in range(TT):
                            k = 2 * j + c
                            last = pe.transpose(bank[TB[j]][:, c * TOK + t * P:c * TOK + (t + 1) * P],
                                                rows_of[:, t, k * P:(k + 1) * P], ident[:])
                    last.then_inc(full[TB[j]], 1)

            def cols_block(banks, tiles, n_cols=BLK, units=2, fresh=()):
                for b in banks:
                    open_bank(b)
                for h in range(units):
                    if fresh:
                        drained(*fresh[h * len(fresh) // 2:(h + 1) * len(fresh) // 2])
                    col_unit(banks, tiles, h, units, n_cols)

            def col_unit(banks, tiles, h, units, n_cols=BLK):
                s = unit()
                for t in range(tiles):
                    last = col_half(banks, t, h, units, s, n_cols)
                last.then_inc(unit_done, 1)

            def col_half(banks, t, h, units, s, n_cols=BLK, mixed=False):
                per = KC // units
                for k in range(per):
                    kk = h * per + k
                    wsl = slice(k * n_cols, (k + 1) * n_cols)
                    a_hi, a_lo = t_hi[:, kk, :], t_lo[:, kk, :]
                    if mixed:
                        a_hi, a_lo = outputs_at(t_hi, h_hi, kk), outputs_at(t_lo, h_lo, kk)
                    last = triple(bank[banks[t]][:, 0:n_cols], a_hi[:, t * P:(t + 1) * P],
                                  a_lo[:, t * P:(t + 1) * P], w_hi[:, s, wsl], w_lo[:, s, wsl],
                                  kk == 0, kk == KC - 1)
                return last

            pe.wait_ge(consts, 12)
            pe.wait_ge(small_in, 64)
            open_bank(4)
            pe.transpose(bank[4][:, 0:56], rows[:], ident[0:56, 0:56]).then_inc(full[4], 1)

            pe.wait_ge(x_in, 16 * TT)
            transposes(X)
            def qk_transposes(j):
                open_bank(QKT[j])
                for c in range(min(2, 13 - 2 * j)):
                    for t in range(TT):
                        hp = 2 * (2 * j + c)
                        last = pe.transpose(bank[QKT[j]][:, c * TOK + t * P:c * TOK + (t + 1) * P],
                                            proj[:, t, hp:hp + 2, :].rearrange("p h d -> p (h d)"), ident[:])
                last.then_inc(full[QKT[j]], 1)

            for nb in range(2):
                cols_block([2 * nb, 2 * nb + 1], TT, fresh=TB if nb == 0 else ())
            open_bank(4)
            open_bank(5)
            col_unit([4, 5], TT, 0, 2)
            pe.wait_ge(roped, 2)
            for j in range(4):
                qk_transposes(j)
            col_unit([4, 5], TT, 1, 2)

            def filler(s):
                u, t = FILLER[s]
                if t == 0:
                    slot[0] = unit()
                if u in (6, 7):
                    if u == 6:
                        open_bank(6 + t)
                    last = col_half([6, 7], t, u - 6, 2, slot[0])
                elif u == 8:
                    if t == 0:
                        open_bank(3)
                    for k in range(KC):
                        ws = slice(k * 256, (k + 1) * 256)
                        last = triple(bank[3][:, t * 256:(t + 1) * 256], t_hi[:, k, t * P:(t + 1) * P],
                                      t_lo[:, k, t * P:(t + 1) * P], w_hi[:, slot[0], ws], w_lo[:, slot[0], ws],
                                      k == 0, k == KC - 1)
                else:
                    if u == 9 and t == 0:
                        drained(VB[(AH // 2 - 1) % 2])
                    open_bank(OUT_A[u - 9][t])
                    last = col_half(OUT_A[u - 9], t, 0, 2, slot[0], mixed=True)
                if t == 1:
                    last.then_inc(unit_done, 1)

            def scores(h):
                if h < AH:
                    qc, kc, half = h // 2, 4 + h // 2, h % 2
                else:
                    qc, kc, half = 8 + (h - AH) % 4, 12, (h - AH) // 4
                if h == 0:
                    drained(*QKT[0:4])
                if h == AH:
                    drained(*QKT[4:7])
                pr = slice(half * HD, (half + 1) * HD)
                b = SB[h % 2]
                open_bank(b)
                pe.matmul(bank[b][:, 0:P], qkT[pr, qc, 0:P], qkT[pr, kc, 0:P], start=True, stop=True)
                pe.matmul(bank[b][:, P:3 * P], qkT[pr, qc, P:TOK], qkT[pr, kc, :], start=True,
                          stop=True).then_inc(full[b], 1)

            slot = [0]
            for s in range(AH + BH + 3):
                if s < AH + BH and s != AH:
                    scores(s)
                if 0 <= s - 3 < AH + BH:
                    h = s - 3
                    b = VB[(h // 2) % 2]
                    vh = 28 + h if h < AH else 26 + (h - AH) // 4
                    if h == 0:
                        drained(4, 5)
                    drained(PB)
                    if h % 2 == 0:
                        open_bank(b)
                    o = bank[b][(h % 2) * HD:(h % 2 + 1) * HD, :]
                    pe.matmul(o[:, 0:TOK], proj[:, 0, vh, :], pT[:, h % 2, 0:TOK], start=True, stop=False)
                    pe.matmul(o[:, P:TOK], proj[:, 1, vh, :], pT[:, h % 2, TOK:3 * P], start=False,
                              stop=True).then_inc(pv_done, 1)
                if 0 <= s - 2 < AH + BH:
                    h = s - 2
                    pe.wait_ge(p_ready, 2 * (h + 1))
                    open_bank(PB)
                    for m in range(3):
                        last = pe.transpose(bank[PB][:, m * P:(m + 1) * P], sc[:, h % 3, m * P:(m + 1) * P],
                                            ident[:])
                    last.then_inc(full[PB], 1)
                if s == AH:
                    scores(s)
                if s == AH - 1:
                    pe.wait_ge(roped, 4)
                    for j in range(4, 7):
                        qk_transposes(j)
                if s in FILLER:
                    filler(s)
            drained(*VB)
            for nb in range(2):
                col_unit(OUT_A[nb], TT, 1, 2)

            def hidden_transposes(g, tiles):
                open_bank(TR + g % 2)
                per = 4 // tiles
                for c in range(per):
                    for t in range(tiles):
                        f0 = (g * per + c) * P
                        last = pe.transpose(bank[TR + g % 2][:, (c * tiles + t) * P:(c * tiles + t + 1) * P],
                                            H[:, t, f0:f0 + P], ident[:])
                last.then_inc(full[TR + g % 2], 1)

            def down_units(g, tiles, ybanks, groups):
                drained(TR + g % 2)
                per = 4 // tiles
                for u in range(per // 2):
                    s = unit()
                    for c in range(2):
                        cc = u * 2 + c
                        for t in range(tiles):
                            for m in range(2):
                                hs = slice((cc * tiles + t) * P, (cc * tiles + t + 1) * P)
                                ws = slice(c * D + m * BLK, c * D + (m + 1) * BLK)
                                fin = g == groups - 1 and cc == per - 1
                                last = triple(bank[ybanks[2 * t + m]][:], h_hi[:, g % 2, hs], h_lo[:, g % 2, hs],
                                              w_hi[:, s, ws], w_lo[:, s, ws], g == 0 and cc == 0, fin)
                    last.then_inc(unit_done, 1)

            transposes(X, OUT_A)
            for b in range(FB):
                cols_block([GATE, GATE + 1], TT, fresh=TB if b == 0 else ())
                cols_block([UP, UP + 1], TT)
                if b == FB - 2:
                    for g in range(2):
                        hidden_transposes(g, TT)
            for b in (YB, YB + 1, GATE, GATE + 1):
                open_bank(b)
            for g in range(14):
                down_units(g, TT, (YB, YB + 1, GATE, GATE + 1), 14)
                if g + 2 < 14:
                    if g + 2 == 12:
                        drained(UP, UP + 1)
                    hidden_transposes(g + 2, TT)

            transposes(X, ((YB, GATE), (YB + 1, GATE + 1)))
            drained(TB[0], TB[1])
            for first in (0, 4):
                for j in range(4):
                    if first == 0 and j == 2:
                        pe.wait_ge(row_done, 2)
                        open_bank(7)
                        pe.matmul(bank[7][:, 0:TOK], ones[:], rs_row[:], start=True, stop=True).then_inc(full[7], 1)
                    open_bank(first + j)
                    s = unit()
                    for c in range(2):
                        for k in range(KC):
                            if first == j == c == 0 and k == KC // 2:
                                drained(TB[2], TB[3])
                            ws = slice(k * 256 + c * P, k * 256 + (c + 1) * P)
                            last = triple(bank[first + j][:, c * TOK:(c + 1) * TOK], w_hi[:, s, ws], w_lo[:, s, ws],
                                          t_hi[:, k, :], t_lo[:, k, :], k == 0, k == KC - 1)
                    last.then_inc(unit_done, 1)
            def level(i, hf):
                pe.wait_ge(qp_done, 4 + (2 * (i - 1) + hf + 1 if i else 0))
                if i:
                    pe.wait_ge(kr_done, 2 * (i - 1) + hf + 1)
                lb = level_bank(i, hf)
                open_bank(lb)
                if i == LEVELS:
                    for c in range(4):
                        at = (4 * hf + c) * TOK
                        last = pe.matmul(bank[lb][:, c * P:(c + 1) * P], kT[:, at:at + P], qT[:, at + P:at + TOK],
                                         start=True, stop=True)
                else:
                    half = 1 << i
                    for c in range(8):
                        at = hf * 1024 + c * P
                        qv = qT[:, at:at + P].rearrange("p (n two h) -> p n two h", two=2, h=half)
                        last = pe.matmul(bank[lb][:, c * P // 2:(c + 1) * P // 2].rearrange("p (n h) -> p n h", h=half),
                                         kT[:, at:at + P], qv[:, :, 1, :], start=True, stop=True)
                last.then_inc(lev_done, 1)

            def own_products():
                pe.wait_ge(qk_done, 4)
                open_bank(4)
                for c in range(CH * TT):
                    last = pe.matmul(bank[4][:, c:c + 1], aT[:, c * P:(c + 1) * P], ones[:, 0:1],
                                     start=True, stop=True)
                last.then_inc(full[4], 1)

            for nb in range(4):
                ba = 2 * nb % 4
                open_bank(ba)
                open_bank(ba + 1)
                for h in range(2):
                    u = 2 * nb + h
                    s = unit()
                    col_half([ba, ba + 1], 0, h, 2, s)
                    if u == 7:
                        level(LEVELS - 1, 0)
                        level(LEVELS - 1, 1)
                    col_half([ba, ba + 1], 1, h, 2, s).then_inc(unit_done, 1)
                    if u == 1:
                        own_products()
                    if u:
                        for hf in range(2):
                            level(u - 1 if u < 7 else LEVELS, hf)
            for t in range(TT):
                drained(*(level_bank(LEVELS - 1 + t, hf) for hf in range(2)))
                for hf in range(2):
                    b = OB[2 * t + hf]
                    open_bank(b)
                    for c in range(4):
                        hd = 4 * hf + c
                        o = bank[b][:, c * P:(c + 1) * P]
                        vs = slice(hd * P, (hd + 1) * P)
                        if t == 1:
                            pe.matmul(o, aX[:, vs], V[:, 0, vs], start=True, stop=False)
                        last = pe.matmul(o, aT[:, hd * TOK + t * P:hd * TOK + (t + 1) * P], V[:, t, vs],
                                         start=t == 0, stop=True)
                    last.then_inc(full[b], 1)
            transposes(U, ((OB[0], OB[2]), (OB[1], OB[3])))
            for nb in range(2):
                cols_block([2 * nb, 2 * nb + 1], TT, fresh=TB if nb == 0 else ())

            transposes(X, OUT_R)
            pe.wait_ge(wr_split, 1)
            open_bank(6)
            for k in range(KC):
                if k % 4 == 0:
                    drained(TB[k // 2], TB[k // 2 + 1])
                for part in (t_hi, t_lo):
                    last = pe.matmul(bank[6][0:2 * NE, 0:TOK], wr16[:, k, :], part[:, k, :],
                                     start=k == 0 and part is t_hi, stop=k == KC - 1 and part is t_lo)
            last.then_inc(full[6], 1)
            drained(6)
            open_bank(5)
            for t in range(TT):
                last = pe.matmul(bank[5][:, t * NE:(t + 1) * NE], lgT[:, t * P:(t + 1) * P], fold[:],
                                 start=True, stop=True)
            last.then_inc(full[5], 1)
            open_bank(4)
            pe.wait_ge(mask_done, 1)
            m0, m1 = rt[:, 8, 0, :], rt[:, 8, 1, :]
            pe.matmul(bank[4][:, 0:8], tri[:], m0, start=True, stop=True)
            pe.matmul(bank[4][:, 8:16], tri[:], m1, start=True, stop=False)
            pe.matmul(bank[4][:, 8:16], ones[:], m0, start=False, stop=True).then_inc(full[4], 1)
            open_bank(5)
            pe.matmul(bank[5][:, 16:24], ones[:], m0, start=True, stop=False)
            pe.matmul(bank[5][:, 16:24], ones[:], m1, start=False, stop=True).then_inc(full[5], 1)

            def gather():
                pe.wait_ge(s_done, n.step("s", 2))
                if n.var is None:
                    pe.wait_ge(u_done, TT)
                for m, b in enumerate((GATE + 1, UP + 1)):
                    open_bank(b)
                    for c in range(4):
                        k = 4 * m + c
                        for t in range(TT):
                            last = pe.matmul(bank[b][:, c * P:(c + 1) * P], U[:, t, k * P:(k + 1) * P],
                                             S[:, t, :], start=t == 0, stop=t == TT - 1)
                    last.then_inc(full[b], 1)

            def scatter(t, banks):
                for m, b in enumerate(banks):
                    open_bank(b)
                    o = bank[b][:].rearrange("p (c n) -> p c n", c=4)
                    pe.matmul(o, ST[:, t * P:(t + 1) * P], y_hi[m], start=True, stop=False)
                    pe.matmul(o, ST[:, t * P:(t + 1) * P], y_lo[m], start=False, stop=True).then_inc(full[b], 1)

            gather()
            pe.wait_ge(rounds_in, 1)
            nr = pe.value_load(nrounds[0:1, 0:1], min_val=NE, max_val=2 * NE)
            with pe.Fori(0, nr) as i:
                n.enter(i, {k: c for k, c in dict(ROUND, s=2).items() if k[:4] != "full"})
                for b in range(FB):
                    cols_block([GATE + b % 2], 1, fresh=(GATE + 1, UP + 1) if b == 0 else ())
                    cols_block([UP + b % 2], 1)
                    if b < 2:
                        if b == 0:
                            drained(YB, YB + 1)
                        scatter(b, LAST[0])
                    if b == 2:
                        open_bank(TR)
                        for t in range(TT):
                            last = pe.transpose(bank[TR][:, t * P:(t + 1) * P], S[:, t, :], ident[:])
                        last.then_inc(full[TR], 1)
                    if b == FB - 2:
                        for g in range(2):
                            hidden_transposes(g, 1)
                gather()
                open_bank(YB)
                open_bank(YB + 1)
                for g in range(7):
                    down_units(g, 1, (YB, YB + 1), 7)
                    if g + 2 < 7:
                        if g + 2 == 6:
                            drained(UP)
                        hidden_transposes(g + 2, 1)
                n.count["u"] = U0
                n.leave(nr)
            drained(YB, YB + 1)
            for t in range(TT):
                scatter(t, LAST[t])


_INS = ["x", "positions", "g_mix", "g_ffn", "g_final", "w_in_attn", "w_out_attn", "attn_sinks", "w_in_rec",
        "rec_lower_bounds", "rec_norm_g", "w_out_rec", "w_gate_dense", "w_up_dense", "w_down_dense",
        "w_router", "w_gate_moe", "w_up_moe", "w_down_moe"]


def kernel(**inputs):
    import numpy as _np
    import concourse.bacc as _bacc
    from concourse import mybir as _mybir
    from concourse.bass_utils import run_bass_kernel_spmd as _run

    nc = _bacc.Bacc("TRN2", target_bir_lowering=False, num_devices=1)
    arrays, args = {}, []
    for name in _INS:
        a = _np.ascontiguousarray(inputs[name])
        arrays[f"in_{name}_dram"] = a
        args.append(nc.dram_tensor(f"in_{name}_dram", a.shape, _mybir.dt.from_np(a.dtype), kind="ExternalInput").ap())
    shape = inputs["x"].shape
    out = nc.dram_tensor("out_0_dram", shape, _mybir.dt.float32, kind="ExternalOutput").ap()
    build(nc, *args, out)
    r = _run(nc, [arrays], core_ids=[0])
    return r.results[0]["out_0_dram"]
```
